# Optimizing a Trainium2 kernel written in Bass

```python
import jax, jax.numpy as jnp
from jax import lax
import numpy as np

D_MODEL = 1024
BATCH = 1
SEQ = 1024
DEPTH = 2
DEC_BATCH = 8
DEC_SEQ = 16
PAST_LEN = 128

CHUNK = 64
N_A_LAYERS = DEPTH // 2
N_B_LAYERS = DEPTH - N_A_LAYERS
RET_HEADS = 4
RET_DK = D_MODEL // RET_HEADS
RET_DV = 2 * RET_DK
RET_QK_W = RET_HEADS * RET_DK
RET_VW = RET_HEADS * RET_DV
RET_IN = 2 * RET_QK_W + 2 * RET_VW
ROPE_BASE = 10000.0
FOX_HEADS = 8
FOX_KV_HEADS = 4
FOX_GROUP = FOX_HEADS // FOX_KV_HEADS
FOX_DH = 128
FOX_W = FOX_HEADS * FOX_DH
FOX_IN = 2 * FOX_W
KV_W = FOX_KV_HEADS * FOX_DH
KV_OUT = 2 * KV_W + FOX_HEADS
Q_BLOCK = 128
EPS = 1e-6

kernel_name = 'yoco_retention_fox_streaming_step'

F32 = jnp.float32

def rms_norm(x, g):
    xf = x.astype(F32)
    y = xf * lax.rsqrt(jnp.mean(xf * xf, axis=-1, keepdims=True) + EPS)
    return (y * g.astype(F32)).astype(x.dtype)

def ada_mod(c, w, b):
    return jax.nn.silu(c) @ w + b

def modulate(x, g, shift, scale):
    return rms_norm(x, g) * (1 + scale[:, None, :]) + shift[:, None, :]

def rotary(x, pos):
    half = x.shape[-1] // 2
    inv = jnp.power(ROPE_BASE, -jnp.arange(half, dtype=F32) / half)
    ang = pos.astype(F32)[:, None] * inv[None, :]
    cos = jnp.cos(ang)[None, :, None, :]
    sin = jnp.sin(ang)[None, :, None, :]
    xf = x.astype(F32)
    x1, x2 = xf[..., :half], xf[..., half:]
    return jnp.concatenate([x1 * cos - x2 * sin, x2 * cos + x1 * sin], axis=-1).astype(x.dtype)

def head_norm(o, g):
    of = o.astype(F32)
    mu = jnp.mean(of, axis=-1, keepdims=True)
    var = jnp.mean(jnp.square(of - mu), axis=-1, keepdims=True)
    return ((of - mu) * lax.rsqrt(var + EPS) * g.astype(F32)).astype(o.dtype)

def ret_log_gamma():
    return jnp.log1p(-jnp.exp2(-5.0 - jnp.arange(RET_HEADS, dtype=F32)))

def retention_scan(q, k, v, r0):
    b, L = q.shape[0], q.shape[1]
    cs = min(CHUNK, L)
    n = L // cs
    lg = ret_log_gamma()
    idx = jnp.arange(cs, dtype=F32)
    diff = idx[:, None] - idx[None, :]
    intra = jnp.where(diff >= 0, jnp.exp(jnp.maximum(diff, 0.0)[None] * lg[:, None, None]), 0.0)
    q_dec = jnp.exp((idx + 1.0)[:, None] * lg[None, :])[None, :, :, None]
    k_dec = jnp.exp((cs - 1.0 - idx)[:, None] * lg[None, :])[None, :, :, None]
    c_dec = jnp.exp(cs * lg)[None, :, None, None]

    def to_chunks(t):
        return t.reshape(b, n, cs, *t.shape[2:]).swapaxes(0, 1)

    def step(r, qkv):
        qc, kc, vc = qkv
        qf, kf, vf = qc.astype(F32), kc.astype(F32), vc.astype(F32)
        s = jnp.einsum('bihd,bjhd->bhij', qf, kf) * intra[None]
        o = jnp.einsum('bhij,bjhe->bihe', s, vf)
        o = o + jnp.einsum('bihd,bhde->bihe', qf, r) * q_dec
        r = r * c_dec + jnp.einsum('bjhd,bjhe->bhde', kf * k_dec, vf)
        return r, o.astype(vc.dtype)

    r, o = lax.scan(step, r0.astype(F32), (to_chunks(q), to_chunks(k), to_chunks(v)))
    o = o.swapaxes(0, 1).reshape(b, L, RET_HEADS, RET_DV)
    return o, r.astype(r0.dtype)

def retention_layer(x, c, pos, r0, norm_g, ada_w, ada_b, w_in, gn_g, w_out):
    shift, scale, gate = jnp.split(ada_mod(c, ada_w, ada_b), 3, axis=-1)
    h = modulate(x, norm_g, shift, scale)
    b, L = x.shape[0], x.shape[1]
    q, k, v, g = jnp.split(h @ w_in, [RET_QK_W, 2 * RET_QK_W, 2 * RET_QK_W + RET_VW], axis=-1)
    q = rotary(q.reshape(b, L, RET_HEADS, RET_DK), pos)
    k = rotary(k.reshape(b, L, RET_HEADS, RET_DK), pos) * (RET_DK ** -0.5)
    v = v.reshape(b, L, RET_HEADS, RET_DV)
    o, r = retention_scan(q, k, v, r0)
    o = head_norm(o, gn_g.reshape(RET_HEADS, RET_DV)).reshape(b, L, RET_VW) * jax.nn.silu(g)
    return x + gate[:, None, :] * (o @ w_out), r

def shared_kv(x, c, kv_norm_g, kv_ada_w, kv_ada_b, kv_w, kv_fb, k_norm_g):
    shift, scale = jnp.split(ada_mod(c, kv_ada_w, kv_ada_b), 2, axis=-1)
    h = modulate(x, kv_norm_g, shift, scale)
    b, L = x.shape[0], x.shape[1]
    k, v, f = jnp.split(h @ kv_w, [KV_W, 2 * KV_W], axis=-1)
    k = rms_norm(k.reshape(b, L, FOX_KV_HEADS, FOX_DH), k_norm_g)
    v = v.reshape(b, L, FOX_KV_HEADS, FOX_DH)
    logf = jax.nn.log_sigmoid((f + kv_fb).astype(F32))
    return k, v, logf

def fox_attend(q, k, v, fq, fk, qpos, kpos):
    b, nq = q.shape[0], q.shape[1]
    s = jnp.einsum('bqkgd,bskd->bkgqs', q.astype(F32), k.astype(F32)) * (FOX_DH ** -0.5)
    fq_ = fq.reshape(b, nq, FOX_KV_HEADS, FOX_GROUP).transpose(0, 2, 3, 1)[..., None]
    s = s + fq_ - fk[:, :, :, None, :]
    s = jnp.where(kpos[None, :] <= qpos[:, None], s, -jnp.inf)
    p = jax.nn.softmax(s, axis=-1)
    o = jnp.einsum('bkgqs,bskd->bqkgd', p, v.astype(F32))
    return o.reshape(b, nq, FOX_HEADS, FOX_DH).astype(v.dtype)

def fox_layer(x, c, k, v, F, F_q, qpos, kpos, norm_g, ada_w, ada_b, w_in, q_norm_g, w_out):
    shift, scale, gate = jnp.split(ada_mod(c, ada_w, ada_b), 3, axis=-1)
    h = modulate(x, norm_g, shift, scale)
    b, L = x.shape[0], x.shape[1]
    q, g = jnp.split(h @ w_in, 2, axis=-1)
    q = rms_norm(q.reshape(b, L, FOX_HEADS, FOX_DH), q_norm_g).reshape(b, L, FOX_KV_HEADS, FOX_GROUP, FOX_DH)
    S = k.shape[1]
    fk = F.reshape(b, S, FOX_KV_HEADS, FOX_GROUP).transpose(0, 2, 3, 1)
    if L <= Q_BLOCK:
        o = fox_attend(q, k, v, F_q, fk, qpos, kpos)
    else:
        nb = L // Q_BLOCK
        qb = q.reshape(b, nb, Q_BLOCK, FOX_KV_HEADS, FOX_GROUP, FOX_DH).swapaxes(0, 1)
        fqb = F_q.reshape(b, nb, Q_BLOCK, FOX_HEADS).swapaxes(0, 1)
        pb = qpos.reshape(nb, Q_BLOCK)
        ob = lax.map(lambda a: fox_attend(a[0], k, v, a[1], fk, a[2], kpos), (qb, fqb, pb))
        o = ob.swapaxes(0, 1).reshape(b, L, FOX_HEADS, FOX_DH)
    o = o.reshape(b, L, FOX_W) * jax.nn.silu(g)
    return x + gate[:, None, :] * (o @ w_out)

def trunk(x, c, pos0, r0, k_past, v_past, logf_past,
          a_norm_g, a_ada_w, a_ada_b, a_w_in, a_gn_g, a_w_out,
          kv_norm_g, kv_ada_w, kv_ada_b, kv_w, kv_fb, k_norm_g,
          b_norm_g, b_ada_w, b_ada_b, b_w_in, b_q_norm_g, b_w_out):
    L = x.shape[1]
    qpos = pos0 + jnp.arange(L)
    r_out = []
    k_new = v_new = logf_new = None
    k_all = v_all = F = F_q = kpos = None
    for layer in range(DEPTH):
        if layer < N_A_LAYERS:
            i = layer
            x, r = retention_layer(x, c, qpos, r0[i], a_norm_g[i], a_ada_w[i], a_ada_b[i],
                                   a_w_in[i], a_gn_g[i], a_w_out[i])
            r_out.append(r)
        else:
            if layer == N_A_LAYERS:
                k_new, v_new, logf_new = shared_kv(x, c, kv_norm_g, kv_ada_w, kv_ada_b, kv_w, kv_fb, k_norm_g)
                if k_past is None:
                    k_all, v_all, logf_all = k_new, v_new, logf_new
                else:
                    k_all = jnp.concatenate([k_past.astype(k_new.dtype), k_new], axis=1)
                    v_all = jnp.concatenate([v_past.astype(v_new.dtype), v_new], axis=1)
                    logf_all = jnp.concatenate([logf_past.astype(F32), logf_new], axis=1)
                F = jnp.cumsum(logf_all, axis=1)
                F_q = F[:, F.shape[1] - L:]
                kpos = jnp.arange(F.shape[1])
            j = layer - N_A_LAYERS
            x = fox_layer(x, c, k_all, v_all, F, F_q, qpos, kpos, b_norm_g[j], b_ada_w[j], b_ada_b[j],
                          b_w_in[j], b_q_norm_g[j], b_w_out[j])
    return x, jnp.stack(r_out, axis=0), k_new, v_new, logf_new

def setup_inputs(seed: int = 0) -> dict:
    key = jax.random.key(seed)
    ks = jax.random.split(key, 32)
    D = D_MODEL
    nrm = jax.random.normal
    s_d = D ** -0.5
    return {
        'x_prompt': nrm(ks[0], (BATCH, SEQ, D), F32),
        'x_sample': nrm(ks[1], (DEC_BATCH, DEC_SEQ, D), F32),
        'state_ret': 0.05 * nrm(ks[2], (N_A_LAYERS, DEC_BATCH, RET_HEADS, RET_DK, RET_DV), F32),
        'cache_k': nrm(ks[3], (DEC_BATCH, PAST_LEN, FOX_KV_HEADS, FOX_DH), F32),
        'cache_v': nrm(ks[4], (DEC_BATCH, PAST_LEN, FOX_KV_HEADS, FOX_DH), F32),
        'cache_logf': jax.nn.log_sigmoid(2.0 + nrm(ks[5], (DEC_BATCH, PAST_LEN, FOX_HEADS), F32)),
        'c_prompt': nrm(ks[6], (BATCH, D), F32),
        'c_sample': nrm(ks[7], (DEC_BATCH, D), F32),
        'a_norm_g': 1.0 + 0.02 * nrm(ks[8], (N_A_LAYERS, D), F32),
        'a_ada_w': 0.5 * s_d * nrm(ks[9], (N_A_LAYERS, D, 3 * D), F32),
        'a_ada_b': 0.02 * nrm(ks[10], (N_A_LAYERS, 3 * D), F32),
        'a_w_in': s_d * nrm(ks[11], (N_A_LAYERS, D, RET_IN), F32),
        'a_gn_g': 1.0 + 0.02 * nrm(ks[12], (N_A_LAYERS, RET_VW), F32),
        'a_w_out': (RET_VW ** -0.5) * nrm(ks[13], (N_A_LAYERS, RET_VW, D), F32),
        'kv_norm_g': 1.0 + 0.02 * nrm(ks[14], (D,), F32),
        'kv_ada_w': 0.5 * s_d * nrm(ks[15], (D, 2 * D), F32),
        'kv_ada_b': 0.02 * nrm(ks[16], (2 * D,), F32),
        'kv_w': s_d * nrm(ks[17], (D, KV_OUT), F32),
        'kv_fb': 2.0 + 0.1 * nrm(ks[18], (FOX_HEADS,), F32),
        'k_norm_g': 1.0 + 0.02 * nrm(ks[19], (FOX_DH,), F32),
        'b_norm_g': 1.0 + 0.02 * nrm(ks[20], (N_B_LAYERS, D), F32),
        'b_ada_w': 0.5 * s_d * nrm(ks[21], (N_B_LAYERS, D, 3 * D), F32),
        'b_ada_b': 0.02 * nrm(ks[22], (N_B_LAYERS, 3 * D), F32),
        'b_w_in': s_d * nrm(ks[23], (N_B_LAYERS, D, FOX_IN), F32),
        'b_q_norm_g': 1.0 + 0.02 * nrm(ks[24], (N_B_LAYERS, FOX_DH), F32),
        'b_w_out': (FOX_W ** -0.5) * nrm(ks[25], (N_B_LAYERS, FOX_W, D), F32),
    }

def reference(x_prompt, x_sample, state_ret, cache_k, cache_v, cache_logf, c_prompt, c_sample,
              a_norm_g, a_ada_w, a_ada_b, a_w_in, a_gn_g, a_w_out,
              kv_norm_g, kv_ada_w, kv_ada_b, kv_w, kv_fb, k_norm_g,
              b_norm_g, b_ada_w, b_ada_b, b_w_in, b_q_norm_g, b_w_out):
    weights = (a_norm_g, a_ada_w, a_ada_b, a_w_in, a_gn_g, a_w_out,
               kv_norm_g, kv_ada_w, kv_ada_b, kv_w, kv_fb, k_norm_g,
               b_norm_g, b_ada_w, b_ada_b, b_w_in, b_q_norm_g, b_w_out)
    r0_p = jnp.zeros((N_A_LAYERS, x_prompt.shape[0], RET_HEADS, RET_DK, RET_DV), F32)
    y_prompt, state_ret_prompt, k_prompt, v_prompt, logf_prompt = trunk(
        x_prompt, c_prompt, 0, r0_p, None, None, None, *weights)
    past = cache_k.shape[1]
    y_sample, state_ret_sample, k_sample, v_sample, logf_sample = trunk(
        x_sample, c_sample, past, state_ret, cache_k, cache_v, cache_logf, *weights)
    return (y_prompt, y_sample, state_ret_prompt, k_prompt, v_prompt, logf_prompt,
            state_ret_sample, k_sample, v_sample, logf_sample)


_drawn_inputs = setup_inputs


def setup_inputs(seed=0):
    import zlib

    import numpy as np

    out = dict(_drawn_inputs(seed))
    spreads = {}
    factors = {'cache_logf': 6.835,
     'a_gn_g': 8.0,
     'kv_norm_g': 2.98,
     'k_norm_g': 2.89,
     'b_norm_g': 8.0,
     'b_ada_b': 7.695,
     'b_q_norm_g': 8.0}
    for name, (base, spread) in spreads.items():
        noise = np.random.default_rng([zlib.crc32(name.encode()), seed]).standard_normal(out[name].shape)
        drawn = base * np.exp(spread * noise) if base else spread * noise
        out[name] = __import__('jax').numpy.asarray(drawn.astype(out[name].dtype))
    for name, factor in factors.items():
        out[name] = (out[name] * factor).astype(out[name].dtype)
    return out
```

```python
from contextlib import ExitStack, contextmanager

import numpy as np
import concourse.bass as bass
from concourse import mybir

F32 = mybir.dt.float32
F32R = mybir.dt.float32r
ALU = mybir.AluOpType
ACT = mybir.ActivationFunctionType
AX = mybir.AxisListType

P = 128
D = 1024
SEQ = 1024
DEC_BATCH, DEC_SEQ, PAST = 8, 16, 128
TOKENS = SEQ + DEC_BATCH * DEC_SEQ
TILES = TOKENS // P
PT = SEQ // P
RH, DK, DV = 4, 256, 512
VW = RH * DV
FH, KVH, DH = 8, 4, 128
KT = D // P
CW = 512
SUBS = 4
KS = KT // SUBS
NB3 = 384
EPS = 1e-6
NEG = -1.0e30
ROPE_BASE = 10000.0
BR = 32


def tables():
    f = np.float32
    pos = np.concatenate([np.arange(SEQ), PAST + np.tile(np.arange(DEC_SEQ), DEC_BATCH)]).astype(f)
    half = DK // 2
    inv = np.power(f(ROPE_BASE), -np.arange(half, dtype=f) / f(half)).astype(f)
    ang = (inv[:, None] * pos[None, :]).astype(f)
    lg = np.log1p(-np.exp2(-5.0 - np.arange(RH, dtype=np.float64)))
    i = np.arange(P)
    ks = DK ** -0.5
    diff = i[None, :] - i[:, None]
    same = (i[None, :] // DEC_SEQ) == (i[:, None] // DEC_SEQ)
    intra = np.stack([np.where(diff >= 0, np.exp(np.maximum(diff, 0) * g), 0) * ks for g in lg], 1)
    intra_s = np.stack([np.where((diff >= 0) & same, np.exp(np.maximum(diff, 0) * g), 0) * ks for g in lg], 1)
    ones = np.ones((P, 1, 1))
    qdec = ones * np.stack([np.exp((i + 1.0) * g) for g in lg], 0)[None]
    loc = i % DEC_SEQ
    par = (i // DEC_SEQ) % 2
    qdec_s = ones[..., None] * np.stack([[np.exp((loc + 1.0) * g) * (par == p) for p in range(2)] for g in lg], 0)[None]
    kdec = np.stack([np.exp((P - 1.0 - i) * g) * ks for g in lg], 1)
    kdec_s = np.stack([np.exp((DEC_SEQ - 1.0 - loc) * g)[:, None] * ks * (i[:, None] // DEC_SEQ == np.arange(DEC_BATCH)) for g in lg], 1)
    cdec = np.ones((P, 1)) * np.exp(P * lg)[None]
    cdec_s = np.ones((P, 1)) * np.exp(DEC_SEQ * lg)[None]
    sel_gate = np.zeros((P, 2, 4, P))
    for j in range(4):
        sel_gate[BR * j + DEC_BATCH, 0, j, :] = 1
        for b in range(DEC_BATCH):
            sel_gate[BR * j + b, 1, j, b * DEC_SEQ:(b + 1) * DEC_SEQ] = 1
    mask = np.where(i[None, :] <= i[:, None], 0, NEG)
    sel_head = np.zeros((FH, FH, P))
    for h in range(FH):
        sel_head[h, h] = 1
    row_j, row_g, row_q = i // 32, (i // DEC_SEQ) % 2, i % DEC_SEQ
    sel_group = np.zeros((FH, KVH, P))
    for kv in range(KVH):
        sel_group[2 * kv + row_g, kv, i] = 1
    mask_s, own_s = np.zeros((P, 2, P)), np.zeros((P, 2, P))
    for r in range(2):
        b = 4 * r + row_j
        ok = (i[None, :] // DEC_SEQ == b[:, None]) & (loc[None, :] <= row_q[:, None])
        mask_s[:, r] = np.where(ok, 0, NEG)
        own_s[:, r] = i[None, :] == (b * DEC_SEQ + row_q)[:, None]
    t = dict(ident=np.eye(P), cos=np.cos(ang), sin=np.sin(ang), intra=intra, intra_s=intra_s,
             qdec=qdec, qdec_s=qdec_s, kdec=kdec, kdec_s=kdec_s, cdec=cdec, cdec_s=cdec_s,
             sel_gate=sel_gate, mask=mask, sel_head=sel_head, sel_group=sel_group,
             mask_s=mask_s, own_s=own_s)
    return {k: np.ascontiguousarray(v.reshape(v.shape[0], -1), dtype=f) for k, v in t.items()}


class Program:

    def __init__(self, nc, ctx, dram, table):
        self.nc, self.ctx, self.dram, self.table = nc, ctx, dram, table
        self.raw = self.sb("w_raw", [P, 2, KS, CW])
        self.w_hi = self.sb("w_hi", [P, 2, KT, CW], F32R)
        self.w_lo = self.sb("w_lo", [P, 2, KT, CW], F32R)
        self.raw_landed = [self.sem(f"raw_landed{s}") for s in range(2)]
        self.raw_split = self.sem("raw_split")
        self.hi_done = self.sem("w_hi_done")
        self.ident = self.sb("ident", [P, P])
        self.passed = self.sem("passed")
        self.mod_a = [self.sb(f"mod_a{m}", [P, KT, DEC_BATCH + 1]) for m in range(3)]
        self.mod_b = [self.sb(f"mod_b{m}", [P, KT, DEC_BATCH + 1]) for m in range(3)]

    def sb(self, name, shape, dt=F32):
        return self.ctx.enter_context(self.nc.sbuf_tensor(name, shape, dt))

    def sem(self, name):
        return self.ctx.enter_context(self.nc.semaphore(name))


def stand(eng, pr):
    eng.sem_inc(pr.passed, 1)


def credit(pool, pr, sems):
    for n, sem in enumerate(sems):
        pool.dma_start(pr.dram["credit"][n:n + 1, :], pr.ident[0:1, :]).then_inc(sem, 16)


@contextmanager
def semaphores(nc, prefix):
    taken = []

    def sem(name):
        taken.append(nc.alloc_semaphore(prefix + name))
        return taken[-1]
    yield sem
    nc.clear_and_free_semaphores(taken)
    nc.all_engine_barrier()


class Chain:

    def __init__(self, eng, sem, start=0):
        self.eng, self.sem, self.n, self.base = eng, sem, start, 0

    def link(self, ins):
        self.n += 1
        ins.then_inc(self.sem, 1)
        self.eng.wait_ge(self.sem, self.base + self.n)



def load_chunk(pr, sp, weight, chunk):
    with sp.Fori(0, SUBS // 2) as j:
        for slot in range(2):
            sp.wait_ge(pr.raw_split, chunk * SUBS + 2 * j + slot + 1)
            for dst, src in weight(pr.raw[:, slot], (2 * j + slot) * KS * P):
                sp.dma_start(dst, src).then_inc(pr.raw_landed[slot], 16)


def columns(w, row0, c0):
    def pieces(raw, r):
        return [(raw[:, k], w[bass.ds(r + row0 + k * P, P), c0:c0 + CW]) for k in range(KS)]
    return pieces


def head_columns(w, h):
    def pieces(raw, r):
        rows = w[bass.ds(r, KS * P), :].rearrange("(k p) c -> p k c", p=P)
        return [(raw[:, :, 0:DK], rows[:, :, h * DK:(h + 1) * DK]), (raw[:, :, DK:2 * DK], rows[:, :, D + h * DK:D + (h + 1) * DK])]
    return pieces


def split_hi(pr, act, chunk, slot, sub):
    act.wait_ge(pr.raw_landed[sub % 2], chunk * (SUBS // 2) * 32 + (sub // 2 + 1) * 32)
    act.copy(pr.w_hi[:, slot, sub * KS:(sub + 1) * KS, :], pr.raw[:, sub % 2]).then_inc(pr.hi_done, 1)


def split_lo(pr, dve, chunk, slot, sub):
    dve.wait_ge(pr.hi_done, chunk * SUBS + sub + 1)
    dve.tensor_tensor(pr.w_lo[:, slot, sub * KS:(sub + 1) * KS, :], pr.raw[:, sub % 2],
                      pr.w_hi[:, slot, sub * KS:(sub + 1) * KS, :].bitcast(F32), ALU.subtract).then_inc(pr.raw_split, 1)


def condition(pr):
    nc = pr.nc
    dr = pr.dram
    ROUNDS = [("a", 0, 2048), ("gates", 0, 0), ("kv", 0, 2048), ("b", 0, 2048)]
    w_of = {"a": dr["a_ada_w"], "kv": dr["kv_ada_w"], "b": dr["b_ada_w"]}
    b_of = {"a": dr["a_ada_b"], "kv": dr["kv_ada_b"], "b": dr["b_ada_b"]}

    def cols(r, j):
        if ROUNDS[r][0] == "gates":
            return ("a", 2048 + 512 * j) if j < 2 else ("b", 2048 + 512 * (j - 2))
        return ROUNDS[r][0], 512 * j

    with ExitStack() as ctx:
        sb = lambda n, s, dt=F32: ctx.enter_context(nc.sbuf_tensor(n, s, dt))
        ps = lambda n, s: ctx.enter_context(nc.psum_tensor(n, s, F32))
        sem = ctx.enter_context(semaphores(nc, "ada_"))
        c_rows = sb("c_rows", [BR, D])
        c_silu = sb("c_silu", [BR, D])
        cT = sb("cT", [P, KT, BR])
        w = sb("ada_w_sb", [P, 4, 4, CW])
        bias = sb("ada_bias", [P, 4, CW])
        rows = sb("ada_rows", [P, 4, CW])
        norm_g = sb("norm_g", [P, 3, KT])
        sel = sb("sel_gate_sb", [P, 2, 4, P])
        gate = sb("gate_sb", [P, 2, 2, D])
        ps_c = ps("ps_c", [P, 512])
        ps_ada = ps("ps_ada", [P, 2, 512])
        ps_t = ps("ps_t", [P, 512])
        ps_g = ps("ps_g", [P, 4, 512])
        in_landed, c_ready, b_zero, b_landed = sem("in_landed"), sem("c_ready"), sem("b_zero"), sem("b_landed")
        s_silu, c_turned, cT_ready = sem("s_silu"), sem("c_turned"), sem("cT_ready")
        w_landed = [sem(f"ada_landed{i}") for i in range(4)]
        w_read, rows_ready = sem("ada_read"), sem("rows_ready")
        turned, mod_ready, gate_done, gate_ready, gate_out = sem("ada_turned"), sem("mod_ready"), sem("gate_done"), sem("gate_ready"), sem("gate_out")
        block = ctx.enter_context(nc.Block())

        @block.sync
        def _(sp):
            sp.wait_ge(c_ready, 1)
            sp.dma_start(c_rows[0:DEC_BATCH], dr["c_sample"]).then_inc(in_landed, 16)
            sp.dma_start(c_rows[DEC_BATCH:DEC_BATCH + 1], dr["c_prompt"]).then_inc(in_landed, 16)
            sp.dma_start(pr.ident[:, :], pr.table["ident"]).then_inc(in_landed, 16)
            for r in range(4):
                for k in range(KT):
                    n = r * KT + k
                    if n >= 4:
                        sp.wait_ge(w_read, n - 3)
                    if cols(r, 0)[0] == cols(r, 3)[0]:
                        sp.dma_start(w[:, n % 4], w_of[cols(r, 0)[0]][k * P:(k + 1) * P, 0:2048].rearrange("p (j c) -> p j c", j=4)).then_inc(w_landed[n % 4], 16)
                    else:
                        for half, m in enumerate("ab"):
                            sp.dma_start(w[:, n % 4, 2 * half:2 * half + 2], w_of[m][k * P:(k + 1) * P, 2048:3072].rearrange("p (j c) -> p j c", j=2)).then_inc(w_landed[n % 4], 16)

        @block.gpsimd
        def _(pool):
            pool.memset(c_rows[:, :], 0.0).then_inc(c_ready, 1)
            pool.memset(bias[:, :, :], 0.0).then_inc(b_zero, 1)
            pool.wait_ge(b_zero, 1)
            for r in range(4):
                for j in range(4):
                    m, c0 = cols(r, j)
                    pool.dma_start(bias[BR * j:BR * j + 9, r, :], b_of[m][0:1, c0:c0 + CW].to_broadcast([9, CW])).then_inc(b_landed, 16)
            for m, g in enumerate(("a_norm_g", "kv_norm_g", "b_norm_g")):
                with nc.allow_non_contiguous_dma(reason="1024 channel gains, once"):
                    pool.dma_start(norm_g[:, m, :], dr[g].rearrange("a (k p) -> p (a k)", p=P)).then_inc(b_landed, 16)
            pool.dma_start(sel[:, :, :, :], pr.table["sel_gate"]).then_inc(b_landed, 16)
            pool.wait_ge(gate_ready, 4)
            pool.dma_start(dr["gate"], gate[:, :, :, :]).then_inc(gate_out, 16)
            pool.wait_ge(gate_out, 16)

        @block.scalar
        def _(act):
            act.wait_ge(in_landed, 48)
            act.activation(c_silu[:, :], c_rows[:, :], ACT.Silu).then_inc(s_silu, 1)

        @block.tensor
        def _(pe):
            pe.wait_ge(s_silu, 1)
            for k in range(KT):
                ins = pe.transpose(ps_c[:, k * BR:(k + 1) * BR], c_silu[:, k * P:(k + 1) * P], pr.ident[0:BR, 0:BR])
            ins.then_inc(c_turned, 1)
            pe.wait_ge(cT_ready, 1)

            def turn(r):
                pe.wait_ge(rows_ready, r + 1)
                if r:
                    pe.wait_ge(mod_ready, {2: 1, 3: 2}[r])
                for c in range(4):
                    ins = pe.transpose(ps_t[:, c * P:(c + 1) * P], rows[:, r, c * P:(c + 1) * P], pr.ident[:, :])
                ins.then_inc(turned, 1)

            landed = [0] * 4
            for r in range(4):
                if r >= 2:
                    pe.wait_ge(rows_ready, r - 1)
                for k in range(KT):
                    n = r * KT + k
                    landed[n % 4] += 16 if cols(r, 0)[0] == cols(r, 3)[0] else 32
                    pe.wait_ge(w_landed[n % 4], landed[n % 4])
                    for j in range(4):
                        ins = pe.matmul(ps_ada[BR * j:BR * (j + 1), r % 2, :], cT[:, k, :], w[:, n % 4, j, :],
                                        start=k == 0, stop=k == KT - 1, tile_position=(0, BR * j), skip_group_check=True)
                    ins.then_inc(w_read, 1)
                if r in (1, 3):
                    turn(r - 1)
            pe.wait_ge(b_landed, 20 * 16)
            for kind in range(2):
                if kind:
                    pe.wait_ge(gate_ready, 2)
                for j in range(4):
                    ins = pe.matmul(ps_g[:, j, :], sel[:, kind, j, :], rows[:, 1, :], start=True, stop=True)
                ins.then_inc(gate_done, 1)
            turn(3)

        @block.vector
        def _(dve):
            dve.sem_inc(pr.raw_split, 2)
            dve.wait_ge(c_turned, 1)
            dve.tensor_copy(cT[:, :, :], ps_c[:, 0:KT * BR]).then_inc(cT_ready, 1)

            def add_bias(r):
                dve.wait_ge(w_read, (r + 1) * KT)
                if r == 0:
                    dve.wait_ge(b_landed, 20 * 16)
                dve.tensor_tensor(rows[:, r, :], ps_ada[:, r % 2, :], bias[:, r, :], ALU.add).then_inc(rows_ready, 1)

            def modulation(r, m):
                dve.wait_ge(turned, m + 1)
                t = ps_t[:, :].rearrange("p (c j b) -> p j c b", c=4, j=4)
                for jj in range(2):
                    dve.tensor_copy(pr.mod_b[m][:, 4 * jj:4 * jj + 4, :], t[:, jj, :, 0:DEC_BATCH + 1])
                for jj in range(2):
                    for c in range(4):
                        ins = dve.tensor_scalar(pr.mod_a[m][:, 4 * jj + c, :], t[:, 2 + jj, c, 0:DEC_BATCH + 1], 1.0, norm_g[:, m, 4 * jj + c:4 * jj + c + 1], ALU.add, ALU.mult)
                ins.then_inc(mod_ready, 1)

            add_bias(0)
            add_bias(1)
            modulation(0, 0)
            add_bias(2)
            add_bias(3)
            modulation(2, 1)
            for kind in range(2):
                dve.wait_ge(gate_done, kind + 1)
                for m in range(2):
                    dve.tensor_copy(gate[:, m, kind, :], ps_g[:, 2 * m:2 * m + 2, :]).then_inc(gate_ready, 1)
            modulation(3, 2)


def project(pr, name, source, norm, mod, groups, chunk0, after, forget=False, gate_layer=None, residual=None, gain=None):
    nc, dr = pr.nc, pr.dram
    with ExitStack() as ctx:
        sb = lambda n, s, dt=F32: ctx.enter_context(nc.sbuf_tensor(f"{name}_{n}", s, dt))
        ps = lambda n, s: ctx.enter_context(nc.psum_tensor(f"{name}_{n}", s, F32))
        sem = ctx.enter_context(semaphores(nc, f"{name}_"))
        hT_hi = sb("hT_hi", [P, KT, TOKENS], F32R)
        hT_lo = sb("hT_lo", [P, KT, TOKENS], F32R)
        x = sb("x", [P, TILES * D])
        xv = x[:, :].rearrange("p (t d) -> p t d", t=TILES)
        xs = sb("xs", [P, 2, TILES * P])
        ht = sb("ht", [P, TOKENS])
        stat = sb("stat", [P, 4, TILES])
        small = sb("small", [P, 2, 4, 4])
        off = [0]

        def part_of_x(n):
            off[0] += n
            assert off[0] <= TILES * D
            return x[:, off[0] - n:off[0]]

        stage = part_of_x(4 * CW).rearrange("p (s c) -> p s c", s=4)
        ost = part_of_x(4 * CW).rearrange("p (s c) -> p s c", s=4)
        tmp = part_of_x(2 * CW).rearrange("p (s c) -> p s c", s=2)
        kinds = [g["kind"] for g in groups]
        if gain is not None:
            gain_sb = sb("gain", [P, KT])
            gain_landed = sem("gain_landed")
        if "rotary" in kinds:
            cs = part_of_x(2 * TOKENS).rearrange("p (s c) -> p s c", s=2)
        if "norm" in kinds:
            gains = part_of_x(2 * DH).rearrange("p (s c) -> p s c", s=2)
        if "residual" in kinds:
            gate = part_of_x(2 * D).rearrange("p (s c) -> p s c", s=2)
            rin = part_of_x(3 * CW).rearrange("p (s c) -> p s c", s=3)
        if forget:
            wf = sb("wf", [P, KT, FH])
            wf_hi = sb("wf_hi", [P, KT, P], F32R)
            wf_lo = sb("wf_lo", [P, KT, P], F32R)
            f_sb = part_of_x(TOKENS)[0:FH]
            wf_landed = sem("wf_landed")
        ps_t = ps("ps_t", [P, 3, 512])
        ps_o = ps("ps_o", [P, 4, 512])

        x_landed, tab_landed = sem("x_landed"), sem("tab_landed")
        sq_done, me_done, rt_done, rstd_ready = sem("sq_done"), sem("me_done"), sem("rt_done"), sem("rstd_ready")
        xs_ready, turned, ht_ready = sem("xs_ready"), sem("turned"), sem("ht_ready")
        hhi_done, h_ready = sem("hhi_done"), sem("h_ready")
        out_done = sem("out_done")
        evac = sem("evac")
        posted = sem("posted")
        stage_read = sem("stage_read")
        stored = [sem(f"stored{s}") for s in range(4)]
        rin_landed = [sem(f"rin{s}") for s in range(3)]
        dve_own = sem("dve_own")
        root_in, root_out = sem("root_in"), sem("root_out")
        f_split, f_lo, f_out, f_stored = sem("f_split"), sem("f_lo"), sem("f_out"), sem("f_stored")
        n_tab = 2 * ("rotary" in kinds) + sum(k == "norm" for k in kinds) + ("residual" in kinds)

        c0 = chunk0
        tile0 = 0
        used = [0, 0, 0, 0]
        for g in groups:
            g["c0"], g["tile0"], g["used"] = c0, tile0, list(used)
            g["tiles"] = 12 if g["kind"] == "rotary" else TILES
            g["per_slot"] = [3, 3, 3, 3] if g["kind"] == "rotary" else [3, 3, 3, 0]
            c0 += 2 * g["pairs"]
            tile0 += 2 * g["pairs"] * g["tiles"]
            used = [u + 2 * g["pairs"] * n for u, n in zip(used, g["per_slot"])]
        post = 0
        for g in groups:
            g["post0"] = post
            if g["kind"] == "rotary":
                post += g["pairs"] * 12
            elif g["kind"] in ("norm", "residual"):
                post += g["pairs"] * 2 * TILES
        all_stored = [16 + 16 * u for u in used]

        def pairs(eng, g, body):
            last = g is groups[-1]
            looped = g["pairs"] - 1 if last and after is None else g["pairs"]
            if looped > 1:
                with eng.Fori(0, looped) as i:
                    for s in range(2):
                        body(i, s, False)
            else:
                for i in range(looped):
                    for s in range(2):
                        body(i, s, False)
            for i in range(looped, g["pairs"]):
                for s in range(2):
                    body(i, s, s == 1)

        block = ctx.enter_context(nc.Block())

        @block.sync
        def _(sp):
            for t in range(TILES):
                sp.dma_start(xv[:, t], source(t)).then_inc(x_landed, 16)
            if gain is not None:
                with nc.allow_non_contiguous_dma(reason="1024 channel gains, once"):
                    sp.dma_start(gain_sb[:, :], gain.rearrange("a (k p) -> p (a k)", p=P)).then_inc(gain_landed, 16)
            if forget:
                with nc.allow_non_contiguous_dma(reason="eight columns"):
                    sp.dma_start(wf[:, :, :], dr["kv_w"][:, 2 * CW:2 * CW + FH].rearrange("(k p) c -> p k c", p=P)).then_inc(wf_landed, 16)
            if chunk0 == 0:
                load_chunk(pr, sp, groups[0]["weights"][0], 0)
            sp.wait_ge(h_ready, KT + 1)
            if "rotary" in kinds:
                sp.dma_start(cs[:, 0], pr.table["cos"]).then_inc(tab_landed, 16)
                sp.dma_start(cs[:, 1], pr.table["sin"]).then_inc(tab_landed, 16)
            for n, g in enumerate(g for g in groups if g["kind"] == "norm"):
                sp.dma_start(gains[:, n], g["gain"].to_broadcast([P, DH])).then_inc(tab_landed, 16)
            if "residual" in kinds:
                sp.dma_start(gate[:, :, :], dr["gate"][:, gate_layer]).then_inc(tab_landed, 16)

            chunks = [w for g in groups for w in g["weights"]][1:] + ([after] if after else [])
            for n, w in enumerate(chunks):
                load_chunk(pr, sp, w, chunk0 + n + 1)

        @block.gpsimd
        def _(pool):
            credit(pool, pr, stored)
            if norm:
                pool.wait_ge(rstd_ready, 1)
            else:
                pool.wait_ge(x_landed, 16 * TILES)
            with pool.Fori(0, KT // 2) as i:
                for s in range(2):
                    pool.wait_ge(turned, i * 2 + s + 1)
                    stand(pool, pr)
                    src = xv[:, :, bass.ds((i * 2 + s) * P, P)]
                    dst = xs[:, s].rearrange("p (t c) -> p t c", t=TILES)
                    if norm:
                        pool.tensor_tensor(dst, src, stat[:, 3, :].rearrange("p (t o) -> p t o", o=1).to_broadcast([P, TILES, P]), ALU.mult).then_inc(xs_ready, 1)
                    else:
                        pool.tensor_copy(dst, src).then_inc(xs_ready, 1)
            pool.wait_ge(h_ready, KT + 1)
            if forget:
                pool.wait_ge(f_out, 1)
                pool.dma_start(dr["f_raw"], f_sb[:, :]).then_inc(f_stored, 16)
                pool.wait_ge(f_stored, 16)
            for g in groups:
                def body(i, s, stop, g=g):
                    base = g["tile0"] + (2 * i + s) * g["tiles"]
                    kind = "copy" if g.get("plain") == s else g["kind"]
                    ready = evac if kind in ("copy", "silu") else posted
                    if g["kind"] == "residual":
                        def load(t):
                            n = base + t
                            pool.wait_ge(posted, n + 1)
                            pool.dma_start(rin[:, t % 3], residual(2 * i + s, t)).then_inc(rin_landed[t % 3], 16)
                        for t in range(3):
                            load(t)
                    if g["kind"] == "rotary":
                        for u in range(6):
                            pool.wait_ge(posted, (base // 2 if isinstance(base, int) else (g["tile0"] // 2 + (2 * i + s) * 6)) + u + 1)
                            for half in range(2):
                                m = 2 * u + half
                                pool.dma_start(g["store"](2 * i + s, m), ost[:, m % 4, 0:NB3]).then_inc(stored[m % 4], 16)
                    else:
                        credit = {"copy": 4, "silu": 4, "residual": 3, "norm": 0}[kind]
                        if ready is posted:
                            first = g["post0"]
                            base2 = first + (2 * i + s) * g["tiles"]
                        else:
                            base2 = base
                        for t in range(TILES):
                            pool.wait_ge(ready, credit + base2 + t + 1)
                            pool.dma_start(g["store"](2 * i + s, t), ost[:, t % 3, :]).then_inc(stored[t % 3], 16)
                            if g["kind"] == "residual" and t + 3 < TILES:
                                load(t + 3)
                pairs(pool, g, body)
            for s in range(4):
                pool.wait_ge(stored[s], all_stored[s])

        @block.scalar
        def _(act):
            act.sem_inc(evac, 4)
            if norm:
                for t in range(TILES):
                    if t == 0:
                        act.wait_ge(x_landed, 16 * TILES)
                    act.activation(ht[:, 0:D] if t % 2 else xs[:, 0, 0:D], xv[:, t], ACT.Square, accum_out=stat[:, 0, t:t + 1]).then_inc(sq_done, 1)
                    act.wait_ge(sq_done, t + 1)
                act.wait_ge(me_done, 1)
                act.activation(stat[:, 2, :], stat[:, 1, :], ACT.Sqrt).then_inc(rt_done, 1)
            if chunk0 == 0:
                for sub in range(SUBS):
                    split_hi(pr, act, 0, 0, sub)
            with act.Fori(0, KT) as d:
                if mod is not None or gain is not None:
                    act.wait_ge(ht_ready, d + 1)
                    act.copy(hT_hi[:, bass.ds(d, 1), :].rearrange("p a c -> p (a c)"), ht[:, :]).then_inc(hhi_done, 1)
                else:
                    act.wait_ge(turned, d + 3)
                    act.copy(hT_hi[:, bass.ds(d, 1), :].rearrange("p a (b c) -> p (a b) c", b=3), ps_t[:, :, 0:NB3]).then_inc(hhi_done, 1)
            act.wait_ge(h_ready, KT + 1)
            if forget:
                act.wait_ge(f_split, 1)
                act.copy(wf_hi[:, :, 0:FH], wf[:, :, :]).then_inc(hhi_done, 1)
            for g in groups:
                def body(i, s, stop, g=g):
                    c = g["c0"] + 2 * i + s
                    base = g["tile0"] + (2 * i + s) * g["tiles"]
                    k = "copy" if g.get("plain") == s else g["kind"]
                    seen = [0, 0, 0, 0]
                    for t in range(g["tiles"]):
                        slot = t % 4 if k == "rotary" else t % 3
                        width = NB3 if k == "rotary" else CW
                        act.wait_ge(out_done, base + t + 1)
                        if k in ("copy", "silu"):
                            act.wait_ge(stored[slot], 16 * (g["used"][slot] + 1 + seen[slot]) + (2 * i + s) * 16 * g["per_slot"][slot])
                            seen[slot] += 1
                            act.activation(ost[:, slot, :], ps_o[:, slot, :], ACT.Silu if k == "silu" else ACT.Copy).then_inc(evac, 1)
                        else:
                            if k == "rotary":
                                act.wait_ge(stage_read, (2 * i + s) * 6 + t // 2 + 1)
                            else:
                                act.wait_ge(stage_read, g["post0"] + (2 * i + s) * TILES + t + 1)
                            act.copy(stage[:, slot, 0:width], ps_o[:, slot, 0:width]).then_inc(evac, 1)
                        if k == "norm":
                            n = g["post0"] + (2 * i + s) * TILES + t
                            act.wait_ge(root_in, n + 1)
                            act.activation(small[:, 0, 2, :], small[:, 0, 1, :], ACT.Sqrt).then_inc(root_out, 1)
                        if t % 2 and t < 2 * SUBS and not stop:
                            split_hi(pr, act, c + 1, 1 - s, t // 2)
                pairs(act, g, body)

        @block.tensor
        def _(pe):
            pe.sem_inc(turned, 2)
            with pe.Fori(0, KT // 2) as i:
                for s in range(2):
                    d = i * 2 + s
                    pe.wait_ge(xs_ready, d + 1)
                    pe.wait_ge(h_ready, d + 1)
                    for t in range(TILES):
                        ins = pe.transpose(ps_t[:, t // 3, (t % 3) * P:(t % 3 + 1) * P], xs[:, s, t * P:(t + 1) * P], pr.ident[:, :])
                    ins.then_inc(turned, 1)
            pe.wait_ge(h_ready, KT + 1)
            if forget:
                pe.wait_ge(f_lo, 1)
                for n in range(3):
                    for k in range(KT):
                        for m, (a, b) in enumerate(((wf_hi, hT_hi), (wf_lo, hT_hi), (wf_hi, hT_lo))):
                            ins = pe.matmul(ps_t[:, n, 0:NB3], a[:, k, :], b[:, k, n * NB3:(n + 1) * NB3], start=k + m == 0, stop=k == KT - 1 and m == 2)
                ins.then_inc(f_lo, 1)
            for g in groups:
                def body(i, s, stop, g=g):
                    c = g["c0"] + 2 * i + s
                    base = g["tile0"] + (2 * i + s) * g["tiles"]
                    pe.wait_ge(pr.raw_split, SUBS * c + SUBS + 2)
                    for t in range(g["tiles"]):
                        if g["kind"] == "rotary":
                            pe.wait_ge(evac, base + t + 1)
                            part, n, half = t // 6, t % 6 // 2, t % 2
                            w0 = part * DK + half * P
                            for k in range(KT):
                                for m, (w, h) in enumerate(((pr.w_hi, hT_hi), (pr.w_hi, hT_lo), (pr.w_lo, hT_hi))):
                                    ins = pe.matmul(ps_o[:, t % 4, 0:NB3], w[:, s, k, w0:w0 + P], h[:, k, n * NB3:(n + 1) * NB3],
                                                    start=k + m == 0, stop=k == KT - 1 and m == 2)
                        else:
                            pe.wait_ge(evac, base + t + 2)
                            for k in range(KT):
                                for m, (h, w) in enumerate(((hT_hi, pr.w_hi), (hT_hi, pr.w_lo), (hT_lo, pr.w_hi))):
                                    ins = pe.matmul(ps_o[:, t % 3, :], h[:, k, t * P:(t + 1) * P], w[:, s, k, :],
                                                    start=k + m == 0, stop=k == KT - 1 and m == 2)
                        ins.then_inc(out_done, 1)
                pairs(pe, g, body)

        @block.vector
        def _(dve):
            chain = Chain(dve, dve_own)
            dve.sem_inc(h_ready, 1)
            if norm:
                dve.wait_ge(sq_done, TILES)
                dve.tensor_scalar(stat[:, 1, :], stat[:, 0, :], 1.0 / D, EPS, ALU.mult, ALU.add).then_inc(me_done, 1)
                dve.wait_ge(rt_done, 1)
                dve.reciprocal(stat[:, 3, :], stat[:, 2, :]).then_inc(rstd_ready, 1)
            if chunk0 == 0:
                for sub in range(SUBS):
                    split_lo(pr, dve, 0, 0, sub)
            if kinds[0] == "rotary":
                dve.sem_inc(stage_read, 2)
            elif kinds[0] in ("norm", "residual"):
                dve.sem_inc(stage_read, 3)
            if "residual" in kinds:
                dve.sem_inc(posted, 3)
            if gain is not None:
                dve.wait_ge(gain_landed, 16)
            with dve.Fori(0, KT) as d:
                dve.wait_ge(turned, d + 3)
                hd = lambda a: a[:, bass.ds(d, 1), :].rearrange("p a c -> p (a c)")
                if mod is not None:
                    A, B = pr.mod_a[mod], pr.mod_b[mod]
                    dve.wait_ge(h_ready, d + 1)
                    sc = [z[:, bass.ds(d, 1), DEC_BATCH:DEC_BATCH + 1].rearrange("p a b -> p (a b)") for z in (A, B)]
                    dve.tensor_scalar(ht[:, 0:2 * NB3].rearrange("p (a c) -> p a c", a=2), ps_t[:, 0:2, 0:NB3], sc[0], sc[1], ALU.mult, ALU.add)
                    dve.tensor_scalar(ht[:, 2 * NB3:SEQ], ps_t[:, 2, 0:SEQ - 2 * NB3], sc[0], sc[1], ALU.mult, ALU.add)
                    smp = ht[:, SEQ:TOKENS].rearrange("p (b s) -> p b s", b=DEC_BATCH)
                    per = [z[:, bass.ds(d, 1), 0:DEC_BATCH].rearrange("p a (b o) -> p (a b) o", o=1).to_broadcast([P, DEC_BATCH, DEC_SEQ]) for z in (A, B)]
                    dve.tensor_tensor(smp, ps_t[:, 2, SEQ - 2 * NB3:NB3].rearrange("p (b s) -> p b s", b=DEC_BATCH), per[0], ALU.mult).then_inc(dve_own, 1)
                    dve.wait_ge(dve_own, d + 1)
                    dve.tensor_tensor(smp, smp, per[1], ALU.add).then_inc(ht_ready, 1)
                    dve.wait_ge(hhi_done, d + 1)
                    dve.tensor_tensor(hd(hT_lo), ht[:, :], hd(hT_hi).bitcast(F32), ALU.subtract).then_inc(h_ready, 1)
                elif gain is not None:
                    dve.wait_ge(h_ready, d + 1)
                    dve.tensor_scalar(ht[:, :].rearrange("p (a c) -> p a c", a=3), ps_t[:, :, 0:NB3], gain_sb[:, bass.ds(d, 1)], None, ALU.mult).then_inc(ht_ready, 1)
                    dve.wait_ge(hhi_done, d + 1)
                    dve.tensor_tensor(hd(hT_lo), ht[:, :], hd(hT_hi).bitcast(F32), ALU.subtract).then_inc(h_ready, 1)
                else:
                    dve.wait_ge(hhi_done, d + 1)
                    v3 = lambda a: a[:, bass.ds(d, 1), :].rearrange("p a (b c) -> p (a b) c", b=3)
                    dve.tensor_tensor(v3(hT_lo), ps_t[:, :, 0:NB3], v3(hT_hi).bitcast(F32), ALU.subtract).then_inc(h_ready, 1)
            chain.n = KT if mod is not None else 0
            if forget:
                chain.link(dve.memset(wf_hi[:, :, :].bitcast(F32), 0.0))
                chain.link(dve.memset(wf_lo[:, :, :].bitcast(F32), 0.0))
                dve.wait_ge(wf_landed, 16)
                dve.sem_inc(f_split, 1)
                dve.wait_ge(hhi_done, KT + 1)
                dve.tensor_tensor(wf_lo[:, :, 0:FH], wf[:, :, :], wf_hi[:, :, 0:FH].bitcast(F32), ALU.subtract).then_inc(f_lo, 1)
                dve.wait_ge(f_lo, 2)
                dve.tensor_copy(f_sb[:, :].rearrange("p (a c) -> p a c", a=3), ps_t[0:FH, :, 0:NB3]).then_inc(f_out, 1)
            if n_tab:
                dve.wait_ge(tab_landed, 16 * n_tab)
            norm_no = 0
            for g in groups:
                k = g["kind"]
                per_chunk = {"rotary": 36, "norm": 5 * TILES, "residual": TILES, "copy": 0, "silu": 0}[k]
                start = chain.n

                def body(i, s, stop, g=g, k=k, per_chunk=per_chunk, start=start, nn=norm_no):
                    if g.get("plain") == s:
                        k, per_chunk = "copy", 0
                    c = g["c0"] + 2 * i + s
                    base = g["tile0"] + (2 * i + s) * g["tiles"]
                    chain.base = (2 * i + s) * per_chunk
                    chain.n = start
                    seen = [0, 0, 0, 0]

                    def free(slot):
                        dve.wait_ge(stored[slot], 16 * (g["used"][slot] + 1 + seen[slot]) + (2 * i + s) * 16 * g["per_slot"][slot])
                        seen[slot] += 1
                    for t in range(g["tiles"]):
                        slot = t % 3
                        if k == "rotary" and t % 2:
                            n = t % 6 // 2
                            dve.wait_ge(evac, 4 + base + t + 1)
                            x1, x2 = stage[:, (t - 1) % 4, 0:NB3], stage[:, t % 4, 0:NB3]
                            co, si = cs[:, 0, n * NB3:(n + 1) * NB3], cs[:, 1, n * NB3:(n + 1) * NB3]
                            a, b = tmp[:, 0, 0:NB3], tmp[:, 1, 0:NB3]
                            free((t - 1) % 4)
                            free(t % 4)
                            chain.link(dve.tensor_tensor(a, x1, co, ALU.mult))
                            chain.link(dve.tensor_tensor(b, x2, si, ALU.mult))
                            chain.link(dve.tensor_tensor(ost[:, (t - 1) % 4, 0:NB3], a, b, ALU.subtract))
                            chain.link(dve.tensor_tensor(a, x2, co, ALU.mult))
                            chain.link(dve.tensor_tensor(b, x1, si, ALU.mult))
                            dve.sem_inc(stage_read, 1)
                            chain.link(dve.tensor_tensor(ost[:, t % 4, 0:NB3], a, b, ALU.add))
                            dve.sem_inc(posted, 1)
                        elif k == "norm":
                            st = stage[:, slot, :].rearrange("p (h c) -> p h c", h=4)
                            os = ost[:, slot, :].rearrange("p (h c) -> p h c", h=4)
                            dve.wait_ge(evac, 4 + base + t + 1)
                            free(slot)
                            chain.link(dve.tensor_tensor(tmp[:, 0, :], stage[:, slot, :], stage[:, slot, :], ALU.mult))
                            chain.link(dve.tensor_reduce(small[:, 0, 0, :], tmp[:, 0, :].rearrange("p (h c) -> p h c", h=4), AX.X, ALU.add))
                            n = g["post0"] + (2 * i + s) * TILES + t
                            dve.tensor_scalar(small[:, 0, 1, :], small[:, 0, 0, :], 1.0 / DH, EPS, ALU.mult, ALU.add).then_inc(root_in, 1)
                            dve.wait_ge(root_out, n + 1)
                            chain.link(dve.reciprocal(small[:, 0, 3, :], small[:, 0, 2, :]))
                            r = small[:, 0, 3, :].rearrange("p (h o) -> p h o", o=1).to_broadcast([P, 4, DH])
                            gb = gains[:, nn:nn + 1, :].to_broadcast([P, 4, DH])
                            t4 = tmp[:, 1, :].rearrange("p (h c) -> p h c", h=4)
                            chain.link(dve.tensor_tensor(t4, st, r, ALU.mult))
                            dve.sem_inc(stage_read, 1)
                            if g["scale"] != 1.0:
                                chain.link(dve.scalar_tensor_tensor(os, t4, g["scale"], gb, ALU.mult, ALU.mult))
                            else:
                                chain.link(dve.tensor_tensor(os, t4, gb, ALU.mult))
                            dve.sem_inc(posted, 1)
                        elif k == "residual":
                            dve.wait_ge(evac, 4 + base + t + 1)
                            free(slot)
                            col = g["col"](i, s)
                            dve.wait_ge(posted, base + max(t, 1) + 2)
                            chain.link(dve.tensor_tensor(tmp[:, t % 2, :], stage[:, slot, :], gate[:, int(t == PT), col:col + CW], ALU.mult))
                            dve.sem_inc(stage_read, 1)
                            dve.wait_ge(rin_landed[t % 3], 16 * (3 * (2 * i + s) + t // 3 + 1))
                            dve.tensor_tensor(ost[:, slot, :], tmp[:, t % 2, :], rin[:, t % 3], ALU.add).then_inc(posted, 1)
                        if t % 2 and t < 2 * SUBS and not stop:
                            split_lo(pr, dve, c + 1, 1 - s, t // 2)
                    assert chain.n - start == per_chunk, (chain.n, start)
                norm_no += k == "norm"
                pairs(dve, g, body)
                chain.n = start + 2 * g["pairs"] * per_chunk
                chain.base = 0


def retention(pr):
    nc, dr = pr.nc, pr.dram
    NH2 = DK // P
    with ExitStack() as ctx:
        sb = lambda n, s, dt=F32: ctx.enter_context(nc.sbuf_tensor(f"ret_{n}", s, dt))
        ps = lambda n, s: ctx.enter_context(nc.psum_tensor(f"ret_{n}", s, F32))
        sem = ctx.enter_context(semaphores(nc, "ret_"))
        qT = sb("qT", [P, NH2, TOKENS])
        kT = sb("kT", [P, NH2, TOKENS])
        v = sb("v", [P, TILES, DV])
        g = sb("g", [P, TILES, DV])
        intra = sb("intra", [P, 2, RH, P])
        qdec = sb("qdec", [P, RH, 3, P])
        kdec = sb("kdec", [P, RH, 1 + DEC_BATCH])
        cdec = sb("cdec", [P, 2, RH])
        s_in = sb("s_in", [P, 2, P])
        k_tok = sb("k_tok", [P, 2, DK])
        k_str = sb("k_str", [P, 2, DK])
        q_dec = sb("q_dec", [P, 2, NH2, P])
        state = sb("state", [P, 2, NH2, DV])
        r_in = sb("r_in", [P, 2, 4, NH2, DV])
        normed = sb("normed", [P, 2, DV])
        ost = sb("ost", [P, 2, DV])
        st6 = sb("st6", [P, 2, 6])
        mv = sb("mv", [P, 2, 2])
        sc = sb("sc", [P, 2, 4])
        ps_s = ps("ps_s", [P, 2, 512])
        ps_o = ps("ps_o", [P, 2, 512])
        ps_u = ps("ps_u", [P, 2, 2, 512])
        tabs, q_in, v_in, g_in = sem("tabs"), sem("q_in"), sem("v_in"), sem("g_in")
        r_landed = [sem(f"r_landed{i}") for i in range(2)]
        r_stored = [sem(f"r_stored{i}") for i in range(2)]
        ost_stored = [sem(f"ost_stored{i}") for i in range(2)]
        p_stored = sem("p_stored")
        scored, decayed, q_ready = sem("scored"), sem("decayed"), sem("q_ready")
        upd, state_new, str_k, o_done = sem("upd"), sem("state_new"), sem("str_k"), sem("o_done")
        own, var, root, scaled, n_done, gated = sem("own"), sem("var"), sem("root"), sem("scaled"), sem("n_done"), sem("gated")
        head_done = sem("head_done")
        PAIRS = DEC_BATCH
        U = PT + PAIRS
        block = ctx.enter_context(nc.Block())

        @block.sync
        def _(sp):
            sp.dma_start(intra[:, 0], pr.table["intra"]).then_inc(tabs, 16)
            sp.dma_start(intra[:, 1], pr.table["intra_s"]).then_inc(tabs, 16)
            sp.dma_start(qdec[:, :, 0], pr.table["qdec"]).then_inc(tabs, 16)
            sp.dma_start(qdec[:, :, 1:3], pr.table["qdec_s"]).then_inc(tabs, 16)
            with nc.allow_non_contiguous_dma(reason="small tables, once"):
                sp.dma_start(kdec[:, :, 0:1], pr.table["kdec"]).then_inc(tabs, 16)
                sp.dma_start(kdec[:, :, 1:], pr.table["kdec_s"]).then_inc(tabs, 16)
            sp.dma_start(cdec[:, 0], pr.table["cdec"]).then_inc(tabs, 16)
            sp.dma_start(cdec[:, 1], pr.table["cdec_s"]).then_inc(tabs, 16)
            with sp.Fori(0, RH) as h:
                sp.wait_ge(o_done, h * TILES + 1)
                sp.wait_ge(q_ready, h * TILES + 1)
                sp.wait_ge(upd, h * U + 1)
                sp.dma_start(kT[:, :, :], dr["qkT"][bass.ds(h * 4 + 2, 2)].rearrange("a p t -> p a t")).then_inc(q_in, 16)
                sp.dma_start(qT[:, :, :], dr["qkT"][bass.ds(h * 4, 2)].rearrange("a p t -> p a t")).then_inc(q_in, 16)
                sp.dma_start(v[:, :, :], dr["v"][:, bass.ds(h * DV, DV)].rearrange("(t p) c -> p t c", p=P)).then_inc(v_in, 16)
                sp.wait_ge(gated, h * TILES + 1)
                sp.dma_start(g[:, :, :], dr["g"][:, bass.ds(h * DV, DV)].rearrange("(t p) c -> p t c", p=P)).then_inc(g_in, 16)
                for par in range(2):
                    sp.wait_ge(r_stored[par], h * 64 + 64)
                    for j in range(4):
                        sp.dma_start(r_in[:, par, j], dr["state_ret"][2 * j + par, bass.ds(h, 1)].rearrange("o (a p) c -> p (o a) c", p=P)).then_inc(r_landed[par], 16)

        @block.tensor
        def _(pe):
            pe.sem_inc(o_done, 1)
            pe.sem_inc(upd, 1)
            with pe.Fori(0, RH) as h:
                def scores(c):
                    pe.wait_ge(decayed, h * TILES + max(c, 1) + 1)
                    for a in range(NH2):
                        pe.matmul(ps_s[:, c % 2, 0:P], kT[:, a, c * P:(c + 1) * P], qT[:, a, c * P:(c + 1) * P], start=a == 0, stop=a == NH2 - 1)
                    for a in range(NH2):
                        ins = pe.transpose(ps_s[:, c % 2, P + a * P:P + (a + 1) * P], kT[:, a, c * P:(c + 1) * P], pr.ident[:, :])
                    ins.then_inc(scored, 1)

                def output(c):
                    o = ps_o[:, c % 2, :]
                    pe.wait_ge(n_done, h * TILES + max(c, 1) + 1)
                    pe.wait_ge(decayed, h * TILES + c + 3)
                    ins = pe.matmul(o, s_in[:, c % 2, :], v[:, c, :], start=True, stop=c == 0)
                    if c:
                        pe.wait_ge(q_ready, h * TILES + c + 2)
                        pe.wait_ge(state_new, h * U + c + 1)
                        for a in range(NH2):
                            ins = pe.matmul(o, q_dec[:, c % 2, a, :], state[:, (c - 1) % 2, a, :], start=False, stop=a == NH2 - 1)
                    ins.then_inc(o_done, 1)

                def update(n, keys):
                    pe.wait_ge(state_new, h * U + max(n, 1))
                    c = min(n, PT)
                    for a in range(NH2):
                        ins = pe.matmul(ps_u[:, n % 2, a, :], keys[:, a * P:(a + 1) * P], v[:, c, :], start=True, stop=True)
                    ins.then_inc(upd, 1)

                pe.wait_ge(q_in, h * 32 + 32)
                scores(0)
                pe.wait_ge(v_in, h * 16 + 16)
                for c in range(PT):
                    scores(c + 1)
                    pe.wait_ge(decayed, h * TILES + c + 3)
                    update(c, k_tok[:, c % 2, :])
                    output(c)
                pe.wait_ge(n_done, h * TILES + PT + 1)
                pe.wait_ge(decayed, h * TILES + PT + 3)
                pe.wait_ge(q_ready, h * TILES + PT + 2)
                pe.matmul(ps_o[:, PT % 2, :], s_in[:, PT % 2, :], v[:, PT, :], start=True, stop=False, skip_group_check=True)
                for par in range(2):
                    pe.wait_ge(r_landed[par], h * 64 + 64)
                    for a in range(NH2):
                        for j in range(4):
                            ins = pe.matmul(ps_o[BR * j:BR * (j + 1), PT % 2, :], q_dec[:, par, a, BR * j:BR * (j + 1)], r_in[:, par, j, a, :],
                                            start=False, stop=par == 1 and a == NH2 - 1, tile_position=(0, BR * j), skip_group_check=True)
                ins.then_inc(o_done, 1)
                for m in range(PAIRS):
                    pe.wait_ge(str_k, h * PAIRS + m + 1)
                    update(PT + m, k_str[:, m % 2, :])

        @block.gpsimd
        def _(pool):
            credit(pool, pr, ost_stored)
            pool.sem_inc(q_ready, 1)
            pool.sem_inc(gated, 1)
            pool.wait_ge(tabs, 8 * 16)
            with pool.Fori(0, RH) as h:
                pool.wait_ge(q_in, h * 32 + 32)
                stand(pool, pr)

                def queries(c):
                    if c < PT:
                        if c >= 2:
                            pool.wait_ge(o_done, h * TILES + c)
                            stand(pool, pr)
                        for a in range(NH2):
                            ins = pool.tensor_tensor(q_dec[:, c % 2, a, :], qT[:, a, c * P:(c + 1) * P], qdec[:, bass.ds(h, 1), 0, :].rearrange("p o i -> p (o i)"), ALU.mult)
                    else:
                        pool.wait_ge(o_done, h * TILES + PT + 1)
                        stand(pool, pr)
                        for par in range(2):
                            for a in range(NH2):
                                ins = pool.tensor_tensor(q_dec[:, par, a, :], qT[:, a, PT * P:], qdec[:, bass.ds(h, 1), 1 + par, :].rearrange("p o i -> p (o i)"), ALU.mult)
                    ins.then_inc(q_ready, 1)

                def gate_and_store(c):
                    pool.wait_ge(scaled, h * TILES + c + 1)
                    if c == 0:
                        pool.wait_ge(g_in, h * 16 + 16)
                    pool.wait_ge(ost_stored[c % 2], h * 16 * (5 - c % 2) + 16 * (c // 2) + 16)
                    pool.tensor_tensor(ost[:, c % 2, :], normed[:, c % 2, :], g[:, c, :], ALU.mult).then_inc(gated, 1)
                    pool.wait_ge(gated, h * TILES + c + 2)
                    pool.dma_start(dr["o"][c * P:(c + 1) * P, bass.ds(h * DV, DV)], ost[:, c % 2, :]).then_inc(ost_stored[c % 2], 16)

                queries(0)
                for c in range(TILES):
                    if c + 1 < TILES:
                        queries(c + 1)
                    gate_and_store(c)
            pool.wait_ge(ost_stored[0], 16 + RH * 16 * 5)
            pool.wait_ge(ost_stored[1], 16 + RH * 16 * 4)

        @block.scalar
        def _(act):
            act.sem_inc(n_done, 2)
            act.sem_inc(p_stored, 16)
            for s in range(2):
                act.sem_inc(r_stored[s], 64)
            with act.Fori(0, RH) as h:
                for c in range(TILES):
                    act.wait_ge(var, h * TILES + c + 1)
                    act.activation(sc[:, c % 2, 1:2], sc[:, c % 2, 0:1], ACT.Sqrt).then_inc(root, 1)
                    act.wait_ge(own, h * 6 * TILES + 6 * c + 6)
                    act.wait_ge(gated, h * TILES + c) if c >= 2 else act.wait_ge(gated, h * TILES + 1)
                    act.activation(normed[:, c % 2, :], ps_o[:, c % 2, :], ACT.Identity, bias=sc[:, c % 2, 3:4], scale=sc[:, c % 2, 2:3]).then_inc(scaled, 1)
                    act.wait_ge(scaled, h * TILES + c + 1)
                    act.sem_inc(n_done, 1)
                act.wait_ge(state_new, h * U + PT + 1)
                act.dma_start(dr["state_prompt"][bass.ds(h, 1)].rearrange("o (a p) c -> p (o a) c", p=P), state[:, (PT - 1) % 2]).then_inc(p_stored, 16)
                for m in range(PAIRS):
                    par, j = m // 4, m % 4
                    act.wait_ge(state_new, h * U + PT + m + 2)
                    act.dma_start(dr["state_sample"][2 * j + par, bass.ds(h, 1)].rearrange("o (a p) c -> p (o a) c", p=P), r_in[:, par, j]).then_inc(r_stored[par], 16)
            act.wait_ge(p_stored, 16 + 16 * RH)
            for s in range(2):
                act.wait_ge(r_stored[s], 64 + 64 * RH)

        def stream_state(dve, h, m):
            par, j = m // 4, m % 4
            dve.wait_ge(upd, h * U + PT + m + 2)
            dve.scalar_tensor_tensor(r_in[:, par, j], r_in[:, par, j], cdec[:, 1, bass.ds(h, 1)], ps_u[:, (PT + m) % 2], ALU.mult, ALU.add).then_inc(state_new, 1)

        @block.vector
        def _(dve):
            dve.sem_inc(decayed, 2)
            dve.sem_inc(state_new, 1)
            dve.wait_ge(tabs, 8 * 16)
            with dve.Fori(0, RH) as h:
                def decay(c):
                    dve.wait_ge(scored, h * TILES + c + 1)
                    if c >= 2:
                        dve.wait_ge(o_done, h * TILES + c)
                        dve.wait_ge(upd, h * U + c)
                    else:
                        dve.wait_ge(o_done, h * TILES + 1)
                        dve.wait_ge(upd, h * U + 1)
                    dve.tensor_tensor(s_in[:, c % 2, :], ps_s[:, c % 2, 0:P], intra[:, int(c == PT), bass.ds(h, 1), :].rearrange("p o i -> p (o i)"), ALU.mult)
                    if c < PT:
                        dve.tensor_scalar(k_tok[:, c % 2, :], ps_s[:, c % 2, P:3 * P], kdec[:, bass.ds(h, 1), 0:1].rearrange("p o i -> p (o i)"), None, ALU.mult).then_inc(decayed, 1)
                    else:
                        dve.tensor_copy(k_tok[:, c % 2, :], ps_s[:, c % 2, P:3 * P]).then_inc(decayed, 1)

                def new_state(c):
                    dve.wait_ge(upd, h * U + c + 2)
                    if c == 0:
                        dve.tensor_copy(state[:, 0], ps_u[:, 0]).then_inc(state_new, 1)
                    else:
                        dve.wait_ge(state_new, h * U + c + 1)
                        dve.scalar_tensor_tensor(state[:, c % 2], state[:, (c - 1) % 2], cdec[:, 0, bass.ds(h, 1)], ps_u[:, c % 2], ALU.mult, ALU.add).then_inc(state_new, 1)

                def statistics(c):
                    dve.wait_ge(o_done, h * TILES + c + 2)
                    n = h * 6 * TILES + 6 * c
                    s, z = c % 2, sc[:, c % 2, :]
                    dve.wait_ge(n_done, h * TILES + max(c, 1) + 1)
                    dve.bn_stats(st6[:, s, :], ps_o[:, s, :]).then_inc(own, 1)
                    dve.wait_ge(own, n + 1)
                    stand(dve, pr)
                    dve.bn_aggr(mv[:, s, :], st6[:, s, :]).then_inc(own, 1)
                    dve.wait_ge(own, n + 2)
                    dve.tensor_scalar(z[:, 0:1], mv[:, s, 1:2], EPS, None, ALU.add).then_inc(own, 1)
                    dve.wait_ge(own, n + 3)
                    dve.sem_inc(var, 1)
                    dve.wait_ge(root, h * TILES + c + 1)
                    dve.reciprocal(z[:, 2:3], z[:, 1:2]).then_inc(own, 1)
                    dve.wait_ge(own, n + 4)
                    dve.tensor_scalar(z[:, 3:4], mv[:, s, 0:1], z[:, 2:3], None, ALU.mult).then_inc(own, 1)
                    dve.wait_ge(own, n + 5)
                    dve.tensor_scalar(z[:, 3:4], z[:, 3:4], -1.0, None, ALU.mult).then_inc(own, 1)

                decay(0)
                for c in range(PT):
                    decay(c + 1)
                    if c == 0:
                        dve.wait_ge(p_stored, h * 16 + 16)
                    new_state(c)
                    statistics(c)
                statistics(PT)
                dve.wait_ge(decayed, h * TILES + TILES + 2)
                for m in range(PAIRS):
                    par, j = m // 4, m % 4
                    dve.wait_ge(upd, h * U + PT + m) if m >= 2 else None
                    dve.tensor_scalar(k_str[:, m % 2, :], k_tok[:, PT % 2, :], kdec[:, bass.ds(h, 1), 1 + 2 * j + par:2 + 2 * j + par].rearrange("p o i -> p (o i)"), None, ALU.mult).then_inc(str_k, 1)
                    if m:
                        stream_state(dve, h, m - 1)
                stream_state(dve, h, PAIRS - 1)


def attention(pr):
    nc, dr = pr.nc, pr.dram
    G = FH // KVH
    UNITS = G * PT + 2
    SCALE_L = (PT + 1) * P
    blocks = [u // G + 1 for u in range(G * PT)] + [2, 2]
    groups = [-(-b // 4) for b in blocks]
    first = [sum(groups[:u]) for u in range(UNITS + 1)]
    GROUPS = first[-1]
    with ExitStack() as ctx:
        sb = lambda n, s, dt=F32: ctx.enter_context(nc.sbuf_tensor(f"fox_{n}", s, dt))
        ps = lambda n, s: ctx.enter_context(nc.psum_tensor(f"fox_{n}", s, F32))
        sem = ctx.enter_context(semaphores(nc, "fox_"))
        work = sb("work", [P, 4 * TOKENS + 2 * SEQ])
        f_tmp = work[0:FH, 0:3 * TOKENS].rearrange("p (a c) -> p a c", a=3)
        f_in = work[0:FH, 3 * TOKENS:4 * TOKENS]
        ones = work[0:FH, 4 * TOKENS:4 * TOKENS + SEQ]
        c_logf = work[0:FH, 4 * TOKENS + SEQ:4 * TOKENS + 2 * SEQ]
        qT = work[:, 0:2 * SEQ].rearrange("p (a c) -> p a c", a=G)
        s_sb = work[:, 2 * SEQ:4 * SEQ].rearrange("p (a c) -> p a c", a=2)
        pT = work[:, 4 * SEQ:5 * SEQ].rearrange("p (a c) -> p a c", a=2)
        kT = work[:, 5 * SEQ:5 * SEQ + TILES * P]
        f_bias = sb("f_bias", [FH, 1])
        logf = sb("logf", [FH, TOKENS])
        logf_tok = sb("logf_tok", [P, TILES, FH])
        c_tok = sb("c_tok", [P, DEC_BATCH, FH])
        cum = sb("cum", [FH, SEQ])
        cum_c = sb("cum_c", [FH, DEC_BATCH * PAST])
        cum_n = sb("cum_n", [FH, P])
        sel_head = sb("sel_head", [FH, FH, P])
        sel_group = sb("sel_group", [FH, KVH, P])
        mask = sb("mask", [P, P])
        mask_s = sb("mask_s", [P, 2, P])
        own_s = sb("own_s", [P, 2, P])
        nf = sb("nf", [P, FH, SEQ])
        nf_s = sb("nf_s", [P, KVH, 2, 2, P])
        fq = sb("fq", [P, PT, FH])
        fq_s = sb("fq_s", [P, KVH, 2])
        own_t = sb("own_t", [P, P])
        q = sb("q", [P, TILES, G * DH])
        k = sb("k", [P, TILES, DH])
        v = sb("v", [P, TILES, DH])
        ck = sb("ck", [P, DEC_BATCH, DH])
        cv = sb("cv", [P, DEC_BATCH, DH])
        gt = sb("gt", [P, G * PT + 2, DH])
        ckT = sb("ckT", [P, DEC_BATCH * P])
        qTs = sb("qTs", [P, DEC_BATCH, G, DEC_SEQ])
        ost = sb("ost", [P, 2, DH])
        mx = sb("mx", [P, 2, 4])
        ps_s = ps("ps_s", [P, 2, 2, 512])
        ps_t = ps("ps_t", [P, 2, 512])
        ps_o = ps("ps_o", [P, 2, 512])
        f_landed, own, rec = sem("f_landed"), sem("own"), sem("rec")
        z_ready, e_done, lf_ready, lf_turned, lf_out = sem("z_ready"), sem("e_done"), sem("lf_ready"), sem("lf_turned"), sem("lf_out")
        c_turned, c_ready, lf_stored = sem("c_turned"), sem("c_ready"), sem("lf_stored")
        cum_ready, nf_done, nf_read, nfs_done, nfs_read, fq_turned, prep = sem("cum_ready"), sem("nf_done"), sem("nf_read"), sem("nfs_done"), sem("nfs_read"), sem("fq_turned"), sem("prep")
        qk_in, v_in, g_in = sem("qk_in"), sem("v_in"), sem("g_in")
        x_turned, x_ready = sem("x_turned"), sem("x_ready")
        s_done, s_read, soft, negm, p_done = sem("s_done"), sem("s_read"), sem("soft"), sem("negm"), sem("p_done")
        t_done, pt_ready, pv_done, fin, diag = sem("t_done"), sem("pt_ready"), sem("pv_done"), sem("fin"), sem("diag")
        stored = [sem(f"stored{i}") for i in range(2)]
        X = -(-(TILES + DEC_BATCH + G * TILES) // 4)
        items = [("k", t) for t in range(TILES)] + [("c", b) for b in range(DEC_BATCH)] + [("q", t * G + h) for h in range(G) for t in range(TILES)]
        SELF = 5
        block = ctx.enter_context(nc.Block())

        @block.sync
        def _(sp):
            sp.dma_start(f_in[:, :], dr["f_raw"]).then_inc(f_landed, 16)
            sp.dma_start(f_bias[:, :], dr["kv_fb"]).then_inc(f_landed, 16)
            with nc.allow_non_contiguous_dma(reason="eight columns"):
                sp.dma_start(c_tok[:, :, :], dr["cache_logf"].rearrange("b p h -> p b h")).then_inc(f_landed, 16)
            for dst, name in ((sel_head, "sel_head"), (sel_group, "sel_group"), (mask, "mask"), (mask_s, "mask_s"), (own_s, "own_s")):
                flat = dst[:] if len(dst.shape) == 2 else dst[:].rearrange("p a b -> p (a b)")
                sp.dma_start(flat, pr.table[name]).then_inc(f_landed, 16)
            with sp.Fori(0, KVH) as n:
                kvc = bass.ds(n * DH, DH)
                hc = bass.ds(n * G * DH, G * DH)
                sp.wait_ge(fin, n * UNITS + 1)
                sp.dma_start(k[:, 0:PT], dr["k_prompt"][:, kvc].rearrange("(t p) c -> p t c", p=P)).then_inc(qk_in, 16)
                sp.dma_start(k[:, PT], dr["k_sample"][:, kvc]).then_inc(qk_in, 16)
                sp.dma_start(ck[:, :, :], dr["cache_k"][:, :, kvc].rearrange("b p c -> p b c")).then_inc(qk_in, 16)
                sp.dma_start(q[:, :, :], dr["q"][:, hc].rearrange("(t p) c -> p t c", p=P)).then_inc(qk_in, 16)
                sp.dma_start(v[:, 0:PT], dr["v_prompt"][:, kvc].rearrange("(t p) c -> p t c", p=P)).then_inc(v_in, 16)
                sp.dma_start(v[:, PT], dr["v_sample"][:, kvc]).then_inc(v_in, 16)
                sp.dma_start(cv[:, :, :], dr["cache_v"][:, :, kvc].rearrange("b p c -> p b c")).then_inc(v_in, 16)
                sp.dma_start(gt[:, 0:G * PT].rearrange("p (t g) c -> p t (g c)", g=G), dr["g2"][0:SEQ, hc].rearrange("(t p) c -> p t c", p=P)).then_inc(g_in, 16)
                for r in range(2):
                    for j in range(4):
                        for h in range(G):
                            p0, b = BR * j + DEC_SEQ * h, 4 * r + j
                            sp.dma_start(gt[p0:p0 + DEC_SEQ, G * PT + r], dr["g2"][SEQ + b * DEC_SEQ:SEQ + (b + 1) * DEC_SEQ, bass.ds(n * G * DH + h * DH, DH)]).then_inc(g_in, 16)

        @block.tensor
        def _(pe):
            pe.wait_ge(lf_ready, 1)
            for t in range(TILES):
                ins = pe.transpose(ps_t[:, 0, t * FH:(t + 1) * FH], logf[:, t * P:(t + 1) * P], pr.ident[0:FH, 0:FH])
            ins.then_inc(lf_turned, 1)
            pe.wait_ge(f_landed, 8 * 16)
            for b in range(DEC_BATCH):
                ins = pe.transpose(ps_s[0:FH, 0, b // 4, (b % 4) * P:(b % 4 + 1) * P], c_tok[:, b, :], pr.ident[:, :])
            ins.then_inc(c_turned, 1)
            pe.wait_ge(cum_ready, 1)
            for t in range(PT):
                ins = pe.transpose(ps_t[:, 1, t * FH:(t + 1) * FH], cum[:, t * P:(t + 1) * P], pr.ident[0:FH, 0:FH])
            ins.then_inc(fq_turned, 1)
            for h in range(FH):
                pe.wait_ge(nf_read, h + 1)
                for a in range(2):
                    ins = pe.matmul(ps_s[:, h % 2, a, :], sel_head[:, h, :], cum[:, a * 512:(a + 1) * 512], start=True, stop=True)
                ins.then_inc(nf_done, 1)
            for n in range(KVH):
                for r in range(2):
                    m = 2 * n + r
                    pe.wait_ge(nfs_read, m + 1)
                    pe.matmul(ps_o[:, m % 2, P:2 * P], sel_group[:, n, :], cum_n[:, :], start=True, stop=True, skip_group_check=True)
                    for j in range(4):
                        b = 4 * r + j
                        ins = pe.matmul(ps_o[BR * j:BR * (j + 1), m % 2, 0:P], sel_group[:, n, BR * j:BR * (j + 1)], cum_c[:, b * PAST:(b + 1) * PAST],
                                        start=True, stop=True, tile_position=(0, BR * j), skip_group_check=True)
                    ins.then_inc(nfs_done, 1)
            pe.wait_ge(prep, 3)

            with pe.Fori(0, KVH) as n:
                pe.wait_ge(qk_in, n * 64 + 64)
                for x in range(X):
                    pe.wait_ge(x_ready, n * X + x + 1)
                    for y, (what, z) in enumerate(items[4 * x:4 * x + 4]):
                        src = {"k": lambda: k[:, z, :], "c": lambda: ck[:, z, :], "q": lambda: q[:, z // G, (z % G) * DH:(z % G + 1) * DH]}[what]()
                        ins = pe.transpose(ps_t[:, x % 2, y * P:(y + 1) * P], src, pr.ident[:, :])
                    ins.then_inc(x_turned, 1)
                pe.wait_ge(x_ready, n * X + X + 2)

                def scores(u):
                    pe.wait_ge(s_read, n * UNITS + u + 1)
                    t, h = u // G, u % G
                    if u < G * PT:
                        L = (t + 1) * P
                        for a in range(-(-L // 512)):
                            w = min(512, L - 512 * a)
                            ins = pe.matmul(ps_s[:, u % 2, a, 0:w], qT[:, h, t * P:(t + 1) * P], kT[:, a * 512:a * 512 + w], start=True, stop=True)
                    else:
                        r = u - G * PT
                        rows = qTs[:, :, :, :].rearrange("p b g q -> p (b g q)")
                        pe.matmul(ps_s[:, u % 2, 0, P:2 * P], rows[:, r * P:(r + 1) * P], kT[:, SEQ:SEQ + P], start=True, stop=True, skip_group_check=True)
                        for j in range(4):
                            b = 4 * r + j
                            ins = pe.matmul(ps_s[BR * j:BR * (j + 1), u % 2, 0, 0:P], rows[:, b * BR:(b + 1) * BR], ckT[:, b * P:(b + 1) * P],
                                            start=True, stop=True, tile_position=(0, BR * j), skip_group_check=True)
                    ins.then_inc(s_done, 1)

                def turn(u, x):
                    m = first[u] + x
                    pe.wait_ge(pt_ready, n * GROUPS + m + 1)
                    for y in range(min(4, blocks[u] - 4 * x)):
                        b = 4 * x + y
                        ins = pe.transpose(ps_t[:, m % 2, y * P:(y + 1) * P], s_sb[:, u % 2, b * P:(b + 1) * P], pr.ident[:, :])
                    ins.then_inc(t_done, 1)

                def values(u, x):
                    m = first[u] + x
                    pe.wait_ge(pt_ready, n * GROUPS + m + 3)
                    o = ps_o[:, u % 2, 0:DH]
                    if u < G * PT:
                        for y in range(min(4, blocks[u] - 4 * x)):
                            b = 4 * x + y
                            ins = pe.matmul(o, pT[:, m % 2, y * P:(y + 1) * P], v[:, b, :], start=b == 0, stop=b == blocks[u] - 1)
                    else:
                        r = u - G * PT
                        pe.matmul(o, pT[:, m % 2, P:2 * P], v[:, PT, :], start=True, stop=False, skip_group_check=True)
                        for j in range(4):
                            ins = pe.matmul(ps_o[BR * j:BR * (j + 1), u % 2, 0:DH], pT[:, m % 2, BR * j:BR * (j + 1)], cv[:, 4 * r + j, :],
                                            start=False, stop=True, tile_position=(0, BR * j), skip_group_check=True)
                    ins.then_inc(pv_done, 1)

                scores(0)
                pe.wait_ge(v_in, n * 48 + 48)
                for u in range(UNITS):
                    if u + 1 < UNITS:
                        scores(u + 1)
                    pe.wait_ge(p_done, n * UNITS + u + 1)
                    for x in range(groups[u]):
                        turn(u, x)
                    pe.wait_ge(fin, n * UNITS + u) if u >= 2 else pe.wait_ge(fin, n * UNITS + 1)
                    for x in range(groups[u]):
                        values(u, x)

        @block.scalar
        def _(act):
            act.sem_inc(nf_read, 2)
            act.sem_inc(x_ready, 2)
            act.sem_inc(pt_ready, 2)
            act.wait_ge(z_ready, 1)
            act.activation(f_tmp[:, 1, :], f_tmp[:, 0, :], ACT.Exp, scale=-1.0).then_inc(e_done, 1)
            act.wait_ge(e_done, 1)
            act.activation(f_tmp[:, 1, :], f_tmp[:, 1, :], ACT.Ln, bias=1.0).then_inc(e_done, 1)
            for h in range(FH):
                act.wait_ge(nf_done, h + 1)
                act.mul(nf[:, h, :].rearrange("p (a c) -> p a c", a=2), ps_s[:, h % 2], -1.0).then_inc(nf_read, 1)
            act.wait_ge(nf_read, 2 + FH)
            act.sem_inc(prep, 1)
            with act.Fori(0, KVH) as n:
                for x in range(X):
                    act.wait_ge(x_turned, n * X + x + 1)
                    for y, (what, z) in enumerate(items[4 * x:4 * x + 4]):
                        src = ps_t[:, x % 2, y * P:(y + 1) * P]
                        if what == "k":
                            ins = act.copy(kT[:, z * P:(z + 1) * P], src)
                        elif what == "c":
                            ins = act.copy(ckT[:, z * P:(z + 1) * P], src)
                        elif z // G < PT:
                            ins = act.copy(qT[:, z % G, (z // G) * P:(z // G + 1) * P], src)
                        else:
                            ins = act.copy(qTs[:, :, z % G, :], src.rearrange("p (b q) -> p b q", q=DEC_SEQ))
                    ins.then_inc(x_ready, 1)

                def exp(u):
                    act.wait_ge(negm, n * UNITS + u + 1)
                    w = s_sb[:, u % 2, 0:blocks[u] * P]
                    act.activation(w, w, ACT.Exp, bias=mx[:, u % 2, 1:2], accum_out=mx[:, u % 2, 2:3]).then_inc(p_done, 1)

                exp(0)
                for u in range(UNITS):
                    for x in range(groups[u]):
                        m = first[u] + x
                        act.wait_ge(t_done, n * GROUPS + m + 1)
                        if m >= 2:
                            act.wait_ge(pv_done, n * GROUPS + m - 1)
                        w = min(4, blocks[u] - 4 * x) * P
                        act.copy(pT[:, m % 2, 0:w], ps_t[:, m % 2, 0:w]).then_inc(pt_ready, 1)
                    if u + 1 < UNITS:
                        exp(u + 1)

        @block.gpsimd
        def _(pool):
            credit(pool, pr, stored)
            pool.wait_ge(lf_out, 1)
            with nc.allow_non_contiguous_dma(reason="rows of eight"):
                pool.dma_start(dr["logf_prompt"].rearrange("(t p) h -> p t h", p=P), logf_tok[:, 0:PT, :]).then_inc(lf_stored, 16)
                pool.dma_start(dr["logf_sample"], logf_tok[:, PT, :]).then_inc(lf_stored, 16)
            with pool.Fori(0, KVH) as n:
                for u in range(UNITS):
                    pool.wait_ge(fin, n * UNITS + u + 2)
                    if u < G * PT:
                        t, h = u // G, u % G
                        pool.dma_start(dr["o2"][t * P:(t + 1) * P, bass.ds(n * G * DH + h * DH, DH)], ost[:, u % 2, :]).then_inc(stored[u % 2], 16)
                    else:
                        r = u - G * PT
                        for j in range(4):
                            for h in range(G):
                                p0, b = BR * j + DEC_SEQ * h, 4 * r + j
                                pool.dma_start(dr["o2"][SEQ + b * DEC_SEQ:SEQ + (b + 1) * DEC_SEQ, bass.ds(n * G * DH + h * DH, DH)], ost[p0:p0 + DEC_SEQ, u % 2, :]).then_inc(stored[u % 2], 16)
            pool.wait_ge(lf_stored, 32)
            for s in range(2):
                pool.wait_ge(stored[s], 16 + KVH * (PT * 16 + 128))

        @block.vector
        def _(dve):
            chain = Chain(dve, own)
            dve.sem_inc(fin, 1)
            dve.sem_inc(s_read, 2)
            dve.sem_inc(nfs_read, 2)
            dve.wait_ge(f_landed, 8 * 16)
            z, a, lo = f_in[:, :], f_tmp[:, 0, :], f_tmp[:, 2, :]
            chain.link(dve.tensor_scalar(z, z, f_bias[:, 0:1], None, ALU.add))
            chain.link(dve.tensor_scalar(a, z, -1.0, None, ALU.mult))
            dve.tensor_tensor(a, a, z, ALU.max).then_inc(z_ready, 1)
            dve.tensor_scalar(lo, z, 0.0, None, ALU.min).then_inc(own, 1)
            chain.n += 1
            dve.wait_ge(own, chain.n)
            dve.memset(ones[:, :], 1.0).then_inc(own, 1)
            chain.n += 1
            dve.wait_ge(own, chain.n)
            dve.wait_ge(e_done, 2)
            chain.link(dve.tensor_tensor(logf[:, :], lo, f_tmp[:, 1, :], ALU.subtract))
            dve.sem_inc(lf_ready, 1)
            dve.wait_ge(lf_turned, 1)
            dve.tensor_copy(logf_tok[:, :, :], ps_t[:, 0, 0:TILES * FH].rearrange("p (t h) -> p t h", t=TILES)).then_inc(lf_out, 1)
            dve.wait_ge(c_turned, 1)
            chain.link(dve.tensor_copy(c_logf[:, :].rearrange("p (a c) -> p a c", a=2), ps_s[0:FH, 0]))
            chain.link(dve.tensor_tensor_scan(cum[:, :], ones[:, :], logf[:, 0:SEQ], 0.0, ALU.mult, ALU.add))
            for b in range(DEC_BATCH):
                c = slice(b * PAST, (b + 1) * PAST)
                chain.link(dve.tensor_tensor_scan(cum_c[:, c], ones[:, 0:PAST], c_logf[:, c], 0.0, ALU.mult, ALU.add))
                w = slice(b * DEC_SEQ, (b + 1) * DEC_SEQ)
                chain.link(dve.tensor_tensor_scan(cum_n[:, w], ones[:, 0:DEC_SEQ], logf[:, SEQ + b * DEC_SEQ:SEQ + (b + 1) * DEC_SEQ],
                                                  cum_c[:, (b + 1) * PAST - 1:(b + 1) * PAST], ALU.mult, ALU.add))
            dve.sem_inc(cum_ready, 1)
            dve.wait_ge(fq_turned, 1)
            chain.link(dve.tensor_copy(fq[:, :, :], ps_t[:, 1, 0:PT * FH].rearrange("p (t h) -> p t h", t=PT)))
            dve.sem_inc(prep, 1)
            for n in range(KVH):
                for r in range(2):
                    m = 2 * n + r
                    dve.wait_ge(nfs_done, m + 1)
                    f_new = ps_o[:, m % 2, P:2 * P]
                    chain.link(dve.tensor_tensor(own_t[:, :], f_new, own_s[:, r, :], ALU.mult))
                    chain.link(dve.tensor_reduce(fq_s[:, n, r:r + 1], own_t[:, :], AX.X, ALU.add))
                    chain.link(dve.tensor_scalar(nf_s[:, n, r, 0, :], ps_o[:, m % 2, 0:P], -1.0, None, ALU.mult))
                    chain.link(dve.scalar_tensor_tensor(nf_s[:, n, r, 1, :], f_new, -1.0, mask_s[:, r, :], ALU.mult, ALU.add))
                    dve.sem_inc(nfs_read, 1)
            dve.sem_inc(prep, 1)
            start = chain.n
            dve.wait_ge(prep, 3)
            with dve.Fori(0, KVH) as n:
                def softmax(u):
                    dve.wait_ge(s_done, n * UNITS + u + 1)
                    if u >= 2:
                        dve.wait_ge(t_done, n * GROUPS + first[u - 1])
                    own0 = start + n * UNITS * 3 + u * 3
                    s, L = u % 2, blocks[u] * P
                    if u < G * PT:
                        t, h = u // G, u % G
                        head = bass.ds(n * G + h, 1)
                        sv, pv = s_sb[:, s, 0:L], ps_s[:, s].rearrange("p a c -> p (a c)")[:, 0:L]
                        dve.scalar_tensor_tensor(sv, pv, fq[:, t, head], nf[:, head, 0:L].rearrange("p o c -> p (o c)"), ALU.add, ALU.add).then_inc(own, 1)
                        dve.wait_ge(own, own0 + 1)
                        dve.tensor_tensor(s_sb[:, s, L - P:L], s_sb[:, s, L - P:L], mask[:, :], ALU.add).then_inc(own, 1)
                    else:
                        r = u - G * PT
                        dve.scalar_tensor_tensor(s_sb[:, s, 0:L], ps_s[:, s, 0, 0:L], fq_s[:, bass.ds(n, 1), r:r + 1].rearrange("p o c -> p (o c)"),
                                                 nf_s[:, bass.ds(n, 1), r].rearrange("p o a c -> p (o a c)"), ALU.add, ALU.add).then_inc(own, 2)
                    dve.wait_ge(own, own0 + 2)
                    dve.sem_inc(s_read, 1)
                    dve.tensor_reduce(mx[:, s, 0:1], s_sb[:, s, 0:L], AX.X, ALU.max).then_inc(own, 1)
                    dve.wait_ge(own, own0 + 3)
                    dve.tensor_scalar(mx[:, s, 1:2], mx[:, s, 0:1], -1.0, None, ALU.mult).then_inc(negm, 1)

                def finish(u):
                    s = u % 2
                    dve.wait_ge(pv_done, n * GROUPS + first[u + 1])
                    if u == 0:
                        dve.wait_ge(g_in, n * 17 * 16 + 17 * 16)
                    dve.wait_ge(stored[s], n * (PT * 16 + 128) + 16 + 16 * (u // 2))
                    dve.reciprocal(mx[:, s, 3:4], mx[:, s, 2:3]).then_inc(rec, 1)
                    dve.wait_ge(rec, n * UNITS + u + 1)
                    dve.scalar_tensor_tensor(ost[:, s, :], ps_o[:, s, 0:DH], mx[:, s, 3:4], gt[:, u, :], ALU.mult, ALU.mult).then_inc(fin, 1)

                softmax(0)
                for u in range(UNITS):
                    if u + 1 < UNITS:
                        softmax(u + 1)
                    finish(u)


def build(nc, dram, table):
    with ExitStack() as ctx:
        pr = Program(nc, ctx, dram, table)
        dr = dram

        def tile_rows(name, t):
            return dr[name][t * P:(t + 1) * P, :]

        def x_rows(t):
            return dr["x_prompt"][t * P:(t + 1) * P, :] if t < PT else dr["x_sample"]

        def to_rows(name, c0=0):
            return lambda c, t: dr[name][t * P:(t + 1) * P, bass.ds(c * CW + c0, CW)]

        def split_rows(prompt, sample):
            return lambda c, t: dr[prompt][t * P:(t + 1) * P, :] if t < PT else dr[sample]

        def turned_rows(c, m):
            part, n, half = m // 6, m % 6 // 2, m % 2
            return dr["qkT"][bass.ds(c * 4 + part * 2 + half, 1), :, n * NB3:(n + 1) * NB3].rearrange("o p t -> p (o t)")

        qk = [head_columns(dr["a_w_in"], h) for h in range(RH)]
        wv = [columns(dr["a_w_in"], 0, 2 * D + CW * c) for c in range(4)]
        wg = [columns(dr["a_w_in"], 0, 2 * D + VW + CW * c) for c in range(4)]
        wo = [[columns(dr["a_w_out"], half * D, CW * c) for c in range(2)] for half in range(2)]
        wk, wvv = columns(dr["kv_w"], 0, 0), columns(dr["kv_w"], 0, CW)
        wq = [columns(dr["b_w_in"], 0, CW * c) for c in range(2)]
        wg2 = [columns(dr["b_w_in"], 0, D + CW * c) for c in range(2)]
        wo2 = [columns(dr["b_w_out"], 0, CW * c) for c in range(2)]

        condition(pr)
        project(pr, "in", x_rows, True, 0,
                [dict(kind="rotary", pairs=2, weights=qk, store=turned_rows),
                 dict(kind="copy", pairs=2, weights=wv, store=to_rows("v")),
                 dict(kind="silu", pairs=2, weights=wg, store=to_rows("g"))], 0, wo[0][0])
        retention(pr)
        for half in range(2):
            before = (lambda c, t: x_rows(t)[:, c * CW:(c + 1) * CW]) if half == 0 else (lambda c, t: tile_rows("x1a", t)[:, c * CW:(c + 1) * CW])
            project(pr, f"out{half}", lambda t, half=half: tile_rows("o", t)[:, half * D:(half + 1) * D], False, None,
                    [dict(kind="residual", pairs=1, weights=wo[half], col=lambda i, s: s * CW,
                          store=lambda c, t, half=half: tile_rows(("x1a", "x1")[half], t)[:, c * CW:(c + 1) * CW])],
                    12 + 2 * half, wo[1][0] if half == 0 else wk, gate_layer=0, residual=before, gain=dr["a_gn_g"][:, half * D:(half + 1) * D])
        project(pr, "kv", lambda t: tile_rows("x1", t), True, 1,
                [dict(kind="norm", pairs=1, weights=[wk, wvv], gain=dr["k_norm_g"], scale=1.0, plain=1,
                      store=lambda c, t: split_rows(*(("k_prompt", "k_sample"), ("v_prompt", "v_sample"))[c])(c, t))],
                16, wq[0], forget=True)
        project(pr, "q", lambda t: tile_rows("x1", t), True, 2,
                [dict(kind="norm", pairs=1, weights=wq, gain=dr["b_q_norm_g"], scale=DH ** -0.5, store=to_rows("q")),
                 dict(kind="silu", pairs=1, weights=wg2, store=to_rows("g2"))], 18, wo2[0])
        attention(pr)
        project(pr, "end", lambda t: tile_rows("o2", t), False, None,
                [dict(kind="residual", pairs=1, weights=wo2, col=lambda i, s: s * CW,
                      store=lambda c, t: (dr["y_prompt"][t * P:(t + 1) * P, c * CW:(c + 1) * CW] if t < PT else dr["y_sample"][:, c * CW:(c + 1) * CW]))],
                22, None, gate_layer=1, residual=lambda c, t: tile_rows("x1", t)[:, c * CW:(c + 1) * CW])


_SHAPES = {
    "x_prompt": (SEQ, D), "x_sample": (P, D), "state_ret": (DEC_BATCH, RH, DK, DV),
    "cache_k": (DEC_BATCH, PAST, KVH * DH), "cache_v": (DEC_BATCH, PAST, KVH * DH), "cache_logf": (DEC_BATCH, PAST, FH),
    "c_prompt": (1, D), "c_sample": (DEC_BATCH, D),
    "a_norm_g": (1, D), "a_ada_w": (D, 3 * D), "a_ada_b": (1, 3 * D), "a_w_in": (D, 6 * D), "a_gn_g": (1, VW), "a_w_out": (VW, D),
    "kv_norm_g": (1, D), "kv_ada_w": (D, 2 * D), "kv_ada_b": (1, 2 * D), "kv_w": (D, 2 * KVH * DH + FH), "kv_fb": (FH, 1), "k_norm_g": (1, DH),
    "b_norm_g": (1, D), "b_ada_w": (D, 3 * D), "b_ada_b": (1, 3 * D), "b_w_in": (D, 2 * D), "b_q_norm_g": (1, DH), "b_w_out": (D, D),
}
_OUTS = {
    "y_prompt": (SEQ, D), "y_sample": (P, D), "state_prompt": (RH, DK, DV), "k_prompt": (SEQ, KVH * DH), "v_prompt": (SEQ, KVH * DH),
    "logf_prompt": (SEQ, FH), "state_sample": (DEC_BATCH, RH, DK, DV), "k_sample": (P, KVH * DH), "v_sample": (P, KVH * DH), "logf_sample": (P, FH),
}
_FINAL = {
    "y_prompt": (1, SEQ, D), "y_sample": (DEC_BATCH, DEC_SEQ, D), "state_prompt": (1, 1, RH, DK, DV), "k_prompt": (1, SEQ, KVH, DH),
    "v_prompt": (1, SEQ, KVH, DH), "logf_prompt": (1, SEQ, FH), "state_sample": (1, DEC_BATCH, RH, DK, DV),
    "k_sample": (DEC_BATCH, DEC_SEQ, KVH, DH), "v_sample": (DEC_BATCH, DEC_SEQ, KVH, DH), "logf_sample": (DEC_BATCH, DEC_SEQ, FH),
}
_SCRATCH = {
    "credit": (4, P),
    "gate": (P, 2, 2, D), "qkT": (4 * RH, P, TOKENS), "v": (TOKENS, VW), "g": (TOKENS, VW), "o": (TOKENS, VW),
    "x1a": (TOKENS, D), "x1": (TOKENS, D), "f_raw": (FH, TOKENS), "q": (TOKENS, D), "g2": (TOKENS, D), "o2": (TOKENS, D),
}


def kernel(**inputs):
    import concourse.bacc as bacc
    from concourse.bass_utils import run_bass_kernel_spmd

    nc = bacc.Bacc("TRN2", target_bir_lowering=False, num_devices=1)
    arrays, dram, table = {}, {}, {}
    for name, shape in _SHAPES.items():
        arrays[f"in_{name}"] = np.ascontiguousarray(inputs[name]).reshape(shape)
        dram[name] = nc.dram_tensor(f"in_{name}", shape, F32, kind="ExternalInput").ap()
    for name, a in tables().items():
        arrays[f"table_{name}"] = a
        table[name] = nc.dram_tensor(f"table_{name}", a.shape, F32, kind="ExternalInput").ap()
    for name, shape in _OUTS.items():
        dram[name] = nc.dram_tensor(f"out_{name}", shape, F32, kind="ExternalOutput").ap()
    for name, shape in _SCRATCH.items():
        dram[name] = nc.dram_tensor(f"scratch_{name}", shape, F32, kind="Internal").ap()
    build(nc, dram, table)
    r = run_bass_kernel_spmd(nc, [arrays], core_ids=[0])
    return tuple(r.results[0][f"out_{name}"].reshape(_FINAL[name]) for name in _OUTS)
```

```python
from contextlib import ExitStack, contextmanager

import numpy as np
import concourse.bass as bass
from concourse import mybir

F32 = mybir.dt.float32
F32R = mybir.dt.float32r
ALU = mybir.AluOpType
ACT = mybir.ActivationFunctionType
AX = mybir.AxisListType

P = 128
D = 1024
SEQ = 1024
DEC_BATCH, DEC_SEQ, PAST = 8, 16, 128
TOKENS = SEQ + DEC_BATCH * DEC_SEQ
TILES = TOKENS // P
PT = SEQ // P
RH, DK, DV = 4, 256, 512
VW = RH * DV
FH, KVH, DH = 8, 4, 128
KT = D // P
CW = 512
SUBS = 4
KS = KT // SUBS
NB3 = 384
EPS = 1e-6
NEG = -1.0e30
ROPE_BASE = 10000.0
BR = 32


def tables():
    f = np.float32
    pos = np.concatenate([np.arange(SEQ), PAST + np.tile(np.arange(DEC_SEQ), DEC_BATCH)]).astype(f)
    half = DK // 2
    inv = np.power(f(ROPE_BASE), -np.arange(half, dtype=f) / f(half)).astype(f)
    ang = (inv[:, None] * pos[None, :]).astype(f)
    lg = np.log1p(-np.exp2(-5.0 - np.arange(RH, dtype=np.float64)))
    i = np.arange(P)
    ks = DK ** -0.5
    diff = i[None, :] - i[:, None]
    same = (i[None, :] // DEC_SEQ) == (i[:, None] // DEC_SEQ)
    intra = np.stack([np.where(diff >= 0, np.exp(np.maximum(diff, 0) * g), 0) * ks for g in lg], 1)
    intra_s = np.stack([np.where((diff >= 0) & same, np.exp(np.maximum(diff, 0) * g), 0) * ks for g in lg], 1)
    ones = np.ones((P, 1, 1))
    qdec = ones * np.stack([np.exp((i + 1.0) * g) for g in lg], 0)[None]
    loc = i % DEC_SEQ
    par = (i // DEC_SEQ) % 2
    qdec_s = ones[..., None] * np.stack([[np.exp((loc + 1.0) * g) * (par == p) for p in range(2)] for g in lg], 0)[None]
    kdec = np.stack([np.exp((P - 1.0 - i) * g) * ks for g in lg], 1)
    kdec_s = np.stack([np.exp((DEC_SEQ - 1.0 - loc) * g)[:, None] * ks * (i[:, None] // DEC_SEQ == np.arange(DEC_BATCH)) for g in lg], 1)
    cdec = np.ones((P, 1)) * np.exp(P * lg)[None]
    cdec_s = np.ones((P, 1)) * np.exp(DEC_SEQ * lg)[None]
    sel_gate = np.zeros((P, 2, 4, P))
    for j in range(4):
        sel_gate[BR * j + DEC_BATCH, 0, j, :] = 1
        for b in range(DEC_BATCH):
            sel_gate[BR * j + b, 1, j, b * DEC_SEQ:(b + 1) * DEC_SEQ] = 1
    mask = np.where(i[None, :] <= i[:, None], 0, NEG)
    sel_head = np.zeros((FH, FH, P))
    for h in range(FH):
        sel_head[h, h] = 1
    row_j, row_g, row_q = i // 32, (i // DEC_SEQ) % 2, i % DEC_SEQ
    sel_group = np.zeros((FH, KVH, P))
    for kv in range(KVH):
        sel_group[2 * kv + row_g, kv, i] = 1
    mask_s, own_s = np.zeros((P, 2, P)), np.zeros((P, 2, P))
    for r in range(2):
        b = 4 * r + row_j
        ok = (i[None, :] // DEC_SEQ == b[:, None]) & (loc[None, :] <= row_q[:, None])
        mask_s[:, r] = np.where(ok, 0, NEG)
        own_s[:, r] = i[None, :] == (b * DEC_SEQ + row_q)[:, None]
    t = dict(ident=np.eye(P), cos=np.cos(ang), sin=np.sin(ang), intra=intra, intra_s=intra_s,
             qdec=qdec, qdec_s=qdec_s, kdec=kdec, kdec_s=kdec_s, cdec=cdec, cdec_s=cdec_s,
             sel_gate=sel_gate, mask=mask, sel_head=sel_head, sel_group=sel_group,
             mask_s=mask_s, own_s=own_s)
    return {k: np.ascontiguousarray(v.reshape(v.shape[0], -1), dtype=f) for k, v in t.items()}


class Program:

    def __init__(self, nc, ctx, dram, table):
        self.nc, self.ctx, self.dram, self.table = nc, ctx, dram, table
        self.raw = self.sb("w_raw", [P, 2, KS, CW])
        self.w_hi = self.sb("w_hi", [P, 2, KT, CW], F32R)
        self.w_lo = self.sb("w_lo", [P, 2, KT, CW], F32R)
        self.raw_landed = [self.sem(f"raw_landed{s}") for s in range(2)]
        self.raw_split = self.sem("raw_split")
        self.hi_done = self.sem("w_hi_done")
        self.ident = self.sb("ident", [P, P])
        self.passed = self.sem("passed")
        self.rstd = self.sb("rstd", [P, TILES])
        self.gn_g = self.sb("gn_g", [P, VW // D, KT])
        self.mod_a = [self.sb(f"mod_a{m}", [P, KT, DEC_BATCH + 1]) for m in range(3)]
        self.mod_b = [self.sb(f"mod_b{m}", [P, KT, DEC_BATCH + 1]) for m in range(3)]

    def sb(self, name, shape, dt=F32):
        return self.ctx.enter_context(self.nc.sbuf_tensor(name, shape, dt))

    def sem(self, name):
        return self.ctx.enter_context(self.nc.semaphore(name))


def stand(eng, pr):
    eng.sem_inc(pr.passed, 1)


def credit(pool, pr, sems):
    for n, sem in enumerate(sems):
        pool.dma_start(pr.dram["credit"][n:n + 1, :], pr.ident[0:1, :]).then_inc(sem, 16)


@contextmanager
def semaphores(nc, prefix):
    taken = []

    def sem(name):
        taken.append(nc.alloc_semaphore(prefix + name))
        return taken[-1]
    yield sem
    nc.clear_and_free_semaphores(taken)
    nc.all_engine_barrier()


class Chain:

    def __init__(self, eng, sem, start=0):
        self.eng, self.sem, self.n, self.base = eng, sem, start, 0

    def link(self, ins):
        self.n += 1
        ins.then_inc(self.sem, 1)
        self.eng.wait_ge(self.sem, self.base + self.n)



def load_chunk(pr, sp, weight, chunk):
    with sp.Fori(0, SUBS // 2) as j:
        for slot in range(2):
            sp.wait_ge(pr.raw_split, chunk * SUBS + 2 * j + slot + 1)
            for dst, src in weight(pr.raw[:, slot], (2 * j + slot) * KS * P):
                sp.dma_start(dst, src).then_inc(pr.raw_landed[slot], 16)


def columns(w, row0, c0):
    def pieces(raw, r):
        return [(raw[:, k], w[bass.ds(r + row0 + k * P, P), c0:c0 + CW]) for k in range(KS)]
    return pieces


def head_columns(w, h):
    def pieces(raw, r):
        rows = w[bass.ds(r, KS * P), :].rearrange("(k p) c -> p k c", p=P)
        return [(raw[:, :, 0:DK], rows[:, :, h * DK:(h + 1) * DK]), (raw[:, :, DK:2 * DK], rows[:, :, D + h * DK:D + (h + 1) * DK])]
    return pieces


def split_hi(pr, act, chunk, slot, sub):
    act.wait_ge(pr.raw_landed[sub % 2], chunk * (SUBS // 2) * 32 + (sub // 2 + 1) * 32)
    act.copy(pr.w_hi[:, slot, sub * KS:(sub + 1) * KS, :], pr.raw[:, sub % 2]).then_inc(pr.hi_done, 1)


def split_lo(pr, dve, chunk, slot, sub):
    dve.wait_ge(pr.hi_done, chunk * SUBS + sub + 1)
    dve.tensor_tensor(pr.w_lo[:, slot, sub * KS:(sub + 1) * KS, :], pr.raw[:, sub % 2],
                      pr.w_hi[:, slot, sub * KS:(sub + 1) * KS, :].bitcast(F32), ALU.subtract).then_inc(pr.raw_split, 1)


def condition(pr):
    nc = pr.nc
    dr = pr.dram
    ROUNDS = [("a", 0, 2048), ("gates", 0, 0), ("kv", 0, 2048), ("b", 0, 2048)]
    w_of = {"a": dr["a_ada_w"], "kv": dr["kv_ada_w"], "b": dr["b_ada_w"]}
    b_of = {"a": dr["a_ada_b"], "kv": dr["kv_ada_b"], "b": dr["b_ada_b"]}

    def cols(r, j):
        if ROUNDS[r][0] == "gates":
            return ("a", 2048 + 512 * j) if j < 2 else ("b", 2048 + 512 * (j - 2))
        return ROUNDS[r][0], 512 * j

    with ExitStack() as ctx:
        sb = lambda n, s, dt=F32: ctx.enter_context(nc.sbuf_tensor(n, s, dt))
        ps = lambda n, s: ctx.enter_context(nc.psum_tensor(n, s, F32))
        sem = ctx.enter_context(semaphores(nc, "ada_"))
        c_rows = sb("c_rows", [BR, D])
        c_silu = sb("c_silu", [BR, D])
        cT = sb("cT", [P, KT, BR])
        w = sb("ada_w_sb", [P, 4, 4, CW])
        bias = sb("ada_bias", [P, 4, CW])
        rows = sb("ada_rows", [P, 4, CW])
        norm_g = sb("norm_g", [P, 3, KT])
        sel = sb("sel_gate_sb", [P, 2, 4, P])
        gate = sb("gate_sb", [P, 2, 2, D])
        ps_c = ps("ps_c", [P, 512])
        ps_ada = ps("ps_ada", [P, 2, 512])
        ps_t = ps("ps_t", [P, 512])
        ps_g = ps("ps_g", [P, 4, 512])
        in_landed, c_ready, b_zero, b_landed = sem("in_landed"), sem("c_ready"), sem("b_zero"), sem("b_landed")
        s_silu, c_turned, cT_ready = sem("s_silu"), sem("c_turned"), sem("cT_ready")
        w_landed = [sem(f"ada_landed{i}") for i in range(4)]
        w_read, rows_ready = sem("ada_read"), sem("rows_ready")
        turned, mod_ready, gate_done, gate_ready, gate_out = sem("ada_turned"), sem("mod_ready"), sem("gate_done"), sem("gate_ready"), sem("gate_out")
        block = ctx.enter_context(nc.Block())

        @block.sync
        def _(sp):
            sp.wait_ge(c_ready, 1)
            sp.dma_start(c_rows[0:DEC_BATCH], dr["c_sample"]).then_inc(in_landed, 16)
            sp.dma_start(c_rows[DEC_BATCH:DEC_BATCH + 1], dr["c_prompt"]).then_inc(in_landed, 16)
            sp.dma_start(pr.ident[:, :], pr.table["ident"]).then_inc(in_landed, 16)
            for r in range(4):
                for k in range(KT):
                    n = r * KT + k
                    if n >= 4:
                        sp.wait_ge(w_read, n - 3)
                    if cols(r, 0)[0] == cols(r, 3)[0]:
                        sp.dma_start(w[:, n % 4], w_of[cols(r, 0)[0]][k * P:(k + 1) * P, 0:2048].rearrange("p (j c) -> p j c", j=4)).then_inc(w_landed[n % 4], 16)
                    else:
                        for half, m in enumerate("ab"):
                            sp.dma_start(w[:, n % 4, 2 * half:2 * half + 2], w_of[m][k * P:(k + 1) * P, 2048:3072].rearrange("p (j c) -> p j c", j=2)).then_inc(w_landed[n % 4], 16)

        @block.gpsimd
        def _(pool):
            pool.memset(c_rows[:, :], 0.0).then_inc(c_ready, 1)
            pool.memset(bias[:, :, :], 0.0).then_inc(b_zero, 1)
            pool.wait_ge(b_zero, 1)
            for r in range(4):
                for j in range(4):
                    m, c0 = cols(r, j)
                    pool.dma_start(bias[BR * j:BR * j + 9, r, :], b_of[m][0:1, c0:c0 + CW].to_broadcast([9, CW])).then_inc(b_landed, 16)
            for m, g in enumerate(("a_norm_g", "kv_norm_g", "b_norm_g")):
                with nc.allow_non_contiguous_dma(reason="1024 channel gains, once"):
                    pool.dma_start(norm_g[:, m, :], dr[g].rearrange("a (k p) -> p (a k)", p=P)).then_inc(b_landed, 16)
            with nc.allow_non_contiguous_dma(reason="2048 channel gains, once"):
                pool.dma_start(pr.gn_g[:, :, :], dr["a_gn_g"].rearrange("a (n k p) -> p (a n) k", p=P, k=KT)).then_inc(b_landed, 16)
            pool.dma_start(sel[:, :, :, :], pr.table["sel_gate"]).then_inc(b_landed, 16)
            pool.wait_ge(gate_ready, 4)
            pool.dma_start(dr["gate"], gate[:, :, :, :]).then_inc(gate_out, 16)
            pool.wait_ge(gate_out, 16)

        @block.scalar
        def _(act):
            act.wait_ge(in_landed, 48)
            act.activation(c_silu[:, :], c_rows[:, :], ACT.Silu).then_inc(s_silu, 1)

        @block.tensor
        def _(pe):
            pe.wait_ge(s_silu, 1)
            for k in range(KT):
                ins = pe.transpose(ps_c[:, k * BR:(k + 1) * BR], c_silu[:, k * P:(k + 1) * P], pr.ident[0:BR, 0:BR])
            ins.then_inc(c_turned, 1)
            pe.wait_ge(cT_ready, 1)

            def turn(r):
                pe.wait_ge(rows_ready, r + 1)
                if r:
                    pe.wait_ge(mod_ready, {2: 1, 3: 2}[r])
                for c in range(4):
                    ins = pe.transpose(ps_t[:, c * P:(c + 1) * P], rows[:, r, c * P:(c + 1) * P], pr.ident[:, :])
                ins.then_inc(turned, 1)

            landed = [0] * 4
            for r in range(4):
                if r >= 2:
                    pe.wait_ge(rows_ready, r - 1)
                for k in range(KT):
                    n = r * KT + k
                    landed[n % 4] += 16 if cols(r, 0)[0] == cols(r, 3)[0] else 32
                    pe.wait_ge(w_landed[n % 4], landed[n % 4])
                    for j in range(4):
                        ins = pe.matmul(ps_ada[BR * j:BR * (j + 1), r % 2, :], cT[:, k, :], w[:, n % 4, j, :],
                                        start=k == 0, stop=k == KT - 1, tile_position=(0, BR * j), skip_group_check=True)
                    ins.then_inc(w_read, 1)
                if r in (1, 3):
                    turn(r - 1)
            pe.wait_ge(b_landed, 21 * 16)
            for kind in range(2):
                if kind:
                    pe.wait_ge(gate_ready, 2)
                for j in range(4):
                    ins = pe.matmul(ps_g[:, j, :], sel[:, kind, j, :], rows[:, 1, :], start=True, stop=True)
                ins.then_inc(gate_done, 1)
            turn(3)

        @block.vector
        def _(dve):
            dve.sem_inc(pr.raw_split, 2)
            dve.wait_ge(c_turned, 1)
            dve.tensor_copy(cT[:, :, :], ps_c[:, 0:KT * BR]).then_inc(cT_ready, 1)

            def add_bias(r):
                dve.wait_ge(w_read, (r + 1) * KT)
                if r == 0:
                    dve.wait_ge(b_landed, 21 * 16)
                dve.tensor_tensor(rows[:, r, :], ps_ada[:, r % 2, :], bias[:, r, :], ALU.add).then_inc(rows_ready, 1)

            def modulation(r, m):
                dve.wait_ge(turned, m + 1)
                t = ps_t[:, :].rearrange("p (c j b) -> p j c b", c=4, j=4)
                for jj in range(2):
                    dve.tensor_copy(pr.mod_b[m][:, 4 * jj:4 * jj + 4, :], t[:, jj, :, 0:DEC_BATCH + 1])
                for jj in range(2):
                    for c in range(4):
                        ins = dve.tensor_scalar(pr.mod_a[m][:, 4 * jj + c, :], t[:, 2 + jj, c, 0:DEC_BATCH + 1], 1.0, norm_g[:, m, 4 * jj + c:4 * jj + c + 1], ALU.add, ALU.mult)
                ins.then_inc(mod_ready, 1)

            add_bias(0)
            add_bias(1)
            modulation(0, 0)
            add_bias(2)
            add_bias(3)
            modulation(2, 1)
            for kind in range(2):
                dve.wait_ge(gate_done, kind + 1)
                for m in range(2):
                    dve.tensor_copy(gate[:, m, kind, :], ps_g[:, 2 * m:2 * m + 2, :]).then_inc(gate_ready, 1)
            modulation(3, 2)


def project(pr, name, source, norm, mod, groups, chunk0, after, known=False, forget=False, gate_layer=None, residual=None, gain=None):
    nc, dr = pr.nc, pr.dram
    with ExitStack() as ctx:
        sb = lambda n, s, dt=F32: ctx.enter_context(nc.sbuf_tensor(f"{name}_{n}", s, dt))
        ps = lambda n, s: ctx.enter_context(nc.psum_tensor(f"{name}_{n}", s, F32))
        sem = ctx.enter_context(semaphores(nc, f"{name}_"))
        hT_hi = sb("hT_hi", [P, KT, TOKENS], F32R)
        hT_lo = sb("hT_lo", [P, KT, TOKENS], F32R)
        x = sb("x", [P, TILES * D])
        xv = x[:, :].rearrange("p (t d) -> p t d", t=TILES)
        xs = sb("xs", [P, 2, TILES * P])
        ht = sb("ht", [P, 2, TOKENS])
        stat = sb("stat", [P, 3, TILES])
        small = sb("small", [P, 2, 4, 4])
        off = [0]

        def part_of_x(n):
            off[0] += n
            assert off[0] <= TILES * D
            return x[:, off[0] - n:off[0]]

        stage = part_of_x(4 * CW).rearrange("p (s c) -> p s c", s=4)
        ost = part_of_x(4 * CW).rearrange("p (s c) -> p s c", s=4)
        tmp = part_of_x(2 * CW).rearrange("p (s c) -> p s c", s=2)
        kinds = [g["kind"] for g in groups]
        if gain is not None:
            assert tuple(gain.shape) == (P, KT)
        if "rotary" in kinds:
            cs = part_of_x(2 * TOKENS).rearrange("p (s c) -> p s c", s=2)
        if "norm" in kinds:
            gains = part_of_x(2 * DH).rearrange("p (s c) -> p s c", s=2)
        if "residual" in kinds:
            gate = part_of_x(2 * D).rearrange("p (s c) -> p s c", s=2)
            rin = part_of_x(3 * CW).rearrange("p (s c) -> p s c", s=3)
        if forget:
            wf = sb("wf", [P, KT, FH])
            wf_hi = sb("wf_hi", [P, KT * FH + P - FH], F32R)
            wf_lo = sb("wf_lo", [P, KT * FH + P - FH], F32R)
            f_sb = part_of_x(TOKENS)[0:FH]
            wf_landed = sem("wf_landed")
        ps_t = ps("ps_t", [P, 3, 512])
        ps_o = ps("ps_o", [P, 5, 512])
        AHEAD = 5

        def bank(g, t, first):
            if first and t < AHEAD:
                return t
            return t % 4 if g["kind"] == "rotary" else t % 3


        LOADS = 3 if norm else 4
        x_landed = [sem(f"x_landed{i}") for i in range(LOADS)]
        tab_landed = sem("tab_landed")
        sq_done, me_done, rt_done, rstd_ready = sem("sq_done"), sem("me_done"), sem("rt_done"), sem("rstd_ready")
        xs_ready, turned, ht_ready = sem("xs_ready"), sem("turned"), sem("ht_ready")
        hhi_done, h_ready = sem("hhi_done"), sem("h_ready")
        out_done = sem("out_done")
        evac = sem("evac")
        posted = sem("posted")
        stage_read = sem("stage_read")
        stored = [sem(f"stored{s}") for s in range(4)]
        rin_landed = [sem(f"rin{s}") for s in range(3)]
        dve_own = sem("dve_own")
        root_in, root_out = sem("root_in"), sem("root_out")
        f_split, f_lo, f_out, f_stored = sem("f_split"), sem("f_lo"), sem("f_out"), sem("f_stored")
        n_tab = 2 * ("rotary" in kinds) + sum(k == "norm" for k in kinds) + ("residual" in kinds)

        c0 = chunk0
        tile0 = 0
        used = [0, 0, 0, 0]
        for g in groups:
            g["c0"], g["tile0"], g["used"] = c0, tile0, list(used)
            g["tiles"] = 12 if g["kind"] == "rotary" else TILES
            g["per_slot"] = [3, 3, 3, 3] if g["kind"] == "rotary" else [3, 3, 3, 0]
            c0 += 2 * g["pairs"]
            tile0 += 2 * g["pairs"] * g["tiles"]
            used = [u + 2 * g["pairs"] * n for u, n in zip(used, g["per_slot"])]
        post = 0
        for g in groups:
            g["post0"] = post
            if g["kind"] == "rotary":
                post += g["pairs"] * 12
            elif g["kind"] in ("norm", "residual"):
                post += g["pairs"] * 2 * TILES
        all_stored = [16 + 16 * u for u in used]

        def pairs(eng, g, body):
            i0 = 1 if g is groups[0] else 0
            i1 = g["pairs"] - 1 if g is groups[-1] and after is None else g["pairs"]
            if i0:
                for s in range(2):
                    body(0, s, i1 == 0 and s == 1, s == 0)
            if i1 > i0:
                with eng.Fori(i0, i1) as i:
                    for s in range(2):
                        body(i, s, False, False)
            for i in range(max(i0, i1), g["pairs"]):
                for s in range(2):
                    body(i, s, s == 1, False)

        block = ctx.enter_context(nc.Block())

        @block.sync
        def _(sp):
            if norm:
                for t in range(TILES):
                    sp.dma_start(xv[:, t], source(t)).then_inc(x_landed[t // 3], 16)
            else:
                for c in range(LOADS):
                    w = D // LOADS
                    sp.dma_start(xv[:, :, c * w:(c + 1) * w], source(c * w, w)).then_inc(x_landed[c], 16)
            if forget:
                with nc.allow_non_contiguous_dma(reason="eight columns"):
                    sp.dma_start(wf[:, :, :], dr["kv_w"][:, 2 * CW:2 * CW + FH].rearrange("(k p) c -> p k c", p=P)).then_inc(wf_landed, 16)
            if chunk0 == 0:
                load_chunk(pr, sp, groups[0]["weights"][0], 0)
            sp.wait_ge(h_ready, KT)
            if "rotary" in kinds:
                sp.dma_start(cs[:, 0], pr.table["cos"]).then_inc(tab_landed, 16)
                sp.dma_start(cs[:, 1], pr.table["sin"]).then_inc(tab_landed, 16)
            for n, g in enumerate(g for g in groups if g["kind"] == "norm"):
                sp.dma_start(gains[:, n], g["gain"].to_broadcast([P, DH])).then_inc(tab_landed, 16)
            if "residual" in kinds:
                sp.dma_start(gate[:, :, :], dr["gate"][:, gate_layer]).then_inc(tab_landed, 16)

            chunks = [w for g in groups for w in g["weights"]][1:] + ([after] if after else [])
            for n, w in enumerate(chunks):
                load_chunk(pr, sp, w, chunk0 + n + 1)

        @block.gpsimd
        def _(pool):
            credit(pool, pr, stored)
            if norm:
                if not known:
                    pool.wait_ge(rstd_ready, 1)
                for n in range(3):
                    pool.wait_ge(x_landed[n], 48)
                for d in range(KT):
                    if d >= 2:
                        pool.wait_ge(turned, d - 1)
                    pool.tensor_tensor(xs[:, d % 2].rearrange("p (t c) -> p t c", t=TILES), xv[:, :, d * P:(d + 1) * P],
                                       pr.rstd[:, :].rearrange("p (t o) -> p t o", o=1).to_broadcast([P, TILES, P]), ALU.mult).then_inc(xs_ready, 1)
            pool.wait_ge(h_ready, KT)
            if forget:
                pool.wait_ge(f_out, 1)
                pool.dma_start(dr["f_raw"], f_sb[:, :]).then_inc(f_stored, 16)
                pool.wait_ge(f_stored, 16)
            for g in groups:
                def body(i, s, stop, head, g=g):
                    base = g["tile0"] + (2 * i + s) * g["tiles"]
                    kind = "copy" if g.get("plain") == s else g["kind"]
                    ready = evac if kind in ("copy", "silu") else posted
                    if g["kind"] == "residual":
                        def load(t):
                            n = base + t
                            pool.wait_ge(posted, n + 1)
                            pool.dma_start(rin[:, t % 3], residual(2 * i + s, t)).then_inc(rin_landed[t % 3], 16)
                        for t in range(3):
                            load(t)
                    if g["kind"] == "rotary":
                        for u in range(6):
                            pool.wait_ge(posted, (base // 2 if isinstance(base, int) else (g["tile0"] // 2 + (2 * i + s) * 6)) + u + 1)
                            for half in range(2):
                                m = 2 * u + half
                                pool.dma_start(g["store"](2 * i + s, m), ost[:, m % 4, 0:NB3]).then_inc(stored[m % 4], 16)
                    else:
                        credit = {"copy": 4, "silu": 4, "residual": 3, "norm": 0}[kind]
                        if ready is posted:
                            first = g["post0"]
                            base2 = first + (2 * i + s) * g["tiles"]
                        else:
                            base2 = base
                        for t in range(TILES):
                            pool.wait_ge(ready, credit + base2 + t + 1)
                            pool.dma_start(g["store"](2 * i + s, t), ost[:, t % 3, :]).then_inc(stored[t % 3], 16)
                            if g["kind"] == "residual" and t + 3 < TILES:
                                load(t + 3)
                pairs(pool, g, body)
            for s in range(4):
                pool.wait_ge(stored[s], all_stored[s])

        @block.scalar
        def _(act):
            act.sem_inc(evac, 4)
            if norm and not known:
                for t in range(TILES):
                    if t % 3 == 0:
                        act.wait_ge(x_landed[t // 3], 48)
                    act.activation(ht[:, t % 2, 0:D], xv[:, t], ACT.Square, accum_out=stat[:, 0, t:t + 1]).then_inc(sq_done, 1)
                    if t:
                        act.wait_ge(sq_done, t)
                act.wait_ge(me_done, 1)
                act.activation(stat[:, 2, :], stat[:, 1, :], ACT.Sqrt).then_inc(rt_done, 1)
            if chunk0 == 0:
                for sub in range(SUBS):
                    split_hi(pr, act, 0, 0, sub)
            for d in range(KT):
                if mod is not None or gain is not None:
                    act.wait_ge(ht_ready, d + 1)
                    act.copy(hT_hi[:, d, :], ht[:, d % 2, :]).then_inc(hhi_done, 1)
                else:
                    act.wait_ge(turned, d + 1)
                    act.copy(hT_hi[:, d, :].rearrange("p (b c) -> p b c", b=3), ps_t[:, :, 0:NB3]).then_inc(hhi_done, 1)
            act.wait_ge(h_ready, KT)
            if forget:
                act.wait_ge(f_split, 1)
                act.copy(wf_hi[:, 0:KT * FH], wf[:, :, :].rearrange("p k f -> p (k f)")).then_inc(hhi_done, 1)
            for g in groups:
                def body(i, s, stop, head, g=g):
                    c = g["c0"] + 2 * i + s
                    base = g["tile0"] + (2 * i + s) * g["tiles"]
                    k = "copy" if g.get("plain") == s else g["kind"]
                    seen = [0, 0, 0, 0]
                    for t in range(g["tiles"]):
                        slot = t % 4 if k == "rotary" else t % 3
                        width = NB3 if k == "rotary" else CW
                        act.wait_ge(out_done, base + t + 1)
                        if k in ("copy", "silu"):
                            act.wait_ge(stored[slot], 16 * (g["used"][slot] + 1 + seen[slot]) + (2 * i + s) * 16 * g["per_slot"][slot])
                            seen[slot] += 1
                            act.activation(ost[:, slot, :], ps_o[:, bank(g, t, head), :], ACT.Silu if k == "silu" else ACT.Copy).then_inc(evac, 1)
                        else:
                            if k == "rotary":
                                act.wait_ge(stage_read, (2 * i + s) * 6 + t // 2 + 1)
                            else:
                                act.wait_ge(stage_read, g["post0"] + (2 * i + s) * TILES + t + 1)
                            act.copy(stage[:, slot, 0:width], ps_o[:, bank(g, t, head), 0:width]).then_inc(evac, 1)
                        if k == "norm":
                            n = g["post0"] + (2 * i + s) * TILES + t
                            act.wait_ge(root_in, n + 1)
                            act.activation(small[:, 0, 2, :], small[:, 0, 1, :], ACT.Sqrt).then_inc(root_out, 1)
                        if t % 2 and t < 2 * SUBS and not stop:
                            split_hi(pr, act, c + 1, 1 - s, t // 2)
                pairs(act, g, body)

        @block.tensor
        def _(pe):
            def turn(d):
                if norm:
                    pe.wait_ge(xs_ready, d + 1)
                elif d % 2 == 0:
                    pe.wait_ge(x_landed[d // 2], 16)
                if d:
                    pe.wait_ge(ht_ready if mod is not None or gain is not None else h_ready, d)
                for t in range(TILES):
                    src = xs[:, d % 2, t * P:(t + 1) * P] if norm else xv[:, t, d * P:(d + 1) * P]
                    ins = pe.transpose(ps_t[:, t // 3, (t % 3) * P:(t % 3 + 1) * P], src, pr.ident[:, :])
                ins.then_inc(turned, 1)

            def products(g, s, t, k, first):
                if g["kind"] == "rotary":
                    part, n, half = t // 6, t % 6 // 2, t % 2
                    w0 = part * DK + half * P
                    for m, (w, h) in enumerate(((pr.w_hi, hT_hi), (pr.w_hi, hT_lo), (pr.w_lo, hT_hi))):
                        ins = pe.matmul(ps_o[:, bank(g, t, first), 0:NB3], w[:, s, k, w0:w0 + P], h[:, k, n * NB3:(n + 1) * NB3],
                                        start=k + m == 0, stop=k == KT - 1 and m == 2)
                else:
                    for m, (h, w) in enumerate(((hT_hi, pr.w_hi), (hT_hi, pr.w_lo), (hT_lo, pr.w_hi))):
                        ins = pe.matmul(ps_o[:, bank(g, t, first), :], h[:, k, t * P:(t + 1) * P], w[:, s, k, :],
                                        start=k + m == 0, stop=k == KT - 1 and m == 2)
                if k == KT - 1:
                    ins.then_inc(out_done, 1)

            turn(0)
            turn(1)
            pe.wait_ge(pr.raw_split, SUBS * chunk0 + SUBS + 2)
            for d in range(KT):
                if d + 2 < KT:
                    turn(d + 2)
                pe.wait_ge(h_ready, d + 1)
                for t in range(AHEAD):
                    products(groups[0], 0, t, d, True)
            if forget:
                pe.wait_ge(f_lo, 1)
                for n in range(3):
                    for k in range(KT):
                        for m, (a, b) in enumerate(((wf_hi, hT_hi), (wf_lo, hT_hi), (wf_hi, hT_lo))):
                            ins = pe.matmul(ps_t[:, n, 0:NB3], a[:, k * FH:k * FH + P], b[:, k, n * NB3:(n + 1) * NB3], start=k + m == 0, stop=k == KT - 1 and m == 2)
                ins.then_inc(f_lo, 1)
            for g in groups:
                def body(i, s, stop, head, g=g):
                    c = g["c0"] + 2 * i + s
                    base = g["tile0"] + (2 * i + s) * g["tiles"]
                    pe.wait_ge(pr.raw_split, SUBS * c + SUBS + 2)
                    for t in range(AHEAD if head else 0, g["tiles"]):
                        pe.wait_ge(evac, base + t + (1 if g["kind"] == "rotary" else 2))
                        for k in range(KT):
                            products(g, s, t, k, head)
                pairs(pe, g, body)

        @block.vector
        def _(dve):
            chain = Chain(dve, dve_own)
            if norm and not known:
                dve.wait_ge(sq_done, TILES)
                dve.tensor_scalar(stat[:, 1, :], stat[:, 0, :], 1.0 / D, EPS, ALU.mult, ALU.add).then_inc(me_done, 1)
                dve.wait_ge(rt_done, 1)
                dve.reciprocal(pr.rstd[:, :], stat[:, 2, :]).then_inc(rstd_ready, 1)
            if chunk0 == 0:
                for sub in range(SUBS):
                    split_lo(pr, dve, 0, 0, sub)
            if kinds[0] == "rotary":
                dve.sem_inc(stage_read, 2)
            elif kinds[0] in ("norm", "residual"):
                dve.sem_inc(stage_read, 3)
            if "residual" in kinds:
                dve.sem_inc(posted, 3)

            def modulated(d):
                z = ht[:, d % 2, :]
                dve.wait_ge(turned, d + 1)
                if d >= 2:
                    dve.wait_ge(h_ready, d - 1)
                if mod is None:
                    dve.tensor_scalar(z.rearrange("p (a c) -> p a c", a=3), ps_t[:, :, 0:NB3], gain[:, d:d + 1], None, ALU.mult).then_inc(ht_ready, 1)
                    return
                A, B = pr.mod_a[mod], pr.mod_b[mod]
                smp = z[:, SEQ:TOKENS].rearrange("p (b s) -> p b s", b=DEC_BATCH)
                per = [m[:, d, 0:DEC_BATCH].rearrange("p (b o) -> p b o", o=1).to_broadcast([P, DEC_BATCH, DEC_SEQ]) for m in (A, B)]
                dve.tensor_tensor(smp, ps_t[:, 2, SEQ - 2 * NB3:NB3].rearrange("p (b s) -> p b s", b=DEC_BATCH), per[0], ALU.mult).then_inc(dve_own, 1)
                dve.tensor_scalar(z[:, 0:2 * NB3].rearrange("p (a c) -> p a c", a=2), ps_t[:, 0:2, 0:NB3], A[:, d, DEC_BATCH:], B[:, d, DEC_BATCH:], ALU.mult, ALU.add)
                dve.tensor_scalar(z[:, 2 * NB3:SEQ], ps_t[:, 2, 0:SEQ - 2 * NB3], A[:, d, DEC_BATCH:], B[:, d, DEC_BATCH:], ALU.mult, ALU.add)
                dve.wait_ge(dve_own, d + 1)
                dve.tensor_tensor(smp, smp, per[1], ALU.add).then_inc(ht_ready, 1)

            turned_first = mod is not None or gain is not None
            if turned_first:
                modulated(0)
            for d in range(KT):
                if turned_first and d + 1 < KT:
                    modulated(d + 1)
                dve.wait_ge(hhi_done, d + 1)
                hi, lo = hT_hi[:, d, :].bitcast(F32), hT_lo[:, d, :]
                if turned_first:
                    dve.tensor_tensor(lo, ht[:, d % 2, :], hi, ALU.subtract).then_inc(h_ready, 1)
                else:
                    v3 = lambda a: a.rearrange("p (b c) -> p b c", b=3)
                    dve.tensor_tensor(v3(lo), ps_t[:, :, 0:NB3], v3(hi), ALU.subtract).then_inc(h_ready, 1)
            chain.n = KT if mod is not None else 0
            if forget:
                chain.link(dve.memset(wf_hi[:, :].bitcast(F32), 0.0))
                chain.link(dve.memset(wf_lo[:, :].bitcast(F32), 0.0))
                dve.wait_ge(wf_landed, 16)
                dve.sem_inc(f_split, 1)
                dve.wait_ge(hhi_done, KT + 1)
                dve.tensor_tensor(wf_lo[:, 0:KT * FH], wf[:, :, :].rearrange("p k f -> p (k f)"), wf_hi[:, 0:KT * FH].bitcast(F32), ALU.subtract).then_inc(f_lo, 1)
                dve.wait_ge(f_lo, 2)
                dve.tensor_copy(f_sb[:, :].rearrange("p (a c) -> p a c", a=3), ps_t[0:FH, :, 0:NB3]).then_inc(f_out, 1)
            if n_tab:
                dve.wait_ge(tab_landed, 16 * n_tab)
            norm_no = 0
            for g in groups:
                k = g["kind"]
                per_chunk = {"rotary": 36, "norm": 5 * TILES, "residual": TILES, "copy": 0, "silu": 0}[k]
                start = chain.n

                def body(i, s, stop, head, g=g, k=k, per_chunk=per_chunk, start=start, nn=norm_no):
                    if g.get("plain") == s:
                        k, per_chunk = "copy", 0
                    c = g["c0"] + 2 * i + s
                    base = g["tile0"] + (2 * i + s) * g["tiles"]
                    chain.base = (2 * i + s) * per_chunk
                    chain.n = start
                    seen = [0, 0, 0, 0]

                    def free(slot):
                        dve.wait_ge(stored[slot], 16 * (g["used"][slot] + 1 + seen[slot]) + (2 * i + s) * 16 * g["per_slot"][slot])
                        seen[slot] += 1
                    for t in range(g["tiles"]):
                        slot = t % 3
                        if k == "rotary" and t % 2:
                            n = t % 6 // 2
                            dve.wait_ge(evac, 4 + base + t + 1)
                            x1, x2 = stage[:, (t - 1) % 4, 0:NB3], stage[:, t % 4, 0:NB3]
                            co, si = cs[:, 0, n * NB3:(n + 1) * NB3], cs[:, 1, n * NB3:(n + 1) * NB3]
                            a, b = tmp[:, 0, 0:NB3], tmp[:, 1, 0:NB3]
                            free((t - 1) % 4)
                            free(t % 4)
                            chain.link(dve.tensor_tensor(a, x1, co, ALU.mult))
                            chain.link(dve.tensor_tensor(b, x2, si, ALU.mult))
                            chain.link(dve.tensor_tensor(ost[:, (t - 1) % 4, 0:NB3], a, b, ALU.subtract))
                            chain.link(dve.tensor_tensor(a, x2, co, ALU.mult))
                            chain.link(dve.tensor_tensor(b, x1, si, ALU.mult))
                            dve.sem_inc(stage_read, 1)
                            chain.link(dve.tensor_tensor(ost[:, t % 4, 0:NB3], a, b, ALU.add))
                            dve.sem_inc(posted, 1)
                        elif k == "norm":
                            st = stage[:, slot, :].rearrange("p (h c) -> p h c", h=4)
                            os = ost[:, slot, :].rearrange("p (h c) -> p h c", h=4)
                            dve.wait_ge(evac, 4 + base + t + 1)
                            free(slot)
                            chain.link(dve.tensor_tensor(tmp[:, 0, :], stage[:, slot, :], stage[:, slot, :], ALU.mult))
                            chain.link(dve.tensor_reduce(small[:, 0, 0, :], tmp[:, 0, :].rearrange("p (h c) -> p h c", h=4), AX.X, ALU.add))
                            n = g["post0"] + (2 * i + s) * TILES + t
                            dve.tensor_scalar(small[:, 0, 1, :], small[:, 0, 0, :], 1.0 / DH, EPS, ALU.mult, ALU.add).then_inc(root_in, 1)
                            dve.wait_ge(root_out, n + 1)
                            chain.link(dve.reciprocal(small[:, 0, 3, :], small[:, 0, 2, :]))
                            r = small[:, 0, 3, :].rearrange("p (h o) -> p h o", o=1).to_broadcast([P, 4, DH])
                            gb = gains[:, nn:nn + 1, :].to_broadcast([P, 4, DH])
                            t4 = tmp[:, 1, :].rearrange("p (h c) -> p h c", h=4)
                            chain.link(dve.tensor_tensor(t4, st, r, ALU.mult))
                            dve.sem_inc(stage_read, 1)
                            if g["scale"] != 1.0:
                                chain.link(dve.scalar_tensor_tensor(os, t4, g["scale"], gb, ALU.mult, ALU.mult))
                            else:
                                chain.link(dve.tensor_tensor(os, t4, gb, ALU.mult))
                            dve.sem_inc(posted, 1)
                        elif k == "residual":
                            dve.wait_ge(evac, 4 + base + t + 1)
                            free(slot)
                            col = g["col"](i, s)
                            dve.wait_ge(posted, base + max(t, 1) + 2)
                            chain.link(dve.tensor_tensor(tmp[:, t % 2, :], stage[:, slot, :], gate[:, int(t == PT), col:col + CW], ALU.mult))
                            dve.sem_inc(stage_read, 1)
                            dve.wait_ge(rin_landed[t % 3], 16 * (3 * (2 * i + s) + t // 3 + 1))
                            dve.tensor_tensor(ost[:, slot, :], tmp[:, t % 2, :], rin[:, t % 3], ALU.add).then_inc(posted, 1)
                        if t % 2 and t < 2 * SUBS and not stop:
                            split_lo(pr, dve, c + 1, 1 - s, t // 2)
                    assert chain.n - start == per_chunk, (chain.n, start)
                norm_no += k == "norm"
                pairs(dve, g, body)
                chain.n = start + 2 * g["pairs"] * per_chunk
                chain.base = 0


def retention(pr):
    nc, dr = pr.nc, pr.dram
    NH2 = DK // P
    with ExitStack() as ctx:
        sb = lambda n, s, dt=F32: ctx.enter_context(nc.sbuf_tensor(f"ret_{n}", s, dt))
        ps = lambda n, s: ctx.enter_context(nc.psum_tensor(f"ret_{n}", s, F32))
        sem = ctx.enter_context(semaphores(nc, "ret_"))
        qT = sb("qT", [P, NH2, TOKENS])
        kT = sb("kT", [P, NH2, TOKENS])
        v = sb("v", [P, TILES, DV])
        g = sb("g", [P, TILES, DV])
        intra = sb("intra", [P, 2, RH, P])
        qdec = sb("qdec", [P, RH, 3, P])
        kdec = sb("kdec", [P, RH, 1 + DEC_BATCH])
        cdec = sb("cdec", [P, 2, RH])
        s_in = sb("s_in", [P, 2, P])
        k_tok = sb("k_tok", [P, 2, DK])
        k_str = sb("k_str", [P, 2, DK])
        q_dec = sb("q_dec", [P, 2, NH2, P])
        state = sb("state", [P, 2, NH2, DV])
        r_in = sb("r_in", [P, 2, 4, NH2, DV])
        normed = sb("normed", [P, 2, DV])
        ost = sb("ost", [P, 2, DV])
        st6 = sb("st6", [P, 2, 6])
        mv = sb("mv", [P, 2, 2])
        sc = sb("sc", [P, 2, 4])
        ps_s = ps("ps_s", [P, 2, 512])
        ps_o = ps("ps_o", [P, 2, 512])
        ps_u = ps("ps_u", [P, 2, 2, 512])
        tabs, q_in, v_in, vs_in, g_in = sem("tabs"), sem("q_in"), sem("v_in"), sem("vs_in"), sem("g_in")
        r_landed = [sem(f"r_landed{i}") for i in range(2)]
        r_stored = [sem(f"r_stored{i}") for i in range(2)]
        ost_stored = [sem(f"ost_stored{i}") for i in range(2)]
        p_stored = sem("p_stored")
        scored, decayed, q_ready = sem("scored"), sem("decayed"), sem("q_ready")
        upd, state_new, str_k, o_done = sem("upd"), sem("state_new"), sem("str_k"), sem("o_done")
        own, var, root, scaled, n_done, gated = sem("own"), sem("var"), sem("root"), sem("scaled"), sem("n_done"), sem("gated")
        head_done = sem("head_done")
        PAIRS = DEC_BATCH
        U = PT + PAIRS
        block = ctx.enter_context(nc.Block())

        @block.sync
        def _(sp):
            sp.dma_start(intra[:, 0], pr.table["intra"]).then_inc(tabs, 16)
            sp.dma_start(intra[:, 1], pr.table["intra_s"]).then_inc(tabs, 16)
            sp.dma_start(qdec[:, :, 0], pr.table["qdec"]).then_inc(tabs, 16)
            sp.dma_start(qdec[:, :, 1:3], pr.table["qdec_s"]).then_inc(tabs, 16)
            with nc.allow_non_contiguous_dma(reason="small tables, once"):
                sp.dma_start(kdec[:, :, 0:1], pr.table["kdec"]).then_inc(tabs, 16)
                sp.dma_start(kdec[:, :, 1:], pr.table["kdec_s"]).then_inc(tabs, 16)
            sp.dma_start(cdec[:, 0], pr.table["cdec"]).then_inc(tabs, 16)
            sp.dma_start(cdec[:, 1], pr.table["cdec_s"]).then_inc(tabs, 16)
            with sp.Fori(0, RH) as h:
                sp.wait_ge(scored, h * TILES + 1)
                sp.wait_ge(q_ready, h * TILES + 1)
                sp.dma_start(kT[:, :, :], dr["qkT"][bass.ds(h * 4 + 2, 2)].rearrange("a p t -> p a t")).then_inc(q_in, 16)
                sp.dma_start(qT[:, :, :], dr["qkT"][bass.ds(h * 4, 2)].rearrange("a p t -> p a t")).then_inc(q_in, 16)
                sp.wait_ge(o_done, h * TILES + 1)
                sp.dma_start(v[:, 0:PT, :], dr["v"][0:SEQ, bass.ds(h * DV, DV)].rearrange("(t p) c -> p t c", p=P)).then_inc(v_in, 16)
                sp.wait_ge(upd, h * U + 1)
                sp.dma_start(v[:, PT, :], dr["v"][SEQ:TOKENS, bass.ds(h * DV, DV)]).then_inc(vs_in, 16)
                sp.wait_ge(gated, h * TILES + 1)
                sp.dma_start(g[:, :, :], dr["g"][:, bass.ds(h * DV, DV)].rearrange("(t p) c -> p t c", p=P)).then_inc(g_in, 16)
                for par in range(2):
                    sp.wait_ge(r_stored[par], h * 64 + 64)
                    for j in range(4):
                        sp.dma_start(r_in[:, par, j], dr["state_ret"][2 * j + par, bass.ds(h, 1)].rearrange("o (a p) c -> p (o a) c", p=P)).then_inc(r_landed[par], 16)

        @block.tensor
        def _(pe):
            pe.sem_inc(o_done, 1)
            pe.sem_inc(upd, 1)
            pe.sem_inc(scored, 1)
            with pe.Fori(0, RH) as h:
                def scores(c):
                    pe.wait_ge(decayed, h * TILES + max(c, 1) + 1)
                    for a in range(NH2):
                        pe.matmul(ps_s[:, c % 2, 0:P], kT[:, a, c * P:(c + 1) * P], qT[:, a, c * P:(c + 1) * P], start=a == 0, stop=a == NH2 - 1)
                    for a in range(NH2):
                        ins = pe.transpose(ps_s[:, c % 2, P + a * P:P + (a + 1) * P], kT[:, a, c * P:(c + 1) * P], pr.ident[:, :])
                    ins.then_inc(scored, 1)

                def output(c):
                    o = ps_o[:, c % 2, :]
                    pe.wait_ge(n_done, h * TILES + max(c, 1) + 1)
                    pe.wait_ge(decayed, h * TILES + c + 3)
                    ins = pe.matmul(o, s_in[:, c % 2, :], v[:, c, :], start=True, stop=c == 0)
                    if c:
                        pe.wait_ge(q_ready, h * TILES + c + 2)
                        pe.wait_ge(state_new, h * U + c + 1)
                        for a in range(NH2):
                            ins = pe.matmul(o, q_dec[:, c % 2, a, :], state[:, (c - 1) % 2, a, :], start=False, stop=a == NH2 - 1)
                    ins.then_inc(o_done, 1)

                def update(n, keys):
                    pe.wait_ge(state_new, h * U + max(n, 1))
                    c = min(n, PT)
                    for a in range(NH2):
                        ins = pe.matmul(ps_u[:, n % 2, a, :], keys[:, a * P:(a + 1) * P], v[:, c, :], start=True, stop=True)
                    ins.then_inc(upd, 1)

                pe.wait_ge(q_in, h * 32 + 32)
                scores(0)
                pe.wait_ge(v_in, h * 16 + 16)
                for c in range(PT):
                    scores(c + 1)
                    pe.wait_ge(decayed, h * TILES + c + 3)
                    update(c, k_tok[:, c % 2, :])
                    output(c)
                pe.wait_ge(vs_in, h * 16 + 16)
                for m in range(2):
                    pe.wait_ge(str_k, h * PAIRS + m + 1)
                    update(PT + m, k_str[:, m % 2, :])
                pe.wait_ge(n_done, h * TILES + PT + 1)
                pe.wait_ge(decayed, h * TILES + PT + 3)
                pe.wait_ge(q_ready, h * TILES + PT + 2)
                pe.matmul(ps_o[:, PT % 2, :], s_in[:, PT % 2, :], v[:, PT, :], start=True, stop=False, skip_group_check=True)
                for par in range(2):
                    pe.wait_ge(r_landed[par], h * 64 + 64)
                    for a in range(NH2):
                        for j in range(4):
                            ins = pe.matmul(ps_o[BR * j:BR * (j + 1), PT % 2, :], q_dec[:, par, a, BR * j:BR * (j + 1)], r_in[:, par, j, a, :],
                                            start=False, stop=par == 1 and a == NH2 - 1, tile_position=(0, BR * j), skip_group_check=True)
                ins.then_inc(o_done, 1)
                for m in range(2, PAIRS):
                    pe.wait_ge(str_k, h * PAIRS + m + 1)
                    update(PT + m, k_str[:, m % 2, :])

        @block.gpsimd
        def _(pool):
            credit(pool, pr, ost_stored)
            pool.sem_inc(q_ready, 1)
            pool.sem_inc(gated, 1)
            pool.wait_ge(tabs, 8 * 16)
            with pool.Fori(0, RH) as h:
                pool.wait_ge(q_in, h * 32 + 32)
                stand(pool, pr)

                def queries(c):
                    if c < PT:
                        if c >= 2:
                            pool.wait_ge(o_done, h * TILES + c)
                            stand(pool, pr)
                        for a in range(NH2):
                            ins = pool.tensor_tensor(q_dec[:, c % 2, a, :], qT[:, a, c * P:(c + 1) * P], qdec[:, bass.ds(h, 1), 0, :].rearrange("p o i -> p (o i)"), ALU.mult)
                    else:
                        pool.wait_ge(o_done, h * TILES + PT + 1)
                        stand(pool, pr)
                        for par in range(2):
                            for a in range(NH2):
                                ins = pool.tensor_tensor(q_dec[:, par, a, :], qT[:, a, PT * P:], qdec[:, bass.ds(h, 1), 1 + par, :].rearrange("p o i -> p (o i)"), ALU.mult)
                    ins.then_inc(q_ready, 1)

                def gate_and_store(c):
                    pool.wait_ge(scaled, h * TILES + c + 1)
                    if c == 0:
                        pool.wait_ge(g_in, h * 16 + 16)
                    pool.wait_ge(ost_stored[c % 2], h * 16 * (5 - c % 2) + 16 * (c // 2) + 16)
                    pool.tensor_tensor(ost[:, c % 2, :], normed[:, c % 2, :], g[:, c, :], ALU.mult).then_inc(gated, 1)
                    pool.wait_ge(gated, h * TILES + c + 2)
                    pool.dma_start(dr["o"][c * P:(c + 1) * P, bass.ds(h * DV, DV)], ost[:, c % 2, :]).then_inc(ost_stored[c % 2], 16)

                queries(0)
                for c in range(TILES):
                    if c + 1 < TILES:
                        queries(c + 1)
                    gate_and_store(c)
            pool.wait_ge(ost_stored[0], 16 + RH * 16 * 5)
            pool.wait_ge(ost_stored[1], 16 + RH * 16 * 4)

        @block.scalar
        def _(act):
            act.sem_inc(n_done, 2)
            act.sem_inc(p_stored, 16)
            for s in range(2):
                act.sem_inc(r_stored[s], 64)
            with act.Fori(0, RH) as h:
                for c in range(TILES):
                    act.wait_ge(var, h * TILES + c + 1)
                    act.activation(sc[:, c % 2, 1:2], sc[:, c % 2, 0:1], ACT.Sqrt).then_inc(root, 1)
                    act.wait_ge(own, h * 6 * TILES + 6 * c + 6)
                    act.wait_ge(gated, h * TILES + c) if c >= 2 else act.wait_ge(gated, h * TILES + 1)
                    act.activation(normed[:, c % 2, :], ps_o[:, c % 2, :], ACT.Identity, bias=sc[:, c % 2, 3:4], scale=sc[:, c % 2, 2:3]).then_inc(scaled, 1)
                    act.wait_ge(scaled, h * TILES + c + 1)
                    act.sem_inc(n_done, 1)
                act.wait_ge(state_new, h * U + PT + 1)
                act.dma_start(dr["state_prompt"][bass.ds(h, 1)].rearrange("o (a p) c -> p (o a) c", p=P), state[:, (PT - 1) % 2]).then_inc(p_stored, 16)
                for m in range(PAIRS):
                    par, j = m // 4, m % 4
                    act.wait_ge(state_new, h * U + PT + m + 2)
                    act.dma_start(dr["state_sample"][2 * j + par, bass.ds(h, 1)].rearrange("o (a p) c -> p (o a) c", p=P), r_in[:, par, j]).then_inc(r_stored[par], 16)
            act.wait_ge(p_stored, 16 + 16 * RH)
            for s in range(2):
                act.wait_ge(r_stored[s], 64 + 64 * RH)

        def stream_state(dve, h, m):
            par, j = m // 4, m % 4
            dve.wait_ge(upd, h * U + PT + m + 2)
            dve.scalar_tensor_tensor(r_in[:, par, j], r_in[:, par, j], cdec[:, 1, bass.ds(h, 1)], ps_u[:, (PT + m) % 2], ALU.mult, ALU.add).then_inc(state_new, 1)

        @block.vector
        def _(dve):
            dve.sem_inc(decayed, 2)
            dve.sem_inc(state_new, 1)
            dve.wait_ge(tabs, 8 * 16)
            with dve.Fori(0, RH) as h:
                def decay(c):
                    dve.wait_ge(scored, h * TILES + c + 2)
                    if c >= 2:
                        dve.wait_ge(o_done, h * TILES + c)
                        dve.wait_ge(upd, h * U + c)
                    else:
                        dve.wait_ge(o_done, h * TILES + 1)
                        dve.wait_ge(upd, h * U + 1)
                    dve.tensor_tensor(s_in[:, c % 2, :], ps_s[:, c % 2, 0:P], intra[:, int(c == PT), bass.ds(h, 1), :].rearrange("p o i -> p (o i)"), ALU.mult)
                    if c < PT:
                        dve.tensor_scalar(k_tok[:, c % 2, :], ps_s[:, c % 2, P:3 * P], kdec[:, bass.ds(h, 1), 0:1].rearrange("p o i -> p (o i)"), None, ALU.mult).then_inc(decayed, 1)
                    else:
                        dve.tensor_copy(k_tok[:, c % 2, :], ps_s[:, c % 2, P:3 * P]).then_inc(decayed, 1)

                def new_state(c):
                    dve.wait_ge(upd, h * U + c + 2)
                    if c == 0:
                        dve.tensor_copy(state[:, 0], ps_u[:, 0]).then_inc(state_new, 1)
                    else:
                        dve.wait_ge(state_new, h * U + c + 1)
                        dve.scalar_tensor_tensor(state[:, c % 2], state[:, (c - 1) % 2], cdec[:, 0, bass.ds(h, 1)], ps_u[:, c % 2], ALU.mult, ALU.add).then_inc(state_new, 1)

                def statistics(c):
                    dve.wait_ge(o_done, h * TILES + c + 2)
                    n = h * 6 * TILES + 6 * c
                    s, z = c % 2, sc[:, c % 2, :]
                    dve.wait_ge(n_done, h * TILES + max(c, 1) + 1)
                    dve.bn_stats(st6[:, s, :], ps_o[:, s, :]).then_inc(own, 1)
                    dve.wait_ge(own, n + 1)
                    stand(dve, pr)
                    dve.bn_aggr(mv[:, s, :], st6[:, s, :]).then_inc(own, 1)
                    dve.wait_ge(own, n + 2)
                    dve.tensor_scalar(z[:, 0:1], mv[:, s, 1:2], EPS, None, ALU.add).then_inc(own, 1)
                    dve.wait_ge(own, n + 3)
                    dve.sem_inc(var, 1)
                    dve.wait_ge(root, h * TILES + c + 1)
                    dve.reciprocal(z[:, 2:3], z[:, 1:2]).then_inc(own, 1)
                    dve.wait_ge(own, n + 4)
                    dve.tensor_scalar(z[:, 3:4], mv[:, s, 0:1], z[:, 2:3], None, ALU.mult).then_inc(own, 1)
                    dve.wait_ge(own, n + 5)
                    dve.tensor_scalar(z[:, 3:4], z[:, 3:4], -1.0, None, ALU.mult).then_inc(own, 1)

                def stream_keys(m):
                    par, j = m // 4, m % 4
                    if m >= 2:
                        dve.wait_ge(upd, h * U + PT + m)
                    dve.tensor_scalar(k_str[:, m % 2, :], k_tok[:, PT % 2, :], kdec[:, bass.ds(h, 1), 1 + 2 * j + par:2 + 2 * j + par].rearrange("p o i -> p (o i)"), None, ALU.mult).then_inc(str_k, 1)

                decay(0)
                for c in range(PT):
                    decay(c + 1)
                    if c == PT - 1:
                        dve.wait_ge(decayed, h * TILES + TILES + 2)
                        for m in range(2):
                            stream_keys(m)
                    if c == 0:
                        dve.wait_ge(p_stored, h * 16 + 16)
                    new_state(c)
                    statistics(c)
                for m in range(2, 4):
                    stream_keys(m)
                dve.wait_ge(o_done, h * TILES + TILES + 1)
                for m in range(2):
                    stream_state(dve, h, m)
                statistics(PT)
                for m in range(4, PAIRS):
                    stream_keys(m)
                    stream_state(dve, h, m - 2)
                stream_state(dve, h, PAIRS - 2)
                stream_state(dve, h, PAIRS - 1)


def attention(pr):
    nc, dr = pr.nc, pr.dram
    G = FH // KVH
    UNITS = G * PT + 2
    SCALE_L = (PT + 1) * P
    blocks = [u // G + 1 for u in range(G * PT)] + [2, 2]
    groups = [-(-b // 4) for b in blocks]
    first = [sum(groups[:u]) for u in range(UNITS + 1)]
    GROUPS = first[-1]
    with ExitStack() as ctx:
        sb = lambda n, s, dt=F32: ctx.enter_context(nc.sbuf_tensor(f"fox_{n}", s, dt))
        ps = lambda n, s: ctx.enter_context(nc.psum_tensor(f"fox_{n}", s, F32))
        sem = ctx.enter_context(semaphores(nc, "fox_"))
        work = sb("work", [P, 4 * TOKENS + 2 * SEQ])
        f_tmp = work[0:FH, 0:3 * TOKENS].rearrange("p (a c) -> p a c", a=3)
        f_in = work[0:FH, 3 * TOKENS:4 * TOKENS]
        ones = work[0:FH, 4 * TOKENS:4 * TOKENS + SEQ]
        c_logf = work[0:FH, 4 * TOKENS + SEQ:4 * TOKENS + 2 * SEQ]
        qT = work[:, 0:2 * SEQ].rearrange("p (a c) -> p a c", a=G)
        s_sb = work[:, 2 * SEQ:4 * SEQ].rearrange("p (a c) -> p a c", a=2)
        pT = work[:, 4 * SEQ:5 * SEQ].rearrange("p (a c) -> p a c", a=2)
        kT = work[:, 5 * SEQ:5 * SEQ + TILES * P]
        f_bias = sb("f_bias", [FH, 1])
        logf = sb("logf", [FH, TOKENS])
        logf_tok = sb("logf_tok", [P, TILES, FH])
        c_tok = sb("c_tok", [P, DEC_BATCH, FH])
        cum = sb("cum", [FH, SEQ])
        cum_c = sb("cum_c", [FH, DEC_BATCH * PAST])
        cum_n = sb("cum_n", [FH, P])
        sel_head = sb("sel_head", [FH, FH, P])
        sel_group = sb("sel_group", [FH, KVH, P])
        mask = sb("mask", [P, P])
        mask_s = sb("mask_s", [P, 2, P])
        own_s = sb("own_s", [P, 2, P])
        nf = sb("nf", [P, FH, SEQ])
        nf_s = sb("nf_s", [P, KVH, 2, 2, P])
        fq = sb("fq", [P, PT, FH])
        fq_s = sb("fq_s", [P, KVH, 2])
        own_t = sb("own_t", [P, P])
        q = sb("q", [P, TILES, G * DH])
        k = sb("k", [P, TILES, DH])
        v = sb("v", [P, TILES, DH])
        ck = sb("ck", [P, DEC_BATCH, DH])
        cv = sb("cv", [P, DEC_BATCH, DH])
        gt = sb("gt", [P, G * PT + 2, DH])
        ckT = sb("ckT", [P, DEC_BATCH * P])
        qTs = sb("qTs", [P, DEC_BATCH, G, DEC_SEQ])
        ost = sb("ost", [P, 2, DH])
        mx = sb("mx", [P, 3, 4])
        ps_s = ps("ps_s", [P, 2, 2, 512])
        ps_t = ps("ps_t", [P, 2, 512])
        ps_o = ps("ps_o", [P, 2, 512])
        f_landed, own, rec = sem("f_landed"), sem("own"), sem("rec")
        z_ready, e_done, lf_ready, lf_turned, lf_out = sem("z_ready"), sem("e_done"), sem("lf_ready"), sem("lf_turned"), sem("lf_out")
        c_turned, c_ready, lf_stored = sem("c_turned"), sem("c_ready"), sem("lf_stored")
        cum_ready, nf_done, nf_read, nfs_done, nfs_read, fq_turned, prep = sem("cum_ready"), sem("nf_done"), sem("nf_read"), sem("nfs_done"), sem("nfs_read"), sem("fq_turned"), sem("prep")
        qk_in, v_in, g_in = sem("qk_in"), sem("v_in"), sem("g_in")
        x_turned, x_ready = sem("x_turned"), sem("x_ready")
        s_done, s_read, soft, negm, p_done = sem("s_done"), sem("s_read"), sem("soft"), sem("negm"), sem("p_done")
        t_done, pt_ready, pv_done, fin, diag = sem("t_done"), sem("pt_ready"), sem("pv_done"), sem("fin"), sem("diag")
        stored = [sem(f"stored{i}") for i in range(2)]
        X = -(-(TILES + DEC_BATCH + G * TILES) // 4)
        items = [("k", t) for t in range(TILES)] + [("c", b) for b in range(DEC_BATCH)] + [("q", t * G + h) for h in range(G) for t in range(TILES)]
        SELF = 5
        block = ctx.enter_context(nc.Block())

        @block.sync
        def _(sp):
            sp.dma_start(f_in[:, :], dr["f_raw"]).then_inc(f_landed, 16)
            sp.dma_start(f_bias[:, :], dr["kv_fb"]).then_inc(f_landed, 16)
            with nc.allow_non_contiguous_dma(reason="eight columns"):
                sp.dma_start(c_tok[:, :, :], dr["cache_logf"].rearrange("b p h -> p b h")).then_inc(f_landed, 16)
            for dst, name in ((sel_head, "sel_head"), (sel_group, "sel_group"), (mask, "mask"), (mask_s, "mask_s"), (own_s, "own_s")):
                flat = dst[:] if len(dst.shape) == 2 else dst[:].rearrange("p a b -> p (a b)")
                sp.dma_start(flat, pr.table[name]).then_inc(f_landed, 16)
            with sp.Fori(0, KVH) as n:
                kvc = bass.ds(n * DH, DH)
                hc = bass.ds(n * G * DH, G * DH)
                sp.wait_ge(x_turned, n * X + 1)
                sp.dma_start(k[:, 0:PT], dr["k_prompt"][:, kvc].rearrange("(t p) c -> p t c", p=P)).then_inc(qk_in, 16)
                sp.dma_start(k[:, PT], dr["k_sample"][:, kvc]).then_inc(qk_in, 16)
                sp.dma_start(ck[:, :, :], dr["cache_k"][:, :, kvc].rearrange("b p c -> p b c")).then_inc(qk_in, 16)
                sp.dma_start(q[:, :, :], dr["q"][:, hc].rearrange("(t p) c -> p t c", p=P)).then_inc(qk_in, 16)
                sp.wait_ge(fin, n * UNITS + 1)
                sp.dma_start(v[:, 0:PT], dr["v_prompt"][:, kvc].rearrange("(t p) c -> p t c", p=P)).then_inc(v_in, 16)
                sp.dma_start(v[:, PT], dr["v_sample"][:, kvc]).then_inc(v_in, 16)
                sp.dma_start(cv[:, :, :], dr["cache_v"][:, :, kvc].rearrange("b p c -> p b c")).then_inc(v_in, 16)
                sp.dma_start(gt[:, 0:G * PT].rearrange("p (t g) c -> p t (g c)", g=G), dr["g2"][0:SEQ, hc].rearrange("(t p) c -> p t c", p=P)).then_inc(g_in, 16)
                for r in range(2):
                    for j in range(4):
                        for h in range(G):
                            p0, b = BR * j + DEC_SEQ * h, 4 * r + j
                            sp.dma_start(gt[p0:p0 + DEC_SEQ, G * PT + r], dr["g2"][SEQ + b * DEC_SEQ:SEQ + (b + 1) * DEC_SEQ, bass.ds(n * G * DH + h * DH, DH)]).then_inc(g_in, 16)

        @block.tensor
        def _(pe):
            pe.wait_ge(lf_ready, 1)
            for t in range(TILES):
                ins = pe.transpose(ps_t[:, 0, t * FH:(t + 1) * FH], logf[:, t * P:(t + 1) * P], pr.ident[0:FH, 0:FH])
            ins.then_inc(lf_turned, 1)
            pe.wait_ge(f_landed, 8 * 16)
            for b in range(DEC_BATCH):
                ins = pe.transpose(ps_s[0:FH, 0, b // 4, (b % 4) * P:(b % 4 + 1) * P], c_tok[:, b, :], pr.ident[:, :])
            ins.then_inc(c_turned, 1)
            pe.wait_ge(cum_ready, 1)
            for t in range(PT):
                ins = pe.transpose(ps_t[:, 1, t * FH:(t + 1) * FH], cum[:, t * P:(t + 1) * P], pr.ident[0:FH, 0:FH])
            ins.then_inc(fq_turned, 1)
            for h in range(FH):
                pe.wait_ge(nf_read, h + 1)
                for a in range(2):
                    ins = pe.matmul(ps_s[:, h % 2, a, :], sel_head[:, h, :], cum[:, a * 512:(a + 1) * 512], start=True, stop=True)
                ins.then_inc(nf_done, 1)
            for n in range(KVH):
                for r in range(2):
                    m = 2 * n + r
                    pe.wait_ge(nfs_read, m + 1)
                    pe.matmul(ps_o[:, m % 2, P:2 * P], sel_group[:, n, :], cum_n[:, :], start=True, stop=True, skip_group_check=True)
                    for j in range(4):
                        b = 4 * r + j
                        ins = pe.matmul(ps_o[BR * j:BR * (j + 1), m % 2, 0:P], sel_group[:, n, BR * j:BR * (j + 1)], cum_c[:, b * PAST:(b + 1) * PAST],
                                        start=True, stop=True, tile_position=(0, BR * j), skip_group_check=True)
                    ins.then_inc(nfs_done, 1)
            pe.wait_ge(prep, 3)

            with pe.Fori(0, KVH) as n:
                pe.wait_ge(qk_in, n * 64 + 64)
                for x in range(X):
                    pe.wait_ge(x_ready, n * X + x + 1)
                    for y, (what, z) in enumerate(items[4 * x:4 * x + 4]):
                        src = {"k": lambda: k[:, z, :], "c": lambda: ck[:, z, :], "q": lambda: q[:, z // G, (z % G) * DH:(z % G + 1) * DH]}[what]()
                        ins = pe.transpose(ps_t[:, x % 2, y * P:(y + 1) * P], src, pr.ident[:, :])
                    ins.then_inc(x_turned, 1)
                pe.wait_ge(x_ready, n * X + X + 2)

                def scores(u):
                    pe.wait_ge(s_read, n * UNITS + u + 1)
                    t, h = u // G, u % G
                    if u < G * PT:
                        L = (t + 1) * P
                        for a in range(-(-L // 512)):
                            w = min(512, L - 512 * a)
                            ins = pe.matmul(ps_s[:, u % 2, a, 0:w], qT[:, h, t * P:(t + 1) * P], kT[:, a * 512:a * 512 + w], start=True, stop=True)
                    else:
                        r = u - G * PT
                        rows = qTs[:, :, :, :].rearrange("p b g q -> p (b g q)")
                        pe.matmul(ps_s[:, u % 2, 0, P:2 * P], rows[:, r * P:(r + 1) * P], kT[:, SEQ:SEQ + P], start=True, stop=True, skip_group_check=True)
                        for j in range(4):
                            b = 4 * r + j
                            ins = pe.matmul(ps_s[BR * j:BR * (j + 1), u % 2, 0, 0:P], rows[:, b * BR:(b + 1) * BR], ckT[:, b * P:(b + 1) * P],
                                            start=True, stop=True, tile_position=(0, BR * j), skip_group_check=True)
                    ins.then_inc(s_done, 1)

                def turn(u, x):
                    m = first[u] + x
                    pe.wait_ge(pt_ready, n * GROUPS + m + 1)
                    for y in range(min(4, blocks[u] - 4 * x)):
                        b = 4 * x + y
                        ins = pe.transpose(ps_t[:, m % 2, y * P:(y + 1) * P], s_sb[:, u % 2, b * P:(b + 1) * P], pr.ident[:, :])
                    ins.then_inc(t_done, 1)

                def values(u, x):
                    m = first[u] + x
                    pe.wait_ge(pt_ready, n * GROUPS + m + 3)
                    o = ps_o[:, u % 2, 0:DH]
                    if u < G * PT:
                        for y in range(min(4, blocks[u] - 4 * x)):
                            b = 4 * x + y
                            ins = pe.matmul(o, pT[:, m % 2, y * P:(y + 1) * P], v[:, b, :], start=b == 0, stop=b == blocks[u] - 1)
                    else:
                        r = u - G * PT
                        pe.matmul(o, pT[:, m % 2, P:2 * P], v[:, PT, :], start=True, stop=False, skip_group_check=True)
                        for j in range(4):
                            ins = pe.matmul(ps_o[BR * j:BR * (j + 1), u % 2, 0:DH], pT[:, m % 2, BR * j:BR * (j + 1)], cv[:, 4 * r + j, :],
                                            start=False, stop=True, tile_position=(0, BR * j), skip_group_check=True)
                    ins.then_inc(pv_done, 1)

                scores(0)
                scores(1)
                pe.wait_ge(v_in, n * 48 + 48)
                for u in range(UNITS):
                    pe.wait_ge(p_done, n * UNITS + u + 1)
                    for x in range(groups[u]):
                        turn(u, x)
                    if u + 2 < UNITS:
                        scores(u + 2)
                    pe.wait_ge(fin, n * UNITS + u) if u >= 2 else pe.wait_ge(fin, n * UNITS + 1)
                    for x in range(groups[u]):
                        values(u, x)

        @block.scalar
        def _(act):
            act.sem_inc(nf_read, 2)
            act.sem_inc(x_ready, 2)
            act.sem_inc(x_turned, 1)
            act.sem_inc(pt_ready, 2)
            act.wait_ge(z_ready, 1)
            act.activation(f_tmp[:, 1, :], f_tmp[:, 0, :], ACT.Exp, scale=-1.0).then_inc(e_done, 1)
            act.wait_ge(e_done, 1)
            act.activation(f_tmp[:, 1, :], f_tmp[:, 1, :], ACT.Ln, bias=1.0).then_inc(e_done, 1)
            for h in range(FH):
                act.wait_ge(nf_done, h + 1)
                act.mul(nf[:, h, :].rearrange("p (a c) -> p a c", a=2), ps_s[:, h % 2], -1.0).then_inc(nf_read, 1)
            act.wait_ge(nf_read, 2 + FH)
            act.sem_inc(prep, 1)
            with act.Fori(0, KVH) as n:
                for x in range(X):
                    act.wait_ge(x_turned, n * X + x + 2)
                    for y, (what, z) in enumerate(items[4 * x:4 * x + 4]):
                        src = ps_t[:, x % 2, y * P:(y + 1) * P]
                        if what == "k":
                            ins = act.copy(kT[:, z * P:(z + 1) * P], src)
                        elif what == "c":
                            ins = act.copy(ckT[:, z * P:(z + 1) * P], src)
                        elif z // G < PT:
                            ins = act.copy(qT[:, z % G, (z // G) * P:(z // G + 1) * P], src)
                        else:
                            ins = act.copy(qTs[:, :, z % G, :], src.rearrange("p (b q) -> p b q", q=DEC_SEQ))
                    ins.then_inc(x_ready, 1)

                def exp(u):
                    act.wait_ge(negm, n * UNITS + u + 1)
                    w = s_sb[:, u % 2, 0:blocks[u] * P]
                    act.activation(w, w, ACT.Exp, bias=mx[:, u % 3, 1:2], accum_out=mx[:, u % 3, 2:3]).then_inc(p_done, 1)

                exp(0)
                for u in range(UNITS):
                    for x in range(groups[u]):
                        m = first[u] + x
                        act.wait_ge(t_done, n * GROUPS + m + 1)
                        if m >= 2:
                            act.wait_ge(pv_done, n * GROUPS + m - 1)
                        w = min(4, blocks[u] - 4 * x) * P
                        act.copy(pT[:, m % 2, 0:w], ps_t[:, m % 2, 0:w]).then_inc(pt_ready, 1)
                    if u + 1 < UNITS:
                        exp(u + 1)

        @block.gpsimd
        def _(pool):
            credit(pool, pr, stored)
            pool.wait_ge(lf_out, 1)
            with nc.allow_non_contiguous_dma(reason="rows of eight"):
                pool.dma_start(dr["logf_prompt"].rearrange("(t p) h -> p t h", p=P), logf_tok[:, 0:PT, :]).then_inc(lf_stored, 16)
                pool.dma_start(dr["logf_sample"], logf_tok[:, PT, :]).then_inc(lf_stored, 16)
            with pool.Fori(0, KVH) as n:
                for u in range(UNITS):
                    pool.wait_ge(fin, n * UNITS + u + 2)
                    if u < G * PT:
                        t, h = u // G, u % G
                        pool.dma_start(dr["o2"][t * P:(t + 1) * P, bass.ds(n * G * DH + h * DH, DH)], ost[:, u % 2, :]).then_inc(stored[u % 2], 16)
                    else:
                        r = u - G * PT
                        for j in range(4):
                            for h in range(G):
                                p0, b = BR * j + DEC_SEQ * h, 4 * r + j
                                pool.dma_start(dr["o2"][SEQ + b * DEC_SEQ:SEQ + (b + 1) * DEC_SEQ, bass.ds(n * G * DH + h * DH, DH)], ost[p0:p0 + DEC_SEQ, u % 2, :]).then_inc(stored[u % 2], 16)
            pool.wait_ge(lf_stored, 32)
            for s in range(2):
                pool.wait_ge(stored[s], 16 + KVH * (PT * 16 + 128))

        @block.vector
        def _(dve):
            chain = Chain(dve, own)
            dve.sem_inc(fin, 1)
            dve.sem_inc(s_read, 2)
            dve.sem_inc(nfs_read, 2)
            dve.wait_ge(f_landed, 8 * 16)
            z, a, lo = f_in[:, :], f_tmp[:, 0, :], f_tmp[:, 2, :]
            chain.link(dve.tensor_scalar(z, z, f_bias[:, 0:1], None, ALU.add))
            chain.link(dve.tensor_scalar(a, z, -1.0, None, ALU.mult))
            dve.tensor_tensor(a, a, z, ALU.max).then_inc(z_ready, 1)
            dve.tensor_scalar(lo, z, 0.0, None, ALU.min).then_inc(own, 1)
            chain.n += 1
            dve.wait_ge(own, chain.n)
            dve.memset(ones[:, :], 1.0).then_inc(own, 1)
            chain.n += 1
            dve.wait_ge(own, chain.n)
            dve.wait_ge(e_done, 2)
            chain.link(dve.tensor_tensor(logf[:, :], lo, f_tmp[:, 1, :], ALU.subtract))
            dve.sem_inc(lf_ready, 1)
            dve.wait_ge(lf_turned, 1)
            dve.tensor_copy(logf_tok[:, :, :], ps_t[:, 0, 0:TILES * FH].rearrange("p (t h) -> p t h", t=TILES)).then_inc(lf_out, 1)
            dve.wait_ge(c_turned, 1)
            chain.link(dve.tensor_copy(c_logf[:, :].rearrange("p (a c) -> p a c", a=2), ps_s[0:FH, 0]))
            chain.link(dve.tensor_tensor_scan(cum[:, :], ones[:, :], logf[:, 0:SEQ], 0.0, ALU.mult, ALU.add))
            for b in range(DEC_BATCH):
                c = slice(b * PAST, (b + 1) * PAST)
                chain.link(dve.tensor_tensor_scan(cum_c[:, c], ones[:, 0:PAST], c_logf[:, c], 0.0, ALU.mult, ALU.add))
                w = slice(b * DEC_SEQ, (b + 1) * DEC_SEQ)
                chain.link(dve.tensor_tensor_scan(cum_n[:, w], ones[:, 0:DEC_SEQ], logf[:, SEQ + b * DEC_SEQ:SEQ + (b + 1) * DEC_SEQ],
                                                  cum_c[:, (b + 1) * PAST - 1:(b + 1) * PAST], ALU.mult, ALU.add))
            dve.sem_inc(cum_ready, 1)
            dve.wait_ge(fq_turned, 1)
            chain.link(dve.tensor_copy(fq[:, :, :], ps_t[:, 1, 0:PT * FH].rearrange("p (t h) -> p t h", t=PT)))
            dve.sem_inc(prep, 1)
            for n in range(KVH):
                for r in range(2):
                    m = 2 * n + r
                    dve.wait_ge(nfs_done, m + 1)
                    f_new = ps_o[:, m % 2, P:2 * P]
                    chain.link(dve.tensor_tensor(own_t[:, :], f_new, own_s[:, r, :], ALU.mult))
                    chain.link(dve.tensor_reduce(fq_s[:, n, r:r + 1], own_t[:, :], AX.X, ALU.add))
                    chain.link(dve.tensor_scalar(nf_s[:, n, r, 0, :], ps_o[:, m % 2, 0:P], -1.0, None, ALU.mult))
                    chain.link(dve.scalar_tensor_tensor(nf_s[:, n, r, 1, :], f_new, -1.0, mask_s[:, r, :], ALU.mult, ALU.add))
                    dve.sem_inc(nfs_read, 1)
            dve.sem_inc(prep, 1)
            start = chain.n
            dve.wait_ge(prep, 3)
            with dve.Fori(0, KVH) as n:
                def softmax(u):
                    dve.wait_ge(s_done, n * UNITS + u + 1)
                    if u >= 2:
                        dve.wait_ge(t_done, n * GROUPS + first[u - 1])
                    own0 = start + n * UNITS * 3 + u * 3
                    s, L = u % 2, blocks[u] * P
                    if u < G * PT:
                        t, h = u // G, u % G
                        head = bass.ds(n * G + h, 1)
                        sv, pv = s_sb[:, s, 0:L], ps_s[:, s].rearrange("p a c -> p (a c)")[:, 0:L]
                        dve.scalar_tensor_tensor(sv, pv, fq[:, t, head], nf[:, head, 0:L].rearrange("p o c -> p (o c)"), ALU.add, ALU.add).then_inc(own, 1)
                        dve.wait_ge(own, own0 + 1)
                        dve.tensor_tensor(s_sb[:, s, L - P:L], s_sb[:, s, L - P:L], mask[:, :], ALU.add).then_inc(own, 1)
                    else:
                        r = u - G * PT
                        dve.scalar_tensor_tensor(s_sb[:, s, 0:L], ps_s[:, s, 0, 0:L], fq_s[:, bass.ds(n, 1), r:r + 1].rearrange("p o c -> p (o c)"),
                                                 nf_s[:, bass.ds(n, 1), r].rearrange("p o a c -> p (o a c)"), ALU.add, ALU.add).then_inc(own, 2)
                    dve.wait_ge(own, own0 + 2)
                    dve.sem_inc(s_read, 1)
                    dve.tensor_reduce(mx[:, u % 3, 0:1], s_sb[:, s, 0:L], AX.X, ALU.max).then_inc(own, 1)
                    dve.wait_ge(own, own0 + 3)
                    dve.tensor_scalar(mx[:, u % 3, 1:2], mx[:, u % 3, 0:1], -1.0, None, ALU.mult).then_inc(negm, 1)

                def finish(u):
                    s = u % 2
                    dve.wait_ge(pv_done, n * GROUPS + first[u + 1])
                    if u == 0:
                        dve.wait_ge(g_in, n * 17 * 16 + 17 * 16)
                    dve.wait_ge(stored[s], n * (PT * 16 + 128) + 16 + 16 * (u // 2))
                    dve.reciprocal(mx[:, u % 3, 3:4], mx[:, u % 3, 2:3]).then_inc(rec, 1)
                    dve.wait_ge(rec, n * UNITS + u + 1)
                    dve.scalar_tensor_tensor(ost[:, s, :], ps_o[:, s, 0:DH], mx[:, u % 3, 3:4], gt[:, u, :], ALU.mult, ALU.mult).then_inc(fin, 1)

                softmax(0)
                softmax(1)
                for u in range(UNITS):
                    if u + 2 < UNITS:
                        softmax(u + 2)
                    finish(u)


def build(nc, dram, table):
    with ExitStack() as ctx:
        pr = Program(nc, ctx, dram, table)
        dr = dram

        def tile_rows(name, t):
            return dr[name][t * P:(t + 1) * P, :]

        def columns_of(name, c0):
            return lambda c, w: dr[name][:, c0 + c:c0 + c + w].rearrange("(t p) c -> p t c", p=P)

        def x_rows(t):
            return dr["x_prompt"][t * P:(t + 1) * P, :] if t < PT else dr["x_sample"]

        def to_rows(name, c0=0):
            return lambda c, t: dr[name][t * P:(t + 1) * P, bass.ds(c * CW + c0, CW)]

        def split_rows(prompt, sample):
            return lambda c, t: dr[prompt][t * P:(t + 1) * P, :] if t < PT else dr[sample]

        def turned_rows(c, m):
            part, n, half = m // 6, m % 6 // 2, m % 2
            return dr["qkT"][bass.ds(c * 4 + part * 2 + half, 1), :, n * NB3:(n + 1) * NB3].rearrange("o p t -> p (o t)")

        qk = [head_columns(dr["a_w_in"], h) for h in range(RH)]
        wv = [columns(dr["a_w_in"], 0, 2 * D + CW * c) for c in range(4)]
        wg = [columns(dr["a_w_in"], 0, 2 * D + VW + CW * c) for c in range(4)]
        wo = [[columns(dr["a_w_out"], half * D, CW * c) for c in range(2)] for half in range(2)]
        wk, wvv = columns(dr["kv_w"], 0, 0), columns(dr["kv_w"], 0, CW)
        wq = [columns(dr["b_w_in"], 0, CW * c) for c in range(2)]
        wg2 = [columns(dr["b_w_in"], 0, D + CW * c) for c in range(2)]
        wo2 = [columns(dr["b_w_out"], 0, CW * c) for c in range(2)]

        condition(pr)
        project(pr, "in", x_rows, True, 0,
                [dict(kind="rotary", pairs=2, weights=qk, store=turned_rows),
                 dict(kind="copy", pairs=2, weights=wv, store=to_rows("v")),
                 dict(kind="silu", pairs=2, weights=wg, store=to_rows("g"))], 0, wo[0][0])
        retention(pr)
        for half in range(2):
            before = (lambda c, t: x_rows(t)[:, c * CW:(c + 1) * CW]) if half == 0 else (lambda c, t: tile_rows("x1a", t)[:, c * CW:(c + 1) * CW])
            project(pr, f"out{half}", columns_of("o", half * D), False, None,
                    [dict(kind="residual", pairs=1, weights=wo[half], col=lambda i, s: s * CW,
                          store=lambda c, t, half=half: tile_rows(("x1a", "x1")[half], t)[:, c * CW:(c + 1) * CW])],
                    12 + 2 * half, wo[1][0] if half == 0 else wk, gate_layer=0, residual=before, gain=pr.gn_g[:, half])
        project(pr, "kv", lambda t: tile_rows("x1", t), True, 1,
                [dict(kind="norm", pairs=1, weights=[wk, wvv], gain=dr["k_norm_g"], scale=1.0, plain=1,
                      store=lambda c, t: split_rows(*(("k_prompt", "k_sample"), ("v_prompt", "v_sample"))[c])(c, t))],
                16, wq[0], forget=True)
        project(pr, "q", lambda t: tile_rows("x1", t), True, 2,
                [dict(kind="norm", pairs=1, weights=wq, gain=dr["b_q_norm_g"], scale=DH ** -0.5, store=to_rows("q")),
                 dict(kind="silu", pairs=1, weights=wg2, store=to_rows("g2"))], 18, wo2[0], known=True)
        attention(pr)
        project(pr, "end", columns_of("o2", 0), False, None,
                [dict(kind="residual", pairs=1, weights=wo2, col=lambda i, s: s * CW,
                      store=lambda c, t: (dr["y_prompt"][t * P:(t + 1) * P, c * CW:(c + 1) * CW] if t < PT else dr["y_sample"][:, c * CW:(c + 1) * CW]))],
                22, None, gate_layer=1, residual=lambda c, t: tile_rows("x1", t)[:, c * CW:(c + 1) * CW])


_SHAPES = {
    "x_prompt": (SEQ, D), "x_sample": (P, D), "state_ret": (DEC_BATCH, RH, DK, DV),
    "cache_k": (DEC_BATCH, PAST, KVH * DH), "cache_v": (DEC_BATCH, PAST, KVH * DH), "cache_logf": (DEC_BATCH, PAST, FH),
    "c_prompt": (1, D), "c_sample": (DEC_BATCH, D),
    "a_norm_g": (1, D), "a_ada_w": (D, 3 * D), "a_ada_b": (1, 3 * D), "a_w_in": (D, 6 * D), "a_gn_g": (1, VW), "a_w_out": (VW, D),
    "kv_norm_g": (1, D), "kv_ada_w": (D, 2 * D), "kv_ada_b": (1, 2 * D), "kv_w": (D, 2 * KVH * DH + FH), "kv_fb": (FH, 1), "k_norm_g": (1, DH),
    "b_norm_g": (1, D), "b_ada_w": (D, 3 * D), "b_ada_b": (1, 3 * D), "b_w_in": (D, 2 * D), "b_q_norm_g": (1, DH), "b_w_out": (D, D),
}
_OUTS = {
    "y_prompt": (SEQ, D), "y_sample": (P, D), "state_prompt": (RH, DK, DV), "k_prompt": (SEQ, KVH * DH), "v_prompt": (SEQ, KVH * DH),
    "logf_prompt": (SEQ, FH), "state_sample": (DEC_BATCH, RH, DK, DV), "k_sample": (P, KVH * DH), "v_sample": (P, KVH * DH), "logf_sample": (P, FH),
}
_FINAL = {
    "y_prompt": (1, SEQ, D), "y_sample": (DEC_BATCH, DEC_SEQ, D), "state_prompt": (1, 1, RH, DK, DV), "k_prompt": (1, SEQ, KVH, DH),
    "v_prompt": (1, SEQ, KVH, DH), "logf_prompt": (1, SEQ, FH), "state_sample": (1, DEC_BATCH, RH, DK, DV),
    "k_sample": (DEC_BATCH, DEC_SEQ, KVH, DH), "v_sample": (DEC_BATCH, DEC_SEQ, KVH, DH), "logf_sample": (DEC_BATCH, DEC_SEQ, FH),
}
_SCRATCH = {
    "credit": (4, P),
    "gate": (P, 2, 2, D), "qkT": (4 * RH, P, TOKENS), "v": (TOKENS, VW), "g": (TOKENS, VW), "o": (TOKENS, VW),
    "x1a": (TOKENS, D), "x1": (TOKENS, D), "f_raw": (FH, TOKENS), "q": (TOKENS, D), "g2": (TOKENS, D), "o2": (TOKENS, D),
}


def kernel(**inputs):
    import concourse.bacc as bacc
    from concourse.bass_utils import run_bass_kernel_spmd

    nc = bacc.Bacc("TRN2", target_bir_lowering=False, num_devices=1)
    arrays, dram, table = {}, {}, {}
    for name, shape in _SHAPES.items():
        arrays[f"in_{name}"] = np.ascontiguousarray(inputs[name]).reshape(shape)
        dram[name] = nc.dram_tensor(f"in_{name}", shape, F32, kind="ExternalInput").ap()
    for name, a in tables().items():
        arrays[f"table_{name}"] = a
        table[name] = nc.dram_tensor(f"table_{name}", a.shape, F32, kind="ExternalInput").ap()
    for name, shape in _OUTS.items():
        dram[name] = nc.dram_tensor(f"out_{name}", shape, F32, kind="ExternalOutput").ap()
    for name, shape in _SCRATCH.items():
        dram[name] = nc.dram_tensor(f"scratch_{name}", shape, F32, kind="Internal").ap()
    build(nc, dram, table)
    r = run_bass_kernel_spmd(nc, [arrays], core_ids=[0])
    return tuple(r.results[0][f"out_{name}"].reshape(_FINAL[name]) for name in _OUTS)
```

```python
from contextlib import ExitStack, contextmanager

import numpy as np
import concourse.bass as bass
from concourse import mybir

F32 = mybir.dt.float32
F32R = mybir.dt.float32r
ALU = mybir.AluOpType
ACT = mybir.ActivationFunctionType
AX = mybir.AxisListType

P = 128
D = 1024
SEQ = 1024
DEC_BATCH, DEC_SEQ, PAST = 8, 16, 128
TOKENS = SEQ + DEC_BATCH * DEC_SEQ
TILES = TOKENS // P
PT = SEQ // P
RH, DK, DV = 4, 256, 512
VW = RH * DV
FH, KVH, DH = 8, 4, 128
KT = D // P
CW = 512
SUBS = 4
KS = KT // SUBS
NB3 = 384
EPS = 1e-6
NEG = -1.0e30
ROPE_BASE = 10000.0
BR = 32


def tables():
    f = np.float32
    pos = np.concatenate([np.arange(SEQ), PAST + np.tile(np.arange(DEC_SEQ), DEC_BATCH)]).astype(f)
    half = DK // 2
    inv = np.power(f(ROPE_BASE), -np.arange(half, dtype=f) / f(half)).astype(f)
    ang = (inv[:, None] * pos[None, :]).astype(f)
    lg = np.log1p(-np.exp2(-5.0 - np.arange(RH, dtype=np.float64)))
    i = np.arange(P)
    ks = DK ** -0.5
    diff = i[None, :] - i[:, None]
    same = (i[None, :] // DEC_SEQ) == (i[:, None] // DEC_SEQ)
    intra = np.stack([np.where(diff >= 0, np.exp(np.maximum(diff, 0) * g), 0) * ks for g in lg], 1)
    intra_s = np.stack([np.where((diff >= 0) & same, np.exp(np.maximum(diff, 0) * g), 0) * ks for g in lg], 1)
    ones = np.ones((P, 1, 1))
    qdec = ones * np.stack([np.exp((i + 1.0) * g) for g in lg], 0)[None]
    loc = i % DEC_SEQ
    par = (i // DEC_SEQ) % 2
    qdec_s = ones[..., None] * np.stack([[np.exp((loc + 1.0) * g) * (par == p) for p in range(2)] for g in lg], 0)[None]
    kdec = np.stack([np.exp((P - 1.0 - i) * g) * ks for g in lg], 1)
    kdec_s = np.stack([np.exp((DEC_SEQ - 1.0 - loc) * g)[:, None] * ks * (i[:, None] // DEC_SEQ == np.arange(DEC_BATCH)) for g in lg], 1)
    cdec = np.ones((P, 1)) * np.exp(P * lg)[None]
    cdec_s = np.ones((P, 1)) * np.exp(DEC_SEQ * lg)[None]
    sel_gate = np.zeros((P, 2, 4, P))
    for j in range(4):
        sel_gate[BR * j + DEC_BATCH, 0, j, :] = 1
        for b in range(DEC_BATCH):
            sel_gate[BR * j + b, 1, j, b * DEC_SEQ:(b + 1) * DEC_SEQ] = 1
    sel_bias = np.zeros((4, 4, BR))
    for j in range(4):
        sel_bias[j, j] = 1
    mask = np.where(i[None, :] <= i[:, None], 0, NEG)
    sel_head = np.zeros((FH, FH, P))
    for h in range(FH):
        sel_head[h, h] = 1
    row_j, row_g, row_q = i // 32, (i // DEC_SEQ) % 2, i % DEC_SEQ
    sel_group = np.zeros((FH, KVH, P))
    for kv in range(KVH):
        sel_group[2 * kv + row_g, kv, i] = 1
    mask_s, own_s = np.zeros((P, 2, P)), np.zeros((P, 2, P))
    for r in range(2):
        b = 4 * r + row_j
        ok = (i[None, :] // DEC_SEQ == b[:, None]) & (loc[None, :] <= row_q[:, None])
        mask_s[:, r] = np.where(ok, 0, NEG)
        own_s[:, r] = i[None, :] == (b * DEC_SEQ + row_q)[:, None]
    t = dict(ident=np.eye(P), cos=np.cos(ang), sin=np.sin(ang), intra=intra, intra_s=intra_s,
             qdec=qdec, qdec_s=qdec_s, kdec=kdec, kdec_s=kdec_s, cdec=cdec, cdec_s=cdec_s,
             sel_gate=sel_gate, sel_bias=sel_bias, mask=mask, sel_head=sel_head, sel_group=sel_group,
             mask_s=mask_s, own_s=own_s)
    return {k: np.ascontiguousarray(v.reshape(v.shape[0], -1), dtype=f) for k, v in t.items()}


class Program:

    def __init__(self, nc, ctx, dram, table):
        self.nc, self.ctx, self.dram, self.table = nc, ctx, dram, table
        self.raw = self.sb("w_raw", [P, 2, KS, CW])
        self.w_hi = self.sb("w_hi", [P, 2, KT, CW], F32R)
        self.w_lo = self.sb("w_lo", [P, 2, KT, CW], F32R)
        self.raw_landed = [self.sem(f"raw_landed{s}") for s in range(2)]
        self.raw_split = self.sem("raw_split")
        self.hi_done = self.sem("w_hi_done")
        self.ident = self.sb("ident", [P, P])
        self.passed = self.sem("passed")
        self.rstd = self.sb("rstd", [P, TILES])
        self.gn_g = self.sb("gn_g", [P, VW // D, KT])
        self.norm_g = self.sb("norm_g", [P, 3, KT])
        self.cT = self.sb("cT", [P, KT, BR])
        self.mod_a = [self.sb(f"mod_a{m}", [P, KT, DEC_BATCH + 1]) for m in range(3)]
        self.mod_b = [self.sb(f"mod_b{m}", [P, KT, DEC_BATCH + 1]) for m in range(3)]

    def sb(self, name, shape, dt=F32):
        return self.ctx.enter_context(self.nc.sbuf_tensor(name, shape, dt))

    def sem(self, name):
        return self.ctx.enter_context(self.nc.semaphore(name))


def stand(eng, pr):
    eng.sem_inc(pr.passed, 1)


def credit(pool, pr, sems):
    for n, sem in enumerate(sems):
        pool.dma_start(pr.dram["credit"][n:n + 1, :], pr.ident[0:1, :]).then_inc(sem, 16)


@contextmanager
def semaphores(nc, prefix):
    taken = []

    def sem(name):
        taken.append(nc.alloc_semaphore(prefix + name))
        return taken[-1]
    yield sem
    nc.clear_and_free_semaphores(taken)
    nc.all_engine_barrier()


class Chain:

    def __init__(self, eng, sem, start=0):
        self.eng, self.sem, self.n, self.base = eng, sem, start, 0

    def link(self, ins):
        self.n += 1
        ins.then_inc(self.sem, 1)
        self.eng.wait_ge(self.sem, self.base + self.n)



def load_chunk(pr, sp, weight, chunk, first):
    with sp.Fori(first, SUBS // 2) as j:
        load_parts(pr, sp, weight, chunk, j)


def load_parts(pr, sp, weight, chunk, j):
    for slot in range(2):
        sp.wait_ge(pr.raw_split, chunk * SUBS + 2 * j + slot + 1)
        for dst, src in weight(pr.raw[:, slot], (2 * j + slot) * KS * P):
            sp.dma_start(dst, src).then_inc(pr.raw_landed[slot], 16)


def columns(w, row0, c0):
    def pieces(raw, r):
        return [(raw[:, k], w[bass.ds(r + row0 + k * P, P), c0:c0 + CW]) for k in range(KS)]
    return pieces


def head_columns(w, h):
    def pieces(raw, r):
        rows = w[bass.ds(r, KS * P), :].rearrange("(k p) c -> p k c", p=P)
        return [(raw[:, :, 0:DK], rows[:, :, h * DK:(h + 1) * DK]), (raw[:, :, DK:2 * DK], rows[:, :, D + h * DK:D + (h + 1) * DK])]
    return pieces


def split_hi(pr, act, chunk, slot, sub):
    act.wait_ge(pr.raw_landed[sub % 2], chunk * (SUBS // 2) * 32 + (sub // 2 + 1) * 32)
    act.copy(pr.w_hi[:, slot, sub * KS:(sub + 1) * KS, :], pr.raw[:, sub % 2]).then_inc(pr.hi_done, 1)


def split_lo(pr, dve, chunk, slot, sub):
    dve.wait_ge(pr.hi_done, chunk * SUBS + sub + 1)
    dve.tensor_tensor(pr.w_lo[:, slot, sub * KS:(sub + 1) * KS, :], pr.raw[:, sub % 2],
                      pr.w_hi[:, slot, sub * KS:(sub + 1) * KS, :].bitcast(F32), ALU.subtract).then_inc(pr.raw_split, 1)



def modulation(pr, dve, m, t):
    t = t.rearrange("p (c j b) -> p j c b", c=4, j=4)
    for jj in range(2):
        dve.tensor_copy(pr.mod_b[m][:, 4 * jj:4 * jj + 4, :], t[:, jj, :, 0:DEC_BATCH + 1])
    for jj in range(2):
        for c in range(4):
            ins = dve.tensor_scalar(pr.mod_a[m][:, 4 * jj + c, :], t[:, 2 + jj, c, 0:DEC_BATCH + 1], 1.0, pr.norm_g[:, m, 4 * jj + c:4 * jj + c + 1], ALU.add, ALU.mult)
    return ins


def condition(pr, x, x_rows, weight):
    nc = pr.nc
    dr = pr.dram
    xv = x[:, :].rearrange("p (t d) -> p t d", t=TILES)
    with ExitStack() as ctx:
        sb = lambda n, s, dt=F32: ctx.enter_context(nc.sbuf_tensor(n, s, dt))
        ps = lambda n, s: ctx.enter_context(nc.psum_tensor(n, s, F32))
        sem = ctx.enter_context(semaphores(nc, "ada_"))
        c_rows = sb("c_rows", [BR, D])
        c_silu = sb("c_silu", [BR, D])
        w = sb("ada_w_sb", [P, 4, 4, CW])
        bias = sb("ada_bias", [P, CW])
        rows = sb("ada_rows", [P, CW])
        squares = sb("squares", [P, 2, D])
        stat = sb("ada_stat", [P, 3, TILES])
        ps_c = ps("ps_c", [P, 512])
        ps_ada = ps("ps_ada", [P, 512])
        ps_t = ps("ps_t", [P, 512])
        in_landed, c_ready, b_zero, b_landed = sem("in_landed"), sem("c_ready"), sem("b_zero"), sem("b_landed")
        s_silu, c_turned, cT_ready = sem("s_silu"), sem("c_turned"), sem("cT_ready")
        w_landed = [sem(f"ada_landed{i}") for i in range(4)]
        x_landed = [sem(f"x_landed{i}") for i in range(3)]
        w_read, rows_ready, turned = sem("ada_read"), sem("rows_ready"), sem("ada_turned")
        sq_done, me_done, rt_done = sem("sq_done"), sem("me_done"), sem("rt_done")
        block = ctx.enter_context(nc.Block())

        @block.sync
        def _(sp):
            sp.wait_ge(c_ready, 1)
            sp.dma_start(c_rows[0:DEC_BATCH], dr["c_sample"]).then_inc(in_landed, 16)
            sp.dma_start(c_rows[DEC_BATCH:DEC_BATCH + 1], dr["c_prompt"]).then_inc(in_landed, 16)
            sp.dma_start(pr.ident[:, :], pr.table["ident"]).then_inc(in_landed, 16)
            for k in range(KT):
                if k >= 4:
                    sp.wait_ge(w_read, k - 3)
                if k == 4:
                    load_parts(pr, sp, weight, 0, 0)
                sp.dma_start(w[:, k % 4], dr["a_ada_w"][k * P:(k + 1) * P, 0:4 * CW].rearrange("p (j c) -> p j c", j=4)).then_inc(w_landed[k % 4], 16)
            load_parts(pr, sp, weight, 0, 1)
            for t in range(TILES):
                sp.dma_start(xv[:, t], x_rows(t)).then_inc(x_landed[t // 3], 16)

        @block.gpsimd
        def _(pool):
            pool.memset(c_rows[:, :], 0.0).then_inc(c_ready, 1)
            pool.memset(bias[:, :], 0.0).then_inc(b_zero, 1)
            pool.wait_ge(b_zero, 1)
            for j in range(4):
                pool.dma_start(bias[BR * j:BR * j + 9, :], dr["a_ada_b"][0:1, j * CW:(j + 1) * CW].to_broadcast([9, CW])).then_inc(b_landed, 16)
            with nc.allow_non_contiguous_dma(reason="channel gains, once"):
                for m, g in enumerate(("a_norm_g", "kv_norm_g", "b_norm_g")):
                    pool.dma_start(pr.norm_g[:, m, :], dr[g].rearrange("a (k p) -> p (a k)", p=P)).then_inc(b_landed, 16)
                pool.dma_start(pr.gn_g[:, :, :], dr["a_gn_g"].rearrange("a (n k p) -> p (a n) k", p=P, k=KT)).then_inc(b_landed, 16)

        @block.scalar
        def _(act):
            act.wait_ge(in_landed, 48)
            act.activation(c_silu[:, :], c_rows[:, :], ACT.Silu).then_inc(s_silu, 1)
            for sub in range(SUBS):
                split_hi(pr, act, 0, 0, sub)
            for t in range(TILES):
                if t % 3 == 0:
                    act.wait_ge(x_landed[t // 3], 48)
                if t:
                    act.wait_ge(sq_done, t)
                act.activation(squares[:, t % 2], xv[:, t], ACT.Square, accum_out=stat[:, 0, t:t + 1]).then_inc(sq_done, 1)
            act.wait_ge(me_done, 1)
            act.activation(stat[:, 2, :], stat[:, 1, :], ACT.Sqrt).then_inc(rt_done, 1)

        @block.tensor
        def _(pe):
            pe.wait_ge(s_silu, 1)
            for k in range(KT):
                ins = pe.transpose(ps_c[:, k * BR:(k + 1) * BR], c_silu[:, k * P:(k + 1) * P], pr.ident[0:BR, 0:BR])
            ins.then_inc(c_turned, 1)
            pe.wait_ge(cT_ready, 1)
            for k in range(KT):
                pe.wait_ge(w_landed[k % 4], 16 * (k // 4 + 1))
                for j in range(4):
                    ins = pe.matmul(ps_ada[BR * j:BR * (j + 1), :], pr.cT[:, k, :], w[:, k % 4, j, :],
                                    start=k == 0, stop=k == KT - 1, tile_position=(0, BR * j), skip_group_check=True)
                ins.then_inc(w_read, 1)
            pe.wait_ge(rows_ready, 1)
            for c in range(4):
                ins = pe.transpose(ps_t[:, c * P:(c + 1) * P], rows[:, c * P:(c + 1) * P], pr.ident[:, :])
            ins.then_inc(turned, 1)

        @block.vector
        def _(dve):
            dve.sem_inc(pr.raw_split, 2)
            dve.wait_ge(c_turned, 1)
            dve.tensor_copy(pr.cT[:, :, :], ps_c[:, 0:KT * BR]).then_inc(cT_ready, 1)
            for sub in range(2):
                split_lo(pr, dve, 0, 0, sub)
            dve.wait_ge(b_landed, 8 * 16)
            dve.wait_ge(w_read, KT)
            dve.tensor_tensor(rows[:, :], ps_ada[:, :], bias[:, :], ALU.add).then_inc(rows_ready, 1)
            dve.wait_ge(turned, 1)
            modulation(pr, dve, 0, ps_t[:, :])
            for sub in range(2, SUBS):
                split_lo(pr, dve, 0, 0, sub)
            dve.wait_ge(sq_done, TILES)
            dve.tensor_scalar(stat[:, 1, :], stat[:, 0, :], 1.0 / D, EPS, ALU.mult, ALU.add).then_inc(me_done, 1)
            dve.wait_ge(rt_done, 1)
            dve.reciprocal(pr.rstd[:, :], stat[:, 2, :])


def project(pr, name, source, norm, mod, groups, chunk0, after, forget=False, gate_layer=None, residual=None, gain=None, sums=False, rows_here=None, side=False):
    nc, dr = pr.nc, pr.dram
    with ExitStack() as ctx:
        sb = lambda n, s, dt=F32: ctx.enter_context(nc.sbuf_tensor(f"{name}_{n}", s, dt))
        ps = lambda n, s: ctx.enter_context(nc.psum_tensor(f"{name}_{n}", s, F32))
        sem = ctx.enter_context(semaphores(nc, f"{name}_"))
        hT_hi = sb("hT_hi", [P, KT, TOKENS], F32R)
        hT_lo = sb("hT_lo", [P, KT, TOKENS], F32R)
        x = sb("x", [P, TILES * D]) if rows_here is None else rows_here
        xv = x[:, :].rearrange("p (t d) -> p t d", t=TILES)
        xs = sb("xs", [P, 2, TILES * P])
        ht = sb("ht", [P, 2, TOKENS])
        stat = sb("stat", [P, 3, TILES])
        small = sb("small", [P, 2, 4, 4])
        if sums:
            half_sums = sb("half_sums", [P, 2 * TILES])
        off = [0]

        def part_of_x(n):
            off[0] += n
            assert off[0] <= TILES * D
            return x[:, off[0] - n:off[0]]

        stage = part_of_x(4 * CW).rearrange("p (s c) -> p s c", s=4)
        ost = part_of_x(4 * CW).rearrange("p (s c) -> p s c", s=4)
        tmp = part_of_x(2 * CW).rearrange("p (s c) -> p s c", s=2)
        kinds = [g["kind"] for g in groups]
        if gain is not None:
            assert tuple(gain.shape) == (P, KT)
        if "rotary" in kinds:
            cs = part_of_x(2 * TOKENS).rearrange("p (s c) -> p s c", s=2)
        if "norm" in kinds:
            gains = part_of_x(2 * DH).rearrange("p (s c) -> p s c", s=2)
        if "residual" in kinds:
            gate = part_of_x(2 * D).rearrange("p (s c) -> p s c", s=2)
            rin = part_of_x(3 * CW).rearrange("p (s c) -> p s c", s=3)
        if forget:
            wf = sb("wf", [P, KT, FH])
            wf_hi = sb("wf_hi", [P, KT * FH + P - FH], F32R)
            wf_lo = sb("wf_lo", [P, KT * FH + P - FH], F32R)
            f_sb, f_abs, f_min = (part_of_x(TOKENS)[0:FH] for _ in range(3))
            f_bias = sb("f_bias", [FH, 1])
            f_own, z_ready, e_done = sem("f_own"), sem("z_ready"), sem("e_done")
            wf_landed = sem("wf_landed")
        turned_first = mod is not None or gain is not None
        early = [0, 1, 3, 4]
        AHEAD = 5
        ps_t = ps("ps_t", [P, 3, 512])
        ps_o = ps("ps_o", [P, AHEAD, 512])
        if side:
            side_w = [xs[:, :, :].rearrange("p a c -> p (a c)")[:, 0:4 * CW].rearrange("p (j c) -> p j c", j=4),
                      ht[:, :, :].rearrange("p a c -> p (a c)")[:, 0:4 * CW].rearrange("p (j c) -> p j c", j=4)]
            side_bias = part_of_x(3 * CW)[0:4].rearrange("p (r c) -> p r c", r=3)
            sel_bias = part_of_x(4 * BR)[0:4].rearrange("p (j b) -> p j b", j=4)
            side_c = part_of_x(4 * BR).rearrange("p (s e b) -> p s e b", s=2, e=2)
            sel_gate = sb("sel_gate_sb", [P, 2, 4, P])
            cs_flat = cs[:, :, :].rearrange("p s c -> p (s c)")
            side_rows = [tmp[:, 0, :], tmp[:, 1, :], cs_flat[:, 3 * CW:4 * CW]]
            gate_out = cs_flat[:, 0:3 * CW].rearrange("p (s c) -> p s c", s=3)
            side_landed = [sem(f"side_landed{e}") for e in range(2)]
            side_tab, side_c_ready, side_used, rows_read = sem("side_tab"), sem("side_c_ready"), sem("side_used"), sem("rows_read")
            g_done, g_read, side_turned, side_mod = sem("g_done"), sem("g_read"), sem("side_turned"), sem("side_mod")
            gate_stored = [sem(f"gate_stored{i}") for i in range(3)]
            ps_side = [ps_o[:, AHEAD - 1, :], ps_o[:, AHEAD - 2, :], ps_o[:, AHEAD - 1, :]]

        def turned_in(d):
            return ps_o[:, AHEAD - 3:AHEAD, :] if d == 1 else ps_t[:, :, :]

        def bank(g, t, first):
            if first and t < AHEAD:
                return t
            return t % 4 if g["kind"] == "rotary" else t % 3

        portions = [0, 1, 2, 4, 6, KT] if rows_here is None else []
        x_landed = [sem(f"x_landed{i}") for i in portions[1:]]
        tab_landed = sem("tab_landed")
        sq_done, me_done, rt_done = sem("sq_done"), sem("me_done"), sem("rt_done")
        xs_ready, turned, ht_ready = sem("xs_ready"), sem("turned"), sem("ht_ready")
        hhi_done, h_ready = sem("hhi_done"), sem("h_ready")
        out_done = sem("out_done")
        evac = sem("evac")
        posted = sem("posted")
        stage_read = sem("stage_read")
        stored = [sem(f"stored{s}") for s in range(4)]
        rin_landed = [sem(f"rin{s}") for s in range(3)]
        dve_own = sem("dve_own")
        root_in, root_out = sem("root_in"), sem("root_out")
        f_split, f_lo, f_out, f_stored = sem("f_split"), sem("f_lo"), sem("f_out"), sem("f_stored")
        n_tab = 2 * ("rotary" in kinds) + sum(k == "norm" for k in kinds) + ("residual" in kinds)

        c0 = chunk0
        tile0 = 0
        used = [0, 0, 0, 0]
        for g in groups:
            g["c0"], g["tile0"], g["used"] = c0, tile0, list(used)
            g["tiles"] = 12 if g["kind"] == "rotary" else TILES
            g["per_slot"] = [3, 3, 3, 3] if g["kind"] == "rotary" else [3, 3, 3, 0]
            c0 += 2 * g["pairs"]
            tile0 += 2 * g["pairs"] * g["tiles"]
            used = [u + 2 * g["pairs"] * n for u, n in zip(used, g["per_slot"])]
        post = 0
        for g in groups:
            g["post0"] = post
            if g["kind"] == "rotary":
                post += g["pairs"] * 12
            elif g["kind"] in ("norm", "residual"):
                post += g["pairs"] * 2 * TILES
        all_stored = [16 + 16 * u for u in used]

        def pairs(eng, g, body):
            i0 = 1 if g is groups[0] else 0
            i1 = g["pairs"] - 1 if g is groups[-1] and after is None else g["pairs"]
            if i0:
                for s in range(2):
                    body(0, s, i1 == 0 and s == 1, s == 0)
            if i1 > i0:
                with eng.Fori(i0, i1) as i:
                    for s in range(2):
                        body(i, s, False, False)
            for i in range(max(i0, i1), g["pairs"]):
                for s in range(2):
                    body(i, s, s == 1, False)

        block = ctx.enter_context(nc.Block())

        @block.sync
        def _(sp):
            for n, (a, b) in enumerate(zip(portions, portions[1:])):
                sp.dma_start(xv[:, :, a * P:b * P], source(a * P, (b - a) * P)).then_inc(x_landed[n], 16)
            if forget:
                with nc.allow_non_contiguous_dma(reason="eight columns"):
                    sp.dma_start(wf[:, :, :], dr["kv_w"][:, 2 * CW:2 * CW + FH].rearrange("(k p) c -> p k c", p=P)).then_inc(wf_landed, 16)
                sp.dma_start(f_bias[:, :], dr["kv_fb"]).then_inc(wf_landed, 16)
            chunks = [w for g in groups for w in g["weights"]][1:] + ([after] if after else [])
            load_parts(pr, sp, chunks[0], chunk0 + 1, 0)
            sp.wait_ge(h_ready, KT)
            if "rotary" in kinds:
                sp.dma_start(cs[:, 0], pr.table["cos"]).then_inc(tab_landed, 16)
                sp.dma_start(cs[:, 1], pr.table["sin"]).then_inc(tab_landed, 16)
            for n, g in enumerate(g for g in groups if g["kind"] == "norm"):
                sp.dma_start(gains[:, n], g["gain"].to_broadcast([P, DH])).then_inc(tab_landed, 16)
            if "residual" in kinds:
                sp.dma_start(gate[:, :, :], dr["gate"][:, gate_layer]).then_inc(tab_landed, 16)

            def side_load(c):
                for e in range(2):
                    k = 2 * (c % 4) + e
                    halves = [(dr["a_ada_w"], 4 * CW), (dr["b_ada_w"], 4 * CW)] if c < 4 else [(dr[("kv_ada_w", "b_ada_w")[c // 4 - 1]], h * 2 * CW) for h in range(2)]
                    for h, (w, c0) in enumerate(halves):
                        sp.dma_start(side_w[e][:, 2 * h:2 * h + 2], w[k * P:(k + 1) * P, c0:c0 + 2 * CW].rearrange("p (j c) -> p j c", j=2)).then_inc(side_landed[e], 16)

            if side:
                side_load(0)
                sp.dma_start(sel_bias[:, :, :], pr.table["sel_bias"].rearrange("p (j b) -> p j b", j=4)).then_inc(side_tab, 16)
                for m, rows in (("a", slice(0, 2)), ("b", slice(2, 4))):
                    sp.dma_start(side_bias[rows, 0, :], dr[f"{m}_ada_b"][0:1, 4 * CW:6 * CW].rearrange("o (j c) -> (o j) c", c=CW)).then_inc(side_tab, 16)
                for r, m in ((1, "kv"), (2, "b")):
                    sp.dma_start(side_bias[:, r, :], dr[f"{m}_ada_b"][0:1, 0:4 * CW].rearrange("o (j c) -> (o j) c", c=CW)).then_inc(side_tab, 16)
                sp.dma_start(sel_gate[:, :, :, :], pr.table["sel_gate"]).then_inc(side_tab, 16)
            for n, w in enumerate(chunks):
                load_chunk(pr, sp, w, chunk0 + n + 1, first=int(n == 0))
                if side and n + 1 < len(chunks):
                    sp.wait_ge(side_used, 2 * (n + 1))
                    side_load(n + 1)

        @block.gpsimd
        def _(pool):
            if norm:
                for d in range(KT):
                    if d in portions:
                        pool.wait_ge(x_landed[portions.index(d)], 16)
                    if d >= 2:
                        pool.wait_ge(turned, d - 1)
                    pool.tensor_tensor(xs[:, d % 2].rearrange("p (t c) -> p t c", t=TILES), xv[:, :, d * P:(d + 1) * P],
                                       pr.rstd[:, :].rearrange("p (t o) -> p t o", o=1).to_broadcast([P, TILES, P]), ALU.mult).then_inc(xs_ready, 1)
            credit(pool, pr, stored)
            pool.wait_ge(h_ready, KT)
            for g in groups:
                def body(i, s, stop, head, g=g):
                    base = g["tile0"] + (2 * i + s) * g["tiles"]
                    kind = "copy" if g.get("plain") == s else g["kind"]
                    if forget and s == 1:
                        pool.wait_ge(f_out, 1)
                        pool.dma_start(dr["logf"], f_sb[:, :]).then_inc(f_stored, 16)
                    ready = evac if kind in ("copy", "silu") else posted
                    if g["kind"] == "residual":
                        def load(t):
                            n = base + t
                            pool.wait_ge(posted, n + 1)
                            pool.dma_start(rin[:, t % 3], residual(2 * i + s, t)).then_inc(rin_landed[t % 3], 16)
                        for t in range(3):
                            load(t)
                    if g["kind"] == "rotary":
                        for u in range(6):
                            pool.wait_ge(posted, g["tile0"] // 2 + (2 * i + s) * 6 + u + 1)
                            for half in range(2):
                                m = 2 * u + half
                                pool.dma_start(g["store"](2 * i + s, m), ost[:, m % 4, 0:NB3]).then_inc(stored[m % 4], 16)
                    else:
                        credit = {"copy": 4, "silu": 4, "residual": 3, "norm": 0}[kind]
                        if ready is posted:
                            first = g["post0"]
                            base2 = first + (2 * i + s) * g["tiles"]
                        else:
                            base2 = base
                        for t in range(TILES):
                            pool.wait_ge(ready, credit + base2 + t + 1)
                            pool.dma_start(g["store"](2 * i + s, t), ost[:, t % 3, :]).then_inc(stored[t % 3], 16)
                            if g["kind"] == "residual" and t + 3 < TILES:
                                load(t + 3)
                pairs(pool, g, body)
                if side and g is groups[1]:
                    for n in range(8):
                        kind, j = n // 4, n % 4
                        pool.wait_ge(g_read, n + 1)
                        pool.dma_start(dr["gate"][:, j // 2, kind, (j % 2) * CW:(j % 2 + 1) * CW], gate_out[:, n % 3, :]).then_inc(gate_stored[n % 3], 16)
            if forget:
                pool.wait_ge(f_stored, 16)
            if side:
                for n in range(3):
                    pool.wait_ge(gate_stored[n], 16 * len(range(n, 8, 3)))
            for s in range(4):
                pool.wait_ge(stored[s], all_stored[s])

        @block.scalar
        def _(act):
            act.sem_inc(evac, 4)
            for d in range(KT):
                if mod is not None or gain is not None:
                    act.wait_ge(ht_ready, d + 1)
                    act.copy(hT_hi[:, d, :], ht[:, d % 2, :]).then_inc(hhi_done, 1)
                else:
                    act.wait_ge(turned, d + 1)
                    act.copy(hT_hi[:, d, :].rearrange("p (b c) -> p b c", b=3), turned_in(d)[:, :, 0:NB3]).then_inc(hhi_done, 1)
            act.wait_ge(h_ready, KT)
            if forget:
                act.wait_ge(f_split, 1)
                act.copy(wf_hi[:, 0:KT * FH], wf[:, :, :].rearrange("p k f -> p (k f)")).then_inc(hhi_done, 1)

            sums_done = [0]

            def squares(n):
                act.wait_ge(posted, n + 4)
                if n:
                    act.wait_ge(sq_done, n)
                act.activation(ht[:, 0, 0:CW], ost[:, n % 3, :], ACT.Square, accum_out=half_sums[:, n:n + 1]).then_inc(sq_done, 1)

            for g in groups:
                def body(i, s, stop, head, g=g):
                    c = g["c0"] + 2 * i + s
                    base = g["tile0"] + (2 * i + s) * g["tiles"]
                    k = "copy" if g.get("plain") == s else g["kind"]
                    seen, roots = [0, 0, 0, 0], []
                    if forget and s == 1:
                        act.wait_ge(z_ready, 1)
                        act.activation(f_abs[:, :], f_abs[:, :], ACT.Exp, scale=-1.0).then_inc(e_done, 1)
                        act.wait_ge(e_done, 1)
                        act.activation(f_abs[:, :], f_abs[:, :], ACT.Ln, bias=1.0).then_inc(e_done, 1)
                    if side:
                        if not (isinstance(i, int) and g is groups[0]):
                            act.wait_ge(side_used, 2 * c - 2)
                        act.copy(side_c[:, s, :, :], pr.cT[:, bass.ds(4 * i + 2 * s, 2), :]).then_inc(side_c_ready, 1)
                    for t in range(g["tiles"]):
                        slot = t % 4 if k == "rotary" else t % 3
                        width = NB3 if k == "rotary" else CW
                        act.wait_ge(out_done, base + t + 1)
                        if k in ("copy", "silu"):
                            act.wait_ge(stored[slot], 16 * (g["used"][slot] + 1 + seen[slot]) + (2 * i + s) * 16 * g["per_slot"][slot])
                            seen[slot] += 1
                            act.activation(ost[:, slot, :], ps_o[:, bank(g, t, head), :], ACT.Silu if k == "silu" else ACT.Copy).then_inc(evac, 1)
                        else:
                            if k == "rotary":
                                act.wait_ge(stage_read, (2 * i + s) * 6 + t // 2 + 1)
                            else:
                                act.wait_ge(stage_read, g["post0"] + (2 * i + s) * TILES + t + 1)
                            act.copy(stage[:, slot, 0:width], ps_o[:, bank(g, t, head), 0:width]).then_inc(evac, 1)
                        if sums:
                            squared = s * TILES + t if not head or t >= AHEAD else t - 2
                            for n in range(sums_done[0], squared):
                                squares(n)
                            sums_done[0] = max(sums_done[0], squared)
                        if head and t in early:
                            split_hi(pr, act, c + 1, 1 - s, early.index(t))
                        if k == "norm":
                            roots.append(g["post0"] + (2 * i + s) * TILES + t)
                            while len(roots) > (2 if head and t < g["tiles"] - 1 else 0):
                                act.wait_ge(root_in, roots.pop(0) + 1)
                                act.activation(small[:, 0, 2, :], small[:, 0, 1, :], ACT.Sqrt).then_inc(root_out, 1)
                        if not head and t % 2 and t < 2 * SUBS and not stop:
                            split_hi(pr, act, c + 1, 1 - s, t // 2)
                pairs(act, g, body)
            if sums:
                squares(2 * TILES - 1)
                act.wait_ge(me_done, 1)
                act.activation(stat[:, 2, :], stat[:, 1, :], ACT.Sqrt).then_inc(rt_done, 1)

        @block.tensor
        def _(pe):
            def turn(d):
                dst = turned_in(d)
                if norm:
                    pe.wait_ge(xs_ready, d + 1)
                elif d in portions:
                    pe.wait_ge(x_landed[portions.index(d)], 16)
                if d >= 2:
                    pe.wait_ge(ht_ready if turned_first else h_ready, d - int(d == 2))
                for t in range(TILES):
                    src = xs[:, d % 2, t * P:(t + 1) * P] if norm else xv[:, t, d * P:(d + 1) * P]
                    ins = pe.transpose(dst[:, t // 3, (t % 3) * P:(t % 3 + 1) * P], src, pr.ident[:, :])
                ins.then_inc(turned, 1)

            def products(g, s, t, k, first):
                if g["kind"] == "rotary":
                    part, n, half = t // 6, t % 6 // 2, t % 2
                    w0 = part * DK + half * P
                    for m, (w, h) in enumerate(((pr.w_hi, hT_hi), (pr.w_hi, hT_lo), (pr.w_lo, hT_hi))):
                        ins = pe.matmul(ps_o[:, bank(g, t, first), 0:NB3], w[:, s, k, w0:w0 + P], h[:, k, n * NB3:(n + 1) * NB3],
                                        start=k + m == 0, stop=k == KT - 1 and m == 2)
                else:
                    for m, (h, w) in enumerate(((hT_hi, pr.w_hi), (hT_hi, pr.w_lo), (hT_lo, pr.w_hi))):
                        ins = pe.matmul(ps_o[:, bank(g, t, first), :], h[:, k, t * P:(t + 1) * P], w[:, s, k, :],
                                        start=k + m == 0, stop=k == KT - 1 and m == 2)
                if k == KT - 1:
                    ins.then_inc(out_done, 1)

            turn(0)
            turn(1)
            pe.wait_ge(pr.raw_split, SUBS * chunk0 + SUBS + 2)
            for d in range(KT):
                if d + 2 < KT:
                    turn(d + 2)
                if d == 0:
                    pe.wait_ge(ht_ready if turned_first else h_ready, 2)
                pe.wait_ge(h_ready, d + 1)
                for t in range(AHEAD):
                    products(groups[0], 0, t, d, True)
            if forget:
                pe.wait_ge(f_lo, 1)
                for n in range(3):
                    for k in range(KT):
                        for m, (a, b) in enumerate(((wf_hi, hT_hi), (wf_lo, hT_hi), (wf_hi, hT_lo))):
                            ins = pe.matmul(ps_t[:, n, 0:NB3], a[:, k * FH:k * FH + P], b[:, k, n * NB3:(n + 1) * NB3], start=k + m == 0, stop=k == KT - 1 and m == 2)
                ins.then_inc(f_lo, 1)

            def side_start(r):
                if r == 0:
                    pe.wait_ge(side_tab, 6 * 16)
                elif r == 1:
                    pe.wait_ge(evac, 4 + groups[1]["tile0"])
                else:
                    pe.wait_ge(rows_read, r - 1)
                for j in range(4):
                    pe.matmul(ps_side[r][BR * j:BR * (j + 1), :], sel_bias[:, j, :], side_bias[:, r, :],
                              start=True, stop=True, tile_position=(0, BR * j), skip_group_check=True)

            def side_steps(r, c, s):
                pe.wait_ge(side_c_ready, c + 1)
                for e in range(2):
                    pe.wait_ge(side_landed[e], 32 * c + 32)
                    for j in range(4):
                        ins = pe.matmul(ps_side[r][BR * j:BR * (j + 1), :], side_c[:, s, e, :], side_w[e][:, j, :],
                                        start=False, stop=True, tile_position=(0, BR * j), skip_group_check=True)
                    ins.then_inc(side_used, 1)

            def side_end(r):
                pe.wait_ge(rows_read, r + 1)
                if r == 0:
                    for n in range(8):
                        if n >= 2:
                            pe.wait_ge(g_read, n - 1)
                        pe.matmul(ps_t[:, n % 2, :], sel_gate[:, n // 4, n % 4, :], side_rows[0], start=True, stop=True).then_inc(g_done, 1)
                else:
                    if r == 2:
                        pe.wait_ge(side_mod, 1)
                    for c in range(4):
                        ins = pe.transpose(ps_t[:, 2, c * P:(c + 1) * P], side_rows[r][:, c * P:(c + 1) * P], pr.ident[:, :])
                    ins.then_inc(side_turned, 1)

            for r, g in enumerate(groups):
                if side and r:
                    side_start(r)

                def body(i, s, stop, head, g=g, r=r):
                    c = g["c0"] + 2 * i + s
                    base = g["tile0"] + (2 * i + s) * g["tiles"]
                    pe.wait_ge(pr.raw_split, SUBS * c + SUBS + 2)
                    for t in range(AHEAD if head else 0, g["tiles"]):
                        pe.wait_ge(evac, base + t + (1 if g["kind"] == "rotary" else 2))
                        for k in range(KT):
                            products(g, s, t, k, head)
                        if side and t == g["tiles"] - 4:
                            if head:
                                side_start(0)
                            side_steps(r, c, s)
                pairs(pe, g, body)
                if side and r:
                    side_end(r - 1)
            if side:
                side_end(2)

        @block.vector
        def _(dve):
            chain = Chain(dve, dve_own)
            if kinds[0] == "rotary":
                dve.sem_inc(stage_read, 2)
            elif kinds[0] in ("norm", "residual"):
                dve.sem_inc(stage_read, 3)
            if "residual" in kinds:
                dve.sem_inc(posted, 3)

            def modulated(d):
                z, src = ht[:, d % 2, :], turned_in(d)
                dve.wait_ge(turned, d + 1)
                if d >= 2:
                    dve.wait_ge(h_ready, d - 1)
                if mod is None:
                    dve.tensor_scalar(z.rearrange("p (a c) -> p a c", a=3), src[:, :, 0:NB3], gain[:, d:d + 1], None, ALU.mult).then_inc(ht_ready, 1)
                    return
                A, B = pr.mod_a[mod], pr.mod_b[mod]
                smp = z[:, SEQ:TOKENS].rearrange("p (b s) -> p b s", b=DEC_BATCH)
                per = [m[:, d, 0:DEC_BATCH].rearrange("p (b o) -> p b o", o=1).to_broadcast([P, DEC_BATCH, DEC_SEQ]) for m in (A, B)]
                dve.tensor_tensor(smp, src[:, 2, SEQ - 2 * NB3:NB3].rearrange("p (b s) -> p b s", b=DEC_BATCH), per[0], ALU.mult).then_inc(dve_own, 1)
                dve.tensor_scalar(z[:, 0:2 * NB3].rearrange("p (a c) -> p a c", a=2), src[:, 0:2, 0:NB3], A[:, d, DEC_BATCH:], B[:, d, DEC_BATCH:], ALU.mult, ALU.add)
                dve.tensor_scalar(z[:, 2 * NB3:SEQ], src[:, 2, 0:SEQ - 2 * NB3], A[:, d, DEC_BATCH:], B[:, d, DEC_BATCH:], ALU.mult, ALU.add)
                dve.wait_ge(dve_own, d + 1)
                dve.tensor_tensor(smp, smp, per[1], ALU.add).then_inc(ht_ready, 1)

            if turned_first:
                modulated(0)
            for d in range(KT):
                if turned_first and d + 1 < KT:
                    modulated(d + 1)
                dve.wait_ge(hhi_done, d + 1)
                hi, lo = hT_hi[:, d, :].bitcast(F32), hT_lo[:, d, :]
                if turned_first:
                    dve.tensor_tensor(lo, ht[:, d % 2, :], hi, ALU.subtract).then_inc(h_ready, 1)
                else:
                    v3 = lambda a: a.rearrange("p (b c) -> p b c", b=3)
                    dve.tensor_tensor(v3(lo), turned_in(d)[:, :, 0:NB3], v3(hi), ALU.subtract).then_inc(h_ready, 1)
            chain.n = KT if mod is not None else 0
            if forget:
                chain.link(dve.memset(wf_hi[:, :].bitcast(F32), 0.0))
                chain.link(dve.memset(wf_lo[:, :].bitcast(F32), 0.0))
                dve.wait_ge(wf_landed, 32)
                dve.sem_inc(f_split, 1)
                dve.wait_ge(hhi_done, KT + 1)
                dve.tensor_tensor(wf_lo[:, 0:KT * FH], wf[:, :, :].rearrange("p k f -> p (k f)"), wf_hi[:, 0:KT * FH].bitcast(F32), ALU.subtract).then_inc(f_lo, 1)

            def forget_gates():
                fc = Chain(dve, f_own)
                dve.wait_ge(f_lo, 2)
                fc.link(dve.tensor_copy(f_sb[:, :].rearrange("p (a c) -> p a c", a=3), ps_t[0:FH, :, 0:NB3]))
                fc.link(dve.tensor_scalar(f_sb[:, :], f_sb[:, :], f_bias[:, 0:1], None, ALU.add))
                fc.link(dve.tensor_scalar(f_abs[:, :], f_sb[:, :], -1.0, None, ALU.mult))
                dve.tensor_tensor(f_abs[:, :], f_abs[:, :], f_sb[:, :], ALU.max).then_inc(z_ready, 1)
                fc.link(dve.tensor_scalar(f_min[:, :], f_sb[:, :], 0.0, None, ALU.min))
                dve.wait_ge(e_done, 2)
                dve.tensor_tensor(f_sb[:, :], f_min[:, :], f_abs[:, :], ALU.subtract).then_inc(f_out, 1)

            if n_tab:
                dve.wait_ge(tab_landed, 16 * n_tab)
            norm_no = 0
            for g in groups:
                k = g["kind"]
                per_chunk = {"rotary": 36, "norm": 5 * TILES, "residual": TILES, "copy": 0, "silu": 0}[k]
                start = chain.n

                def body(i, s, stop, head, g=g, k=k, per_chunk=per_chunk, start=start, nn=norm_no):
                    if g.get("plain") == s:
                        k, per_chunk = "copy", 0
                    c = g["c0"] + 2 * i + s
                    base = g["tile0"] + (2 * i + s) * g["tiles"]
                    chain.base = (2 * i + s) * per_chunk
                    chain.n = start
                    seen = [0, 0, 0, 0]

                    def free(slot):
                        dve.wait_ge(stored[slot], 16 * (g["used"][slot] + 1 + seen[slot]) + (2 * i + s) * 16 * g["per_slot"][slot])
                        seen[slot] += 1
                    if forget and s == 1:
                        forget_gates()
                    for t in range(g["tiles"]):
                        slot = t % 3
                        if head and t in early:
                            split_lo(pr, dve, c + 1, 1 - s, early.index(t))
                        if k == "rotary" and t % 2:
                            n = t % 6 // 2
                            dve.wait_ge(evac, 4 + base + t + 1)
                            x1, x2 = stage[:, (t - 1) % 4, 0:NB3], stage[:, t % 4, 0:NB3]
                            co, si = cs[:, 0, n * NB3:(n + 1) * NB3], cs[:, 1, n * NB3:(n + 1) * NB3]
                            a, b = tmp[:, 0, 0:NB3], tmp[:, 1, 0:NB3]
                            free((t - 1) % 4)
                            free(t % 4)
                            chain.link(dve.tensor_tensor(a, x1, co, ALU.mult))
                            chain.link(dve.tensor_tensor(b, x2, si, ALU.mult))
                            chain.link(dve.tensor_tensor(ost[:, (t - 1) % 4, 0:NB3], a, b, ALU.subtract))
                            chain.link(dve.tensor_tensor(a, x2, co, ALU.mult))
                            chain.link(dve.tensor_tensor(b, x1, si, ALU.mult))
                            dve.sem_inc(stage_read, 1)
                            chain.link(dve.tensor_tensor(ost[:, t % 4, 0:NB3], a, b, ALU.add))
                            dve.sem_inc(posted, 1)
                        elif k == "norm":
                            st = stage[:, slot, :].rearrange("p (h c) -> p h c", h=4)
                            os = ost[:, slot, :].rearrange("p (h c) -> p h c", h=4)
                            dve.wait_ge(evac, 4 + base + t + 1)
                            free(slot)
                            chain.link(dve.tensor_tensor(tmp[:, 0, :], stage[:, slot, :], stage[:, slot, :], ALU.mult))
                            chain.link(dve.tensor_reduce(small[:, 0, 0, :], tmp[:, 0, :].rearrange("p (h c) -> p h c", h=4), AX.X, ALU.add))
                            n = g["post0"] + (2 * i + s) * TILES + t
                            dve.tensor_scalar(small[:, 0, 1, :], small[:, 0, 0, :], 1.0 / DH, EPS, ALU.mult, ALU.add).then_inc(root_in, 1)
                            dve.wait_ge(root_out, n + 1)
                            chain.link(dve.reciprocal(small[:, 0, 3, :], small[:, 0, 2, :]))
                            r = small[:, 0, 3, :].rearrange("p (h o) -> p h o", o=1).to_broadcast([P, 4, DH])
                            gb = gains[:, nn:nn + 1, :].to_broadcast([P, 4, DH])
                            t4 = tmp[:, 1, :].rearrange("p (h c) -> p h c", h=4)
                            chain.link(dve.tensor_tensor(t4, st, r, ALU.mult))
                            dve.sem_inc(stage_read, 1)
                            if g["scale"] != 1.0:
                                chain.link(dve.scalar_tensor_tensor(os, t4, g["scale"], gb, ALU.mult, ALU.mult))
                            else:
                                chain.link(dve.tensor_tensor(os, t4, gb, ALU.mult))
                            dve.sem_inc(posted, 1)
                        elif k == "residual":
                            dve.wait_ge(evac, 4 + base + t + 1)
                            free(slot)
                            col = g["col"](i, s)
                            dve.wait_ge(posted, base + max(t, 1) + 2)
                            if sums and s * TILES + t >= 3:
                                dve.wait_ge(sq_done, s * TILES + t - 2)
                            chain.link(dve.tensor_tensor(tmp[:, t % 2, :], stage[:, slot, :], gate[:, int(t == PT), col:col + CW], ALU.mult))
                            dve.sem_inc(stage_read, 1)
                            dve.wait_ge(rin_landed[t % 3], 16 * (3 * (2 * i + s) + t // 3 + 1))
                            dve.tensor_tensor(ost[:, slot, :], tmp[:, t % 2, :], rin[:, t % 3], ALU.add).then_inc(posted, 1)
                        if not head and t % 2 and t < 2 * SUBS and not stop:
                            split_lo(pr, dve, c + 1, 1 - s, t // 2)
                    assert chain.n - start == per_chunk, (chain.n, start)
                norm_no += k == "norm"
                pairs(dve, g, body)
                if side:
                    r = groups.index(g)
                    dve.wait_ge(side_used, 8 * (r + 1))
                    dve.tensor_copy(side_rows[r], ps_side[r]).then_inc(rows_read, 1)
                    if r == 1:
                        for n in range(8):
                            dve.wait_ge(g_done, n + 1)
                            if n >= 3:
                                dve.wait_ge(gate_stored[n % 3], 16 * (n // 3))
                            dve.tensor_copy(gate_out[:, n % 3, :], ps_t[:, n % 2, :]).then_inc(g_read, 1)
                    if r == 2:
                        for m in range(1, 3):
                            dve.wait_ge(side_turned, m)
                            modulation(pr, dve, m, ps_t[:, 2, :]).then_inc(side_mod, 1)
                chain.n = start + 2 * g["pairs"] * per_chunk
                chain.base = 0
            if sums:
                dve.wait_ge(sq_done, 2 * TILES)
                chain.link(dve.tensor_tensor(stat[:, 0, :], half_sums[:, 0:TILES], half_sums[:, TILES:2 * TILES], ALU.add))
                dve.tensor_scalar(stat[:, 1, :], stat[:, 0, :], 1.0 / D, EPS, ALU.mult, ALU.add).then_inc(me_done, 1)
                dve.wait_ge(rt_done, 1)
                dve.reciprocal(pr.rstd[:, :], stat[:, 2, :])


def retention(pr):
    nc, dr = pr.nc, pr.dram
    NH2 = DK // P
    with ExitStack() as ctx:
        sb = lambda n, s, dt=F32: ctx.enter_context(nc.sbuf_tensor(f"ret_{n}", s, dt))
        ps = lambda n, s: ctx.enter_context(nc.psum_tensor(f"ret_{n}", s, F32))
        sem = ctx.enter_context(semaphores(nc, "ret_"))
        qT = sb("qT", [P, NH2, TOKENS])
        kT = sb("kT", [P, NH2, TOKENS])
        v = sb("v", [P, TILES, DV])
        g = sb("g", [P, TILES, DV])
        intra = sb("intra", [P, 2, RH, P])
        qdec = sb("qdec", [P, RH, 3, P])
        kdec = sb("kdec", [P, RH, 1 + DEC_BATCH])
        cdec = sb("cdec", [P, 2, RH])
        s_in = sb("s_in", [P, 2, P])
        k_tok = sb("k_tok", [P, 2, DK])
        k_str = sb("k_str", [P, 2, DK])
        q_dec = sb("q_dec", [P, 2, NH2, P])
        state = sb("state", [P, 2, NH2, DV])
        r_in = sb("r_in", [P, 2, 4, NH2, DV])
        normed = sb("normed", [P, 2, DV])
        ost = sb("ost", [P, 2, DV])
        st6 = sb("st6", [P, 2, 6])
        mv = sb("mv", [P, 2, 2])
        sc = sb("sc", [P, 2, 4])
        ps_s = ps("ps_s", [P, 2, 512])
        ps_o = ps("ps_o", [P, 2, 512])
        ps_u = ps("ps_u", [P, 2, 2, 512])
        FIRST = 2
        q0_in, v0_in = sem("q0_in"), sem("v0_in")
        tabs, q_in, v_in, vs_in, g_in = sem("tabs"), sem("q_in"), sem("v_in"), sem("vs_in"), sem("g_in")
        r_landed = [sem(f"r_landed{i}") for i in range(2)]
        r_stored = [sem(f"r_stored{i}") for i in range(2)]
        ost_stored = [sem(f"ost_stored{i}") for i in range(2)]
        p_stored = sem("p_stored")
        scored, decayed, q_ready = sem("scored"), sem("decayed"), sem("q_ready")
        upd, state_new, str_k, o_done = sem("upd"), sem("state_new"), sem("str_k"), sem("o_done")
        own, var, root, scaled, n_done, gated = sem("own"), sem("var"), sem("root"), sem("scaled"), sem("n_done"), sem("gated")
        PAIRS = DEC_BATCH
        U = PT + PAIRS
        block = ctx.enter_context(nc.Block())

        @block.sync
        def _(sp):
            portions = (slice(0, FIRST), slice(FIRST, TILES))

            def load_qk(h, part):
                c, landed = slice(portions[part].start * P, portions[part].stop * P), (q0_in, q_in)[part]
                sp.dma_start(kT[:, :, c], dr["qkT"][bass.ds(h * 4 + 2, 2), :, c].rearrange("a p t -> p a t")).then_inc(landed, 16)
                sp.dma_start(qT[:, :, c], dr["qkT"][bass.ds(h * 4, 2), :, c].rearrange("a p t -> p a t")).then_inc(landed, 16)

            def load_v(h, part):
                a, b = portions[part].start, min(portions[part].stop, PT)
                sp.dma_start(v[:, a:b, :], dr["v"][a * P:b * P, bass.ds(h * DV, DV)].rearrange("(t p) c -> p t c", p=P)).then_inc((v0_in, v_in)[part], 16)

            def load_rest(h):
                sp.wait_ge(gated, h * TILES + 1)
                sp.dma_start(g[:, :, :], dr["g"][:, bass.ds(h * DV, DV)].rearrange("(t p) c -> p t c", p=P)).then_inc(g_in, 16)
                sp.wait_ge(upd, h * U + 1)
                sp.dma_start(v[:, PT, :], dr["v"][SEQ:TOKENS, bass.ds(h * DV, DV)]).then_inc(vs_in, 16)
                for par in range(2):
                    sp.wait_ge(r_stored[par], h * 64 + 64)
                    for j in range(4):
                        sp.dma_start(r_in[:, par, j], dr["state_ret"][2 * j + par, bass.ds(h, 1)].rearrange("o (a p) c -> p (o a) c", p=P)).then_inc(r_landed[par], 16)

            load_qk(0, 0)
            load_v(0, 0)
            sp.dma_start(intra[:, 0], pr.table["intra"]).then_inc(tabs, 16)
            sp.dma_start(intra[:, 1], pr.table["intra_s"]).then_inc(tabs, 16)
            sp.dma_start(qdec[:, :, 0], pr.table["qdec"]).then_inc(tabs, 16)
            sp.dma_start(qdec[:, :, 1:3], pr.table["qdec_s"]).then_inc(tabs, 16)
            with nc.allow_non_contiguous_dma(reason="small tables, once"):
                sp.dma_start(kdec[:, :, 0:1], pr.table["kdec"]).then_inc(tabs, 16)
                sp.dma_start(kdec[:, :, 1:], pr.table["kdec_s"]).then_inc(tabs, 16)
            sp.dma_start(cdec[:, 0], pr.table["cdec"]).then_inc(tabs, 16)
            sp.dma_start(cdec[:, 1], pr.table["cdec_s"]).then_inc(tabs, 16)
            load_qk(0, 1)
            load_v(0, 1)
            load_rest(0)
            with sp.Fori(1, RH) as h:
                sp.wait_ge(scored, h * TILES + 1)
                sp.wait_ge(q_ready, h * TILES + 1)
                for part in range(2):
                    load_qk(h, part)
                sp.wait_ge(o_done, h * TILES + 1)
                for part in range(2):
                    load_v(h, part)
                load_rest(h)

        @block.tensor
        def _(pe):
            pe.sem_inc(o_done, 1)
            pe.sem_inc(upd, 1)
            pe.sem_inc(scored, 1)
            with pe.Fori(0, RH) as h:
                def scores(c):
                    pe.wait_ge(decayed, h * TILES + max(c, 1) + 1)
                    if c in (0, FIRST):
                        pe.wait_ge(q_in if c else q0_in, h * 32 + 32)
                    for a in range(NH2):
                        pe.matmul(ps_s[:, c % 2, 0:P], kT[:, a, c * P:(c + 1) * P], qT[:, a, c * P:(c + 1) * P], start=a == 0, stop=a == NH2 - 1)
                    for a in range(NH2):
                        ins = pe.transpose(ps_s[:, c % 2, P + a * P:P + (a + 1) * P], kT[:, a, c * P:(c + 1) * P], pr.ident[:, :])
                    ins.then_inc(scored, 1)

                def output(c):
                    o = ps_o[:, c % 2, :]
                    pe.wait_ge(n_done, h * TILES + max(c, 1) + 1)
                    pe.wait_ge(decayed, h * TILES + c + 3)
                    ins = pe.matmul(o, s_in[:, c % 2, :], v[:, c, :], start=True, stop=c == 0)
                    if c:
                        pe.wait_ge(q_ready, h * TILES + c + 2)
                        pe.wait_ge(state_new, h * U + c + 1)
                        for a in range(NH2):
                            ins = pe.matmul(o, q_dec[:, c % 2, a, :], state[:, (c - 1) % 2, a, :], start=False, stop=a == NH2 - 1)
                    ins.then_inc(o_done, 1)

                def update(n, keys):
                    pe.wait_ge(state_new, h * U + max(n, 1))
                    c = min(n, PT)
                    for a in range(NH2):
                        ins = pe.matmul(ps_u[:, n % 2, a, :], keys[:, a * P:(a + 1) * P], v[:, c, :], start=True, stop=True)
                    ins.then_inc(upd, 1)

                scores(0)
                for c in range(PT):
                    scores(c + 1)
                    if c in (0, FIRST):
                        pe.wait_ge(v_in if c else v0_in, h * 16 + 16)
                    pe.wait_ge(decayed, h * TILES + c + 3)
                    update(c, k_tok[:, c % 2, :])
                    output(c)
                pe.wait_ge(vs_in, h * 16 + 16)
                for m in range(2):
                    pe.wait_ge(str_k, h * PAIRS + m + 1)
                    update(PT + m, k_str[:, m % 2, :])
                pe.wait_ge(n_done, h * TILES + PT + 1)
                pe.wait_ge(decayed, h * TILES + PT + 3)
                pe.wait_ge(q_ready, h * TILES + PT + 2)
                pe.matmul(ps_o[:, PT % 2, :], s_in[:, PT % 2, :], v[:, PT, :], start=True, stop=False, skip_group_check=True)
                for par in range(2):
                    pe.wait_ge(r_landed[par], h * 64 + 64)
                    for a in range(NH2):
                        for j in range(4):
                            ins = pe.matmul(ps_o[BR * j:BR * (j + 1), PT % 2, :], q_dec[:, par, a, BR * j:BR * (j + 1)], r_in[:, par, j, a, :],
                                            start=False, stop=par == 1 and a == NH2 - 1, tile_position=(0, BR * j), skip_group_check=True)
                ins.then_inc(o_done, 1)
                for m in range(2, PAIRS):
                    pe.wait_ge(str_k, h * PAIRS + m + 1)
                    update(PT + m, k_str[:, m % 2, :])

        @block.gpsimd
        def _(pool):
            credit(pool, pr, ost_stored)
            pool.sem_inc(q_ready, 1)
            pool.sem_inc(gated, 1)
            pool.wait_ge(tabs, 8 * 16)
            with pool.Fori(0, RH) as h:
                def queries(c):
                    if c in (0, FIRST):
                        pool.wait_ge(q_in if c else q0_in, h * 32 + 32)
                        stand(pool, pr)
                    if c < PT:
                        if c >= 2:
                            pool.wait_ge(o_done, h * TILES + c)
                            stand(pool, pr)
                        for a in range(NH2):
                            ins = pool.tensor_tensor(q_dec[:, c % 2, a, :], qT[:, a, c * P:(c + 1) * P], qdec[:, bass.ds(h, 1), 0, :].rearrange("p o i -> p (o i)"), ALU.mult)
                    else:
                        pool.wait_ge(o_done, h * TILES + PT + 1)
                        stand(pool, pr)
                        for par in range(2):
                            for a in range(NH2):
                                ins = pool.tensor_tensor(q_dec[:, par, a, :], qT[:, a, PT * P:], qdec[:, bass.ds(h, 1), 1 + par, :].rearrange("p o i -> p (o i)"), ALU.mult)
                    ins.then_inc(q_ready, 1)

                def gate_and_store(c):
                    pool.wait_ge(scaled, h * TILES + c + 1)
                    if c == 0:
                        pool.wait_ge(g_in, h * 16 + 16)
                    pool.wait_ge(ost_stored[c % 2], h * 16 * (5 - c % 2) + 16 * (c // 2) + 16)
                    pool.tensor_tensor(ost[:, c % 2, :], normed[:, c % 2, :], g[:, c, :], ALU.mult).then_inc(gated, 1)
                    pool.wait_ge(gated, h * TILES + c + 2)
                    pool.dma_start(dr["o"][c * P:(c + 1) * P, bass.ds(h * DV, DV)], ost[:, c % 2, :]).then_inc(ost_stored[c % 2], 16)

                queries(0)
                for c in range(TILES):
                    if c + 1 < TILES:
                        queries(c + 1)
                    gate_and_store(c)
            pool.wait_ge(ost_stored[0], 16 + RH * 16 * 5)
            pool.wait_ge(ost_stored[1], 16 + RH * 16 * 4)

        @block.scalar
        def _(act):
            act.sem_inc(n_done, 2)
            act.sem_inc(p_stored, 16)
            for s in range(2):
                act.sem_inc(r_stored[s], 64)
            with act.Fori(0, RH) as h:
                for c in range(TILES):
                    act.wait_ge(var, h * TILES + c + 1)
                    act.activation(sc[:, c % 2, 1:2], sc[:, c % 2, 0:1], ACT.Sqrt).then_inc(root, 1)
                    act.wait_ge(own, h * 6 * TILES + 6 * c + 6)
                    act.wait_ge(gated, h * TILES + c) if c >= 2 else act.wait_ge(gated, h * TILES + 1)
                    act.activation(normed[:, c % 2, :], ps_o[:, c % 2, :], ACT.Identity, bias=sc[:, c % 2, 3:4], scale=sc[:, c % 2, 2:3]).then_inc(scaled, 1)
                    act.wait_ge(scaled, h * TILES + c + 1)
                    act.sem_inc(n_done, 1)
                act.wait_ge(state_new, h * U + PT + 1)
                act.dma_start(dr["state_prompt"][bass.ds(h, 1)].rearrange("o (a p) c -> p (o a) c", p=P), state[:, (PT - 1) % 2]).then_inc(p_stored, 16)
                for m in range(PAIRS):
                    par, j = m // 4, m % 4
                    act.wait_ge(state_new, h * U + PT + m + 2)
                    act.dma_start(dr["state_sample"][2 * j + par, bass.ds(h, 1)].rearrange("o (a p) c -> p (o a) c", p=P), r_in[:, par, j]).then_inc(r_stored[par], 16)
            act.wait_ge(p_stored, 16 + 16 * RH)
            for s in range(2):
                act.wait_ge(r_stored[s], 64 + 64 * RH)

        def stream_state(dve, h, m):
            par, j = m // 4, m % 4
            dve.wait_ge(upd, h * U + PT + m + 2)
            dve.scalar_tensor_tensor(r_in[:, par, j], r_in[:, par, j], cdec[:, 1, bass.ds(h, 1)], ps_u[:, (PT + m) % 2], ALU.mult, ALU.add).then_inc(state_new, 1)

        @block.vector
        def _(dve):
            dve.sem_inc(decayed, 2)
            dve.sem_inc(state_new, 1)
            dve.wait_ge(tabs, 8 * 16)
            with dve.Fori(0, RH) as h:
                def decay(c):
                    dve.wait_ge(scored, h * TILES + c + 2)
                    if c >= 2:
                        dve.wait_ge(o_done, h * TILES + c)
                        dve.wait_ge(upd, h * U + c)
                    else:
                        dve.wait_ge(o_done, h * TILES + 1)
                        dve.wait_ge(upd, h * U + 1)
                    dve.tensor_tensor(s_in[:, c % 2, :], ps_s[:, c % 2, 0:P], intra[:, int(c == PT), bass.ds(h, 1), :].rearrange("p o i -> p (o i)"), ALU.mult)
                    if c < PT:
                        dve.tensor_scalar(k_tok[:, c % 2, :], ps_s[:, c % 2, P:3 * P], kdec[:, bass.ds(h, 1), 0:1].rearrange("p o i -> p (o i)"), None, ALU.mult).then_inc(decayed, 1)
                    else:
                        dve.tensor_copy(k_tok[:, c % 2, :], ps_s[:, c % 2, P:3 * P]).then_inc(decayed, 1)

                def new_state(c):
                    dve.wait_ge(upd, h * U + c + 2)
                    if c == 0:
                        dve.tensor_copy(state[:, 0], ps_u[:, 0]).then_inc(state_new, 1)
                    else:
                        dve.wait_ge(state_new, h * U + c + 1)
                        dve.scalar_tensor_tensor(state[:, c % 2], state[:, (c - 1) % 2], cdec[:, 0, bass.ds(h, 1)], ps_u[:, c % 2], ALU.mult, ALU.add).then_inc(state_new, 1)

                def statistics(c):
                    dve.wait_ge(o_done, h * TILES + c + 2)
                    n = h * 6 * TILES + 6 * c
                    s, z = c % 2, sc[:, c % 2, :]
                    dve.wait_ge(n_done, h * TILES + max(c, 1) + 1)
                    dve.bn_stats(st6[:, s, :], ps_o[:, s, :]).then_inc(own, 1)
                    dve.wait_ge(own, n + 1)
                    stand(dve, pr)
                    dve.bn_aggr(mv[:, s, :], st6[:, s, :]).then_inc(own, 1)
                    dve.wait_ge(own, n + 2)
                    dve.tensor_scalar(z[:, 0:1], mv[:, s, 1:2], EPS, None, ALU.add).then_inc(own, 1)
                    dve.wait_ge(own, n + 3)
                    dve.sem_inc(var, 1)
                    dve.wait_ge(root, h * TILES + c + 1)
                    dve.reciprocal(z[:, 2:3], z[:, 1:2]).then_inc(own, 1)
                    dve.wait_ge(own, n + 4)
                    dve.tensor_scalar(z[:, 3:4], mv[:, s, 0:1], z[:, 2:3], None, ALU.mult).then_inc(own, 1)
                    dve.wait_ge(own, n + 5)
                    dve.tensor_scalar(z[:, 3:4], z[:, 3:4], -1.0, None, ALU.mult).then_inc(own, 1)

                def stream_keys(m):
                    par, j = m // 4, m % 4
                    if m >= 2:
                        dve.wait_ge(upd, h * U + PT + m)
                    dve.tensor_scalar(k_str[:, m % 2, :], k_tok[:, PT % 2, :], kdec[:, bass.ds(h, 1), 1 + 2 * j + par:2 + 2 * j + par].rearrange("p o i -> p (o i)"), None, ALU.mult).then_inc(str_k, 1)

                decay(0)
                for c in range(PT):
                    decay(c + 1)
                    if c == PT - 1:
                        dve.wait_ge(decayed, h * TILES + TILES + 2)
                        for m in range(2):
                            stream_keys(m)
                    if c == 0:
                        dve.wait_ge(p_stored, h * 16 + 16)
                    new_state(c)
                    statistics(c)
                for m in range(2, 4):
                    stream_keys(m)
                dve.wait_ge(o_done, h * TILES + TILES + 1)
                for m in range(2):
                    stream_state(dve, h, m)
                statistics(PT)
                for m in range(4, PAIRS):
                    stream_keys(m)
                    stream_state(dve, h, m - 2)
                stream_state(dve, h, PAIRS - 2)
                stream_state(dve, h, PAIRS - 1)


def attention(pr):
    nc, dr = pr.nc, pr.dram
    G = FH // KVH
    UNITS = G * PT + 2
    SCALE_L = (PT + 1) * P
    blocks = [u // G + 1 for u in range(G * PT)] + [2, 2]
    groups = [-(-b // 4) for b in blocks]
    first = [sum(groups[:u]) for u in range(UNITS + 1)]
    GROUPS = first[-1]
    with ExitStack() as ctx:
        sb = lambda n, s, dt=F32: ctx.enter_context(nc.sbuf_tensor(f"fox_{n}", s, dt))
        ps = lambda n, s: ctx.enter_context(nc.psum_tensor(f"fox_{n}", s, F32))
        sem = ctx.enter_context(semaphores(nc, "fox_"))
        work = sb("work", [P, 4 * TOKENS + 2 * SEQ])
        ones = work[0:FH, 4 * TOKENS:4 * TOKENS + SEQ]
        c_logf = work[0:FH, 4 * TOKENS + SEQ:4 * TOKENS + 2 * SEQ]
        qT = work[:, 0:2 * SEQ].rearrange("p (a c) -> p a c", a=G)
        s_sb = work[:, 2 * SEQ:4 * SEQ].rearrange("p (a c) -> p a c", a=2)
        pT = work[:, 4 * SEQ:5 * SEQ].rearrange("p (a c) -> p a c", a=2)
        kT = work[:, 5 * SEQ:5 * SEQ + TILES * P]
        logf_tok = sb("logf_tok", [P, TILES, FH])
        c_tok = sb("c_tok", [P, DEC_BATCH, FH])
        cum_c = sb("cum_c", [FH, DEC_BATCH * PAST])
        cum_n = sb("cum_n", [FH, P])
        cum_hi, cum_lo = sb("cum_hi", [FH, SEQ], F32R), sb("cum_lo", [FH, SEQ], F32R)
        sel_r = sb("sel_r", [FH, FH, P], F32R)
        sel_group = sb("sel_group", [FH, KVH, P])
        mask = sb("mask", [P, P])
        mask_s = sb("mask_s", [P, 2, P])
        own_s = sb("own_s", [P, 2, P])
        nf = sb("nf", [P, FH, SEQ])
        cum = nf[0:FH, 4, :]
        logf = nf[0:FH, 5:7, :].rearrange("p a c -> p (a c)")[:, 0:TOKENS]
        sel_head = nf[0:FH, 7, :].rearrange("p (a b) -> p a b", a=FH)
        nf_s = sb("nf_s", [P, KVH, 2, 2, P])
        fq = sb("fq", [P, PT, FH])
        fq_s = sb("fq_s", [P, KVH, 2])
        own_t = sb("own_t", [P, P])
        q = sb("q", [P, TILES, G * DH])
        k = sb("k", [P, TILES, DH])
        v = sb("v", [P, TILES, DH])
        ck = sb("ck", [P, DEC_BATCH, DH])
        cv = sb("cv", [P, DEC_BATCH, DH])
        gt = sb("gt", [P, G * PT + 2, DH])
        ckT = sb("ckT", [P, DEC_BATCH * P])
        qTs = sb("qTs", [P, DEC_BATCH, G, DEC_SEQ])
        ost = sb("ost", [P, 2, DH])
        scaled = sb("scaled", [P, 2, DH])
        mx = sb("mx", [P, 3, 3])
        ps_s = ps("ps_s", [P, 2, 2, 512])
        ps_t = ps("ps_t", [P, 2, 512])
        ps_o = ps("ps_o", [P, 2, 512])
        f_landed, sel_landed, tabs, own, rec = sem("f_landed"), sem("sel_landed"), sem("tabs"), sem("own"), sem("rec")
        lf_turned, lf_out = sem("lf_turned"), sem("lf_out")
        c_turned, c_read, lf_stored = sem("c_turned"), sem("c_read"), sem("lf_stored")
        cum_ready, cum_split, sums_ready, nf_done, nf_read, nfs_done, nfs_read, fq_turned, prep = sem("cum_ready"), sem("cum_split"), sem("sums_ready"), sem("nf_done"), sem("nf_read"), sem("nfs_done"), sem("nfs_read"), sem("fq_turned"), sem("prep")
        qk_in, v_in, g_in, gs_in = sem("qk_in"), sem("v_in"), sem("g_in"), sem("gs_in")
        x_turned, x_ready = sem("x_turned"), sem("x_ready")
        s_done, s_read, negm, p_done = sem("s_done"), sem("s_read"), sem("negm"), sem("p_done")
        t_done, pt_ready, pv_done, scales_used, fin = sem("t_done"), sem("pt_ready"), sem("pv_done"), sem("scales_used"), sem("fin")
        stored = [sem(f"stored{i}") for i in range(2)]
        streams_out = [sem(f"streams_out{i}") for i in range(2)]
        X = -(-(TILES + DEC_BATCH + G * TILES) // 4)
        items = ([("k", t) for t in range(PT)] + [("q", t * G + h) for h in range(G) for t in range(PT)]
                 + [("k", PT)] + [("q", PT * G + h) for h in range(G)] + [None] + [("c", b) for b in range(DEC_BATCH)])
        X0 = X - DEC_BATCH // 4
        SELF = 5
        block = ctx.enter_context(nc.Block())

        def stream_rows(n, r, name, heads=range(G)):
            for j in range(4):
                for h in heads:
                    p0, b = BR * j + DEC_SEQ * h, 4 * r + j
                    yield slice(p0, p0 + DEC_SEQ), dr[name][SEQ + b * DEC_SEQ:SEQ + (b + 1) * DEC_SEQ, bass.ds(n * G * DH + h * DH, DH)]

        def store_streams(eng, n, heads=range(G)):
            for r in range(2):
                u = G * PT + r
                eng.wait_ge(fin, n * UNITS + u + 2)
                for rows, dst in stream_rows(n, r, "o2", heads):
                    eng.dma_start(dst, ost[rows, u % 2, :]).then_inc(streams_out[u % 2], 16)

        @block.sync
        def _(sp):
            sp.dma_start(logf[:, :], dr["logf"]).then_inc(f_landed, 16)
            sp.dma_start(sel_head[:, :, :].rearrange("p a b -> p (a b)"), pr.table["sel_head"]).then_inc(sel_landed, 16)
            with nc.allow_non_contiguous_dma(reason="eight columns"):
                sp.dma_start(c_tok[:, :, :], dr["cache_logf"].rearrange("b p h -> p b h")).then_inc(tabs, 16)
            for dst, name in ((sel_group, "sel_group"), (mask, "mask"), (mask_s, "mask_s"), (own_s, "own_s")):
                flat = dst[:] if len(dst.shape) == 2 else dst[:].rearrange("p a b -> p (a b)")
                sp.dma_start(flat, pr.table[name]).then_inc(tabs, 16)

            def load_qk(n):
                kvc = bass.ds(n * DH, DH)
                sp.dma_start(k[:, 0:PT], dr["k_prompt"][:, kvc].rearrange("(t p) c -> p t c", p=P)).then_inc(qk_in, 16)
                sp.dma_start(k[:, PT], dr["k_sample"][:, kvc]).then_inc(qk_in, 16)
                sp.dma_start(ck[:, :, :], dr["cache_k"][:, :, kvc].rearrange("b p c -> p b c")).then_inc(qk_in, 16)
                sp.dma_start(q[:, :, :], dr["q"][:, bass.ds(n * G * DH, G * DH)].rearrange("(t p) c -> p t c", p=P)).then_inc(qk_in, 16)

            def load_values(n):
                kvc = bass.ds(n * DH, DH)
                sp.dma_start(v[:, 0:PT], dr["v_prompt"][:, kvc].rearrange("(t p) c -> p t c", p=P)).then_inc(v_in, 16)
                sp.dma_start(v[:, PT], dr["v_sample"][:, kvc]).then_inc(v_in, 16)
                sp.dma_start(cv[:, :, :], dr["cache_v"][:, :, kvc].rearrange("b p c -> p b c")).then_inc(v_in, 16)
                sp.dma_start(gt[:, 0:G * PT].rearrange("p (t g) c -> p t (g c)", g=G), dr["g2"][0:SEQ, bass.ds(n * G * DH, G * DH)].rearrange("(t p) c -> p t c", p=P)).then_inc(g_in, 16)

            def load_stream_gates(n):
                for r in range(2):
                    for rows, src in stream_rows(n, r, "g2"):
                        sp.dma_start(gt[rows, G * PT + r], src).then_inc(gs_in, 16)

            for s in range(2):
                sp.sem_inc(streams_out[s], 128)
            load_qk(0)
            load_values(0)
            load_stream_gates(0)
            with sp.Fori(0, KVH - 1) as n:
                sp.wait_ge(x_turned, n * X + X + 1)
                load_qk(n + 1)
                sp.wait_ge(fin, n * UNITS + UNITS + 1)
                load_values(n + 1)
                store_streams(sp, n)
                load_stream_gates(n + 1)
            store_streams(sp, KVH - 1, range(1))
            for s in range(2):
                sp.wait_ge(streams_out[s], 128 + KVH * 128)

        @block.tensor
        def _(pe):
            pe.wait_ge(f_landed, 16)
            for t in range(TILES):
                ins = pe.transpose(ps_t[:, 0, t * FH:(t + 1) * FH], logf[:, t * P:(t + 1) * P], pr.ident[0:FH, 0:FH])
            ins.then_inc(lf_turned, 1)
            pe.wait_ge(cum_ready, 1)
            for t in range(PT):
                ins = pe.transpose(ps_t[:, 1, t * FH:(t + 1) * FH], cum[:, t * P:(t + 1) * P], pr.ident[0:FH, 0:FH])
            ins.then_inc(fq_turned, 1)
            pe.wait_ge(tabs, 5 * 16)
            for b in range(DEC_BATCH):
                ins = pe.transpose(ps_s[0:FH, 1, b // 4, (b % 4) * P:(b % 4 + 1) * P], c_tok[:, b, :], pr.ident[:, :])
            ins.then_inc(c_turned, 1)
            pe.wait_ge(cum_split, 3)
            for h in range(FH):
                pe.wait_ge(nf_read, h + 1)
                if h == 1:
                    pe.wait_ge(c_read, 1)
                for a in range(2):
                    for m, part in enumerate((cum_hi, cum_lo)):
                        ins = pe.matmul(ps_s[:, h % 2, a, :], sel_r[:, h, :], part[:, a * 512:(a + 1) * 512], start=m == 0, stop=m == 1)
                ins.then_inc(nf_done, 1)
            pe.wait_ge(sums_ready, 1)
            for n in range(KVH):
                for r in range(2):
                    m = 2 * n + r
                    pe.wait_ge(nfs_read, m + 1)
                    pe.matmul(ps_o[:, m % 2, P:2 * P], sel_group[:, n, :], cum_n[:, :], start=True, stop=True, skip_group_check=True)
                    for j in range(4):
                        b = 4 * r + j
                        ins = pe.matmul(ps_o[BR * j:BR * (j + 1), m % 2, 0:P], sel_group[:, n, BR * j:BR * (j + 1)], cum_c[:, b * PAST:(b + 1) * PAST],
                                        start=True, stop=True, tile_position=(0, BR * j), skip_group_check=True)
                    ins.then_inc(nfs_done, 1)
            pe.wait_ge(nf_read, 2 + FH)

            with pe.Fori(0, KVH) as n:
                pe.wait_ge(qk_in, n * 64 + 64)

                def turn_inputs(x):
                    pe.wait_ge(x_ready, n * X + x + 1)
                    for y, item in enumerate(items[4 * x:4 * x + 4]):
                        if item:
                            what, z = item
                            src = k[:, z, :] if what == "k" else ck[:, z, :] if what == "c" else q[:, z // G, (z % G) * DH:(z % G + 1) * DH]
                            ins = pe.transpose(ps_t[:, x % 2, y * P:(y + 1) * P], src, pr.ident[:, :])
                    ins.then_inc(x_turned, 1)

                for x in range(X0):
                    turn_inputs(x)
                pe.wait_ge(x_ready, n * X + X0 + 2)

                def scores(u):
                    pe.wait_ge(s_read, n * UNITS + u + 1)
                    t, h = u // G, u % G
                    if u < G * PT:
                        L = (t + 1) * P
                        for a in range(-(-L // 512)):
                            w = min(512, L - 512 * a)
                            ins = pe.matmul(ps_s[:, u % 2, a, 0:w], qT[:, h, t * P:(t + 1) * P], kT[:, a * 512:a * 512 + w], start=True, stop=True)
                    else:
                        r = u - G * PT
                        rows = qTs[:, :, :, :].rearrange("p b g q -> p (b g q)")
                        pe.matmul(ps_s[:, u % 2, 0, P:2 * P], rows[:, r * P:(r + 1) * P], kT[:, SEQ:SEQ + P], start=True, stop=True, skip_group_check=True)
                        for j in range(4):
                            b = 4 * r + j
                            ins = pe.matmul(ps_s[BR * j:BR * (j + 1), u % 2, 0, 0:P], rows[:, b * BR:(b + 1) * BR], ckT[:, b * P:(b + 1) * P],
                                            start=True, stop=True, tile_position=(0, BR * j), skip_group_check=True)
                    ins.then_inc(s_done, 1)

                def turn(u, x):
                    m = first[u] + x
                    pe.wait_ge(pt_ready, n * GROUPS + m + 1)
                    for y in range(min(4, blocks[u] - 4 * x)):
                        b = 4 * x + y
                        ins = pe.transpose(ps_t[:, m % 2, y * P:(y + 1) * P], s_sb[:, u % 2, b * P:(b + 1) * P], pr.ident[:, :])
                    ins.then_inc(t_done, 1)

                def values(u, x):
                    m = first[u] + x
                    pe.wait_ge(pt_ready, n * GROUPS + m + 3)
                    o = ps_o[:, u % 2, 0:DH]
                    if u < G * PT:
                        for y in range(min(4, blocks[u] - 4 * x)):
                            b = 4 * x + y
                            ins = pe.matmul(o, pT[:, m % 2, y * P:(y + 1) * P], v[:, b, :], start=b == 0, stop=b == blocks[u] - 1)
                    else:
                        r = u - G * PT
                        pe.matmul(o, pT[:, m % 2, P:2 * P], v[:, PT, :], start=True, stop=False, skip_group_check=True)
                        for j in range(4):
                            ins = pe.matmul(ps_o[BR * j:BR * (j + 1), u % 2, 0:DH], pT[:, m % 2, BR * j:BR * (j + 1)], cv[:, 4 * r + j, :],
                                            start=False, stop=True, tile_position=(0, BR * j), skip_group_check=True)
                    ins.then_inc(pv_done, 1)

                scores(0)
                scores(1)
                pe.wait_ge(nfs_read, 2 + 2 * KVH)
                for x in range(X0, X):
                    turn_inputs(x)
                pe.wait_ge(x_ready, n * X + X + 2)
                pe.wait_ge(v_in, n * 48 + 48)
                for u in range(UNITS):
                    pe.wait_ge(p_done, n * UNITS + u + 1)
                    for x in range(groups[u]):
                        turn(u, x)
                    if u + 2 < UNITS:
                        scores(u + 2)
                    pe.wait_ge(scales_used, n * UNITS + u + 1)
                    for x in range(groups[u]):
                        values(u, x)

        @block.scalar
        def _(act):
            act.sem_inc(nf_read, 2)
            act.sem_inc(scales_used, 2)
            act.sem_inc(x_ready, 2)
            act.sem_inc(x_turned, 1)
            act.sem_inc(pt_ready, 2)
            act.wait_ge(sel_landed, 16)
            act.copy(sel_r[:, :, :], sel_head[:, :, :]).then_inc(cum_split, 1)
            act.wait_ge(cum_ready, 1)
            act.copy(cum_hi[:, :], cum[:, :]).then_inc(cum_split, 1)
            for h in range(FH):
                act.wait_ge(nf_done, h + 1)
                if h == 4:
                    act.wait_ge(sums_ready, 1)
                act.mul(nf[:, h, :].rearrange("p (a c) -> p a c", a=2), ps_s[:, h % 2], -1.0).then_inc(nf_read, 1)
            act.wait_ge(nf_read, 2 + FH)
            act.sem_inc(prep, 1)
            with act.Fori(0, KVH) as n:
                for x in range(X):
                    act.wait_ge(x_turned, n * X + x + 2)
                    src = ps_t[:, x % 2, :]
                    if x < X0 - 1:
                        what, z = items[4 * x]
                        dst = kT[:, z * P:(z + 4) * P] if what == "k" else qT[:, z % G, (z // G) * P:(z // G + 4) * P]
                        ins = act.copy(dst, src)
                    elif x < X0:
                        act.copy(kT[:, SEQ:SEQ + P], src[:, 0:P])
                        for h in range(G):
                            ins = act.copy(qTs[:, :, h, :], src[:, (1 + h) * P:(2 + h) * P].rearrange("p (b q) -> p b q", q=DEC_SEQ))
                    else:
                        b = items[4 * x][1]
                        ins = act.copy(ckT[:, b * P:(b + 4) * P], src)
                    ins.then_inc(x_ready, 1)

                def exp(u):
                    act.wait_ge(negm, n * UNITS + u + 1)
                    w = s_sb[:, u % 2, 0:blocks[u] * P]
                    act.activation(w, w, ACT.Exp, bias=mx[:, u % 3, 0:1], accum_out=mx[:, u % 3, 1:2]).then_inc(p_done, 1)

                def scale(u):
                    act.wait_ge(pv_done, n * GROUPS + first[u + 1])
                    act.wait_ge(rec, n * UNITS + u + 4)
                    act.wait_ge(fin, n * UNITS + max(u, 1))
                    act.activation(scaled[:, u % 2, :], ps_o[:, u % 2, 0:DH], ACT.Copy, scale=mx[:, u % 3, 2:3]).then_inc(scales_used, 1)

                exp(0)
                for u in range(UNITS):
                    for x in range(groups[u]):
                        m = first[u] + x
                        act.wait_ge(t_done, n * GROUPS + m + 1)
                        if m >= 2:
                            act.wait_ge(pv_done, n * GROUPS + m - 1)
                        w = min(4, blocks[u] - 4 * x) * P
                        act.copy(pT[:, m % 2, 0:w], ps_t[:, m % 2, 0:w]).then_inc(pt_ready, 1)
                    if u + 1 < UNITS:
                        exp(u + 1)
                    if u:
                        scale(u - 1)
            store_streams(act, KVH - 1, range(1, G))

        @block.gpsimd
        def _(pool):
            credit(pool, pr, stored)
            pool.sem_inc(fin, 1)
            pool.wait_ge(lf_out, 1)
            with nc.allow_non_contiguous_dma(reason="rows of eight"):
                pool.dma_start(dr["logf_prompt"].rearrange("(t p) h -> p t h", p=P), logf_tok[:, 0:PT, :]).then_inc(lf_stored, 16)
                pool.dma_start(dr["logf_sample"], logf_tok[:, PT, :]).then_inc(lf_stored, 16)
            with pool.Fori(0, KVH) as n:
                for u in range(UNITS):
                    s = u % 2
                    pool.wait_ge(scales_used, n * UNITS + u + 3)
                    if u == 0:
                        pool.wait_ge(g_in, n * 16 + 16)
                    if u == G * PT:
                        pool.wait_ge(gs_in, n * 256 + 256)
                    pool.wait_ge(stored[s], n * PT * 16 + 16 + 16 * (u // 2))
                    if u < 2:
                        pool.wait_ge(streams_out[s], n * 128 + 128)
                    pool.tensor_tensor(ost[:, s, :], scaled[:, s, :], gt[:, u, :], ALU.mult).then_inc(fin, 1)
                    if u < G * PT:
                        pool.wait_ge(fin, n * UNITS + u + 2)
                        t, h = u // G, u % G
                        pool.dma_start(dr["o2"][t * P:(t + 1) * P, bass.ds(n * G * DH + h * DH, DH)], ost[:, s, :]).then_inc(stored[s], 16)
            pool.wait_ge(lf_stored, 32)
            for s in range(2):
                pool.wait_ge(stored[s], 16 + KVH * PT * 16)

        @block.vector
        def _(dve):
            chain = Chain(dve, own)
            dve.sem_inc(rec, 3)
            dve.sem_inc(s_read, 2)
            dve.sem_inc(nfs_read, 2)
            chain.link(dve.memset(ones[:, :], 1.0))
            dve.wait_ge(f_landed, 16)
            chain.link(dve.tensor_tensor_scan(cum[:, :], ones[:, :], logf[:, 0:SEQ], 0.0, ALU.mult, ALU.add))
            dve.sem_inc(cum_ready, 1)
            dve.wait_ge(lf_turned, 1)
            dve.tensor_copy(logf_tok[:, :, :], ps_t[:, 0, 0:TILES * FH].rearrange("p (t h) -> p t h", t=TILES)).then_inc(lf_out, 1)
            dve.wait_ge(cum_split, 2)
            dve.tensor_tensor(cum_lo[:, :], cum[:, :], cum_hi[:, :].bitcast(F32), ALU.subtract).then_inc(cum_split, 1)
            dve.wait_ge(c_turned, 1)
            chain.link(dve.tensor_copy(c_logf[:, :].rearrange("p (a c) -> p a c", a=2), ps_s[0:FH, 1]))
            dve.sem_inc(c_read, 1)

            def stream_sums(b):
                c = slice(b * PAST, (b + 1) * PAST)
                chain.link(dve.tensor_tensor_scan(cum_c[:, c], ones[:, 0:PAST], c_logf[:, c], 0.0, ALU.mult, ALU.add))
                w = slice(b * DEC_SEQ, (b + 1) * DEC_SEQ)
                chain.link(dve.tensor_tensor_scan(cum_n[:, w], ones[:, 0:DEC_SEQ], logf[:, SEQ + b * DEC_SEQ:SEQ + (b + 1) * DEC_SEQ],
                                                  cum_c[:, (b + 1) * PAST - 1:(b + 1) * PAST], ALU.mult, ALU.add))

            for b in range(2):
                stream_sums(b)
            dve.wait_ge(fq_turned, 1)
            chain.link(dve.tensor_copy(fq[:, :, :], ps_t[:, 1, 0:PT * FH].rearrange("p (t h) -> p t h", t=PT)))
            for b in range(2, DEC_BATCH):
                stream_sums(b)
            dve.sem_inc(sums_ready, 1)
            dve.sem_inc(prep, 1)
            for n in range(KVH):
                for r in range(2):
                    m = 2 * n + r
                    dve.wait_ge(nfs_done, m + 1)
                    f_new = ps_o[:, m % 2, P:2 * P]
                    chain.link(dve.tensor_tensor(own_t[:, :], f_new, own_s[:, r, :], ALU.mult))
                    chain.link(dve.tensor_reduce(fq_s[:, n, r:r + 1], own_t[:, :], AX.X, ALU.add))
                    chain.link(dve.tensor_scalar(nf_s[:, n, r, 0, :], ps_o[:, m % 2, 0:P], -1.0, None, ALU.mult))
                    chain.link(dve.scalar_tensor_tensor(nf_s[:, n, r, 1, :], f_new, -1.0, mask_s[:, r, :], ALU.mult, ALU.add))
                    dve.sem_inc(nfs_read, 1)
            dve.sem_inc(prep, 1)
            start = chain.n
            dve.wait_ge(prep, 3)
            with dve.Fori(0, KVH) as n:
                def softmax(u):
                    dve.wait_ge(s_done, n * UNITS + u + 1)
                    if u >= 2:
                        dve.wait_ge(t_done, n * GROUPS + first[u - 1])
                    own0 = start + n * UNITS * 2 + u * 2
                    s, L = u % 2, blocks[u] * P
                    if u < G * PT:
                        t, h = u // G, u % G
                        head = bass.ds(n * G + h, 1)
                        sv, pv = s_sb[:, s, 0:L], ps_s[:, s].rearrange("p a c -> p (a c)")[:, 0:L]
                        dve.scalar_tensor_tensor(sv, pv, fq[:, t, head], nf[:, head, 0:L].rearrange("p o c -> p (o c)"), ALU.add, ALU.add).then_inc(own, 1)
                        dve.wait_ge(own, own0 + 1)
                        dve.tensor_tensor(s_sb[:, s, L - P:L], s_sb[:, s, L - P:L], mask[:, :], ALU.add).then_inc(own, 1)
                    else:
                        r = u - G * PT
                        dve.scalar_tensor_tensor(s_sb[:, s, 0:L], ps_s[:, s, 0, 0:L], fq_s[:, bass.ds(n, 1), r:r + 1].rearrange("p o c -> p (o c)"),
                                                 nf_s[:, bass.ds(n, 1), r].rearrange("p o a c -> p (o a c)"), ALU.add, ALU.add).then_inc(own, 2)
                    dve.wait_ge(own, own0 + 2)
                    dve.sem_inc(s_read, 1)
                    dve.wait_ge(rec, n * UNITS + u + 1)
                    dve.tensor_reduce(mx[:, u % 3, 0:1], s_sb[:, s, 0:L], AX.X, ALU.max, negate=True).then_inc(negm, 1)

                def over_sum(u):
                    dve.wait_ge(p_done, n * UNITS + u + 1)
                    dve.wait_ge(scales_used, n * UNITS + max(u, 1))
                    dve.reciprocal(mx[:, u % 3, 2:3], mx[:, u % 3, 1:2]).then_inc(rec, 1)

                softmax(0)
                softmax(1)
                for u in range(UNITS):
                    if u + 2 < UNITS:
                        softmax(u + 2)
                    over_sum(u)
                u = UNITS - 1
                dve.wait_ge(scales_used, n * UNITS + u + 2)
                dve.wait_ge(pv_done, n * GROUPS + GROUPS)
                dve.wait_ge(rec, n * UNITS + UNITS + 3)
                dve.wait_ge(fin, n * UNITS + u)
                dve.tensor_scalar(scaled[:, u % 2, :], ps_o[:, u % 2, 0:DH], mx[:, u % 3, 2:3], None, ALU.mult).then_inc(scales_used, 1)


def build(nc, dram, table):
    with ExitStack() as ctx:
        pr = Program(nc, ctx, dram, table)
        dr = dram

        def tile_rows(name, t):
            return dr[name][t * P:(t + 1) * P, :]

        def columns_of(name, c0):
            return lambda c, w: dr[name][:, c0 + c:c0 + c + w].rearrange("(t p) c -> p t c", p=P)

        def x_rows(t):
            return dr["x_prompt"][t * P:(t + 1) * P, :] if t < PT else dr["x_sample"]

        def to_rows(name, c0=0):
            return lambda c, t: dr[name][t * P:(t + 1) * P, bass.ds(c * CW + c0, CW)]

        def split_rows(prompt, sample):
            return lambda c, t: dr[prompt][t * P:(t + 1) * P, :] if t < PT else dr[sample]

        def turned_rows(c, m):
            part, n, half = m // 6, m % 6 // 2, m % 2
            return dr["qkT"][bass.ds(c * 4 + part * 2 + half, 1), :, n * NB3:(n + 1) * NB3].rearrange("o p t -> p (o t)")

        qk = [head_columns(dr["a_w_in"], h) for h in range(RH)]
        wv = [columns(dr["a_w_in"], 0, 2 * D + CW * c) for c in range(4)]
        wg = [columns(dr["a_w_in"], 0, 2 * D + VW + CW * c) for c in range(4)]
        wo = [[columns(dr["a_w_out"], half * D, CW * c) for c in range(2)] for half in range(2)]
        wk, wvv = columns(dr["kv_w"], 0, 0), columns(dr["kv_w"], 0, CW)
        wq = [columns(dr["b_w_in"], 0, CW * c) for c in range(2)]
        wg2 = [columns(dr["b_w_in"], 0, D + CW * c) for c in range(2)]
        wo2 = [columns(dr["b_w_out"], 0, CW * c) for c in range(2)]

        source = ExitStack()
        x = source.enter_context(nc.sbuf_tensor("x", [P, TILES * D], F32))
        condition(pr, x, x_rows, qk[0])
        project(pr, "in", None, True, 0,
                [dict(kind="rotary", pairs=2, weights=qk, store=turned_rows),
                 dict(kind="copy", pairs=2, weights=wv, store=to_rows("v")),
                 dict(kind="silu", pairs=2, weights=wg, store=to_rows("g"))], 0, wo[0][0], rows_here=x, side=True)
        source.close()
        retention(pr)
        for half in range(2):
            before = (lambda c, t: x_rows(t)[:, c * CW:(c + 1) * CW]) if half == 0 else (lambda c, t: tile_rows("x1a", t)[:, c * CW:(c + 1) * CW])
            project(pr, f"out{half}", columns_of("o", half * D), False, None,
                    [dict(kind="residual", pairs=1, weights=wo[half], col=lambda i, s: s * CW,
                          store=lambda c, t, half=half: tile_rows(("x1a", "x1")[half], t)[:, c * CW:(c + 1) * CW])],
                    12 + 2 * half, wo[1][0] if half == 0 else wk, gate_layer=0, residual=before, gain=pr.gn_g[:, half], sums=half == 1)
        project(pr, "kv", columns_of("x1", 0), True, 1,
                [dict(kind="norm", pairs=1, weights=[wk, wvv], gain=dr["k_norm_g"], scale=1.0, plain=1,
                      store=lambda c, t: split_rows(*(("k_prompt", "k_sample"), ("v_prompt", "v_sample"))[c])(c, t))],
                16, wq[0], forget=True)
        project(pr, "q", columns_of("x1", 0), True, 2,
                [dict(kind="norm", pairs=1, weights=wq, gain=dr["b_q_norm_g"], scale=DH ** -0.5, store=to_rows("q")),
                 dict(kind="silu", pairs=1, weights=wg2, store=to_rows("g2"))], 18, wo2[0])
        attention(pr)
        project(pr, "end", columns_of("o2", 0), False, None,
                [dict(kind="residual", pairs=1, weights=wo2, col=lambda i, s: s * CW,
                      store=lambda c, t: (dr["y_prompt"][t * P:(t + 1) * P, c * CW:(c + 1) * CW] if t < PT else dr["y_sample"][:, c * CW:(c + 1) * CW]))],
                22, None, gate_layer=1, residual=lambda c, t: tile_rows("x1", t)[:, c * CW:(c + 1) * CW])


_SHAPES = {
    "x_prompt": (SEQ, D), "x_sample": (P, D), "state_ret": (DEC_BATCH, RH, DK, DV),
    "cache_k": (DEC_BATCH, PAST, KVH * DH), "cache_v": (DEC_BATCH, PAST, KVH * DH), "cache_logf": (DEC_BATCH, PAST, FH),
    "c_prompt": (1, D), "c_sample": (DEC_BATCH, D),
    "a_norm_g": (1, D), "a_ada_w": (D, 3 * D), "a_ada_b": (1, 3 * D), "a_w_in": (D, 6 * D), "a_gn_g": (1, VW), "a_w_out": (VW, D),
    "kv_norm_g": (1, D), "kv_ada_w": (D, 2 * D), "kv_ada_b": (1, 2 * D), "kv_w": (D, 2 * KVH * DH + FH), "kv_fb": (FH, 1), "k_norm_g": (1, DH),
    "b_norm_g": (1, D), "b_ada_w": (D, 3 * D), "b_ada_b": (1, 3 * D), "b_w_in": (D, 2 * D), "b_q_norm_g": (1, DH), "b_w_out": (D, D),
}
_OUTS = {
    "y_prompt": (SEQ, D), "y_sample": (P, D), "state_prompt": (RH, DK, DV), "k_prompt": (SEQ, KVH * DH), "v_prompt": (SEQ, KVH * DH),
    "logf_prompt": (SEQ, FH), "state_sample": (DEC_BATCH, RH, DK, DV), "k_sample": (P, KVH * DH), "v_sample": (P, KVH * DH), "logf_sample": (P, FH),
}
_FINAL = {
    "y_prompt": (1, SEQ, D), "y_sample": (DEC_BATCH, DEC_SEQ, D), "state_prompt": (1, 1, RH, DK, DV), "k_prompt": (1, SEQ, KVH, DH),
    "v_prompt": (1, SEQ, KVH, DH), "logf_prompt": (1, SEQ, FH), "state_sample": (1, DEC_BATCH, RH, DK, DV),
    "k_sample": (DEC_BATCH, DEC_SEQ, KVH, DH), "v_sample": (DEC_BATCH, DEC_SEQ, KVH, DH), "logf_sample": (DEC_BATCH, DEC_SEQ, FH),
}
_SCRATCH = {
    "credit": (4, P),
    "gate": (P, 2, 2, D), "qkT": (4 * RH, P, TOKENS), "v": (TOKENS, VW), "g": (TOKENS, VW), "o": (TOKENS, VW),
    "x1a": (TOKENS, D), "x1": (TOKENS, D), "logf": (FH, TOKENS), "q": (TOKENS, D), "g2": (TOKENS, D), "o2": (TOKENS, D),
}


def kernel(**inputs):
    import concourse.bacc as bacc
    from concourse.bass_utils import run_bass_kernel_spmd

    nc = bacc.Bacc("TRN2", target_bir_lowering=False, num_devices=1)
    arrays, dram, table = {}, {}, {}
    for name, shape in _SHAPES.items():
        arrays[f"in_{name}"] = np.ascontiguousarray(inputs[name]).reshape(shape)
        dram[name] = nc.dram_tensor(f"in_{name}", shape, F32, kind="ExternalInput").ap()
    for name, a in tables().items():
        arrays[f"table_{name}"] = a
        table[name] = nc.dram_tensor(f"table_{name}", a.shape, F32, kind="ExternalInput").ap()
    for name, shape in _OUTS.items():
        dram[name] = nc.dram_tensor(f"out_{name}", shape, F32, kind="ExternalOutput").ap()
    for name, shape in _SCRATCH.items():
        dram[name] = nc.dram_tensor(f"scratch_{name}", shape, F32, kind="Internal").ap()
    build(nc, dram, table)
    r = run_bass_kernel_spmd(nc, [arrays], core_ids=[0])
    return tuple(r.results[0][f"out_{name}"].reshape(_FINAL[name]) for name in _OUTS)
```
